# Optimizing a Trainium2 kernel written in Bass

```python
import jax, jax.numpy as jnp
from jax import lax
import numpy as np
import math

D_MODEL = 1024
BATCH = 1
SEQ = 512
DEPTH = 2

HEAD_DIM = 64
BLOCK = 128
ROPE_THETA = 10000.0
EPS = 1e-6
FOX_HEADS = 8
DSA_HEADS = 8
IDX_HEADS = 4
IDX_DIM = 64
DSA_TOPK_MAX = 256
RET_HEADS = 8
SWA_Q_HEADS = 8
SWA_KV_HEADS = 2
SWA_WINDOW = 128
N_BRANCH = 4
BRANCH_WIDTH = 8 * HEAD_DIM
D_FF = 2816
CONV_WIDTH = 3

COL_SIZES = (
    FOX_HEADS * HEAD_DIM, FOX_HEADS * HEAD_DIM, FOX_HEADS * HEAD_DIM, FOX_HEADS,
    DSA_HEADS * HEAD_DIM, HEAD_DIM, HEAD_DIM, IDX_HEADS * IDX_DIM, IDX_DIM, IDX_HEADS,
    RET_HEADS * HEAD_DIM, RET_HEADS * HEAD_DIM, RET_HEADS * HEAD_DIM, RET_HEADS * HEAD_DIM,
    SWA_Q_HEADS * HEAD_DIM, SWA_KV_HEADS * HEAD_DIM, SWA_KV_HEADS * HEAD_DIM,
    N_BRANCH * D_MODEL,
)
N_IN = sum(COL_SIZES)


def rmsnorm(x, g):
    x32 = x.astype(jnp.float32)
    y = x32 * lax.rsqrt(jnp.mean(x32 * x32, axis=-1, keepdims=True) + EPS)
    return (y * g.astype(jnp.float32)).astype(x.dtype)

def rope(x, pos):
    d = x.shape[-1]
    half = d // 2
    inv = 1.0 / (ROPE_THETA ** (jnp.arange(half, dtype=jnp.float32) * 2.0 / d))
    ang = pos[:, None] * inv[None, :]
    cos = jnp.cos(ang)[None, :, None, :]
    sin = jnp.sin(ang)[None, :, None, :]
    x32 = x.astype(jnp.float32)
    x1, x2 = x32[..., :half], x32[..., half:]
    return jnp.concatenate([x1 * cos - x2 * sin, x2 * cos + x1 * sin], axis=-1).astype(x.dtype)

def to_blocks(t, nb):
    return t.reshape(t.shape[0], nb, BLOCK, *t.shape[2:]).swapaxes(0, 1)

def from_blocks(t):
    t = t.swapaxes(0, 1)
    return t.reshape(t.shape[0], t.shape[1] * t.shape[2], -1)

def forgetting_attention(q, k, v, f_logit, f_bias):
    B, S, H, d = q.shape
    nb = S // BLOCK
    neg = jnp.finfo(jnp.float32).min
    logf = jax.nn.log_sigmoid((f_logit + f_bias).astype(jnp.float32))
    F = jnp.cumsum(logf, axis=1).transpose(0, 2, 1)
    Fq_blocks = F.reshape(B, H, nb, BLOCK).transpose(2, 0, 1, 3)
    key_pos = jnp.arange(S, dtype=jnp.int32)
    scale = d ** -0.5

    def blk(inp):
        qb, Fq, off = inp
        t = off + jnp.arange(BLOCK, dtype=jnp.int32)
        logits = (jnp.einsum('bqhd,bshd->bhqs', qb, k).astype(jnp.float32) * scale
                  + Fq[..., None] - F[:, :, None, :])
        causal = key_pos[None, :] <= t[:, None]
        p = jax.nn.softmax(jnp.where(causal[None, None], logits, neg), axis=-1)
        return jnp.einsum('bhqs,bshd->bqhd', p.astype(v.dtype), v)

    offs = jnp.arange(nb, dtype=jnp.int32) * BLOCK
    out = lax.map(blk, (to_blocks(q, nb), Fq_blocks, offs))
    return from_blocks(out)

def dsa_attention(q, k, v, qi, ki, wi):
    B, S, H, d = q.shape
    nb = S // BLOCK
    topk = min(DSA_TOPK_MAX, S // 4)
    neg = jnp.finfo(jnp.float32).min
    key_pos = jnp.arange(S, dtype=jnp.int32)
    bidx = jnp.arange(B, dtype=jnp.int32)[:, None, None]
    ki32 = ki.astype(jnp.float32)
    w_scale = (IDX_HEADS ** -0.5) * (IDX_DIM ** -0.5)
    scale = d ** -0.5

    def blk(inp):
        qb, qib, wb, off = inp
        t = off + jnp.arange(BLOCK, dtype=jnp.int32)
        dots = jnp.einsum('bqhd,bsd->bqhs', qib.astype(jnp.float32), ki32)
        score = jnp.einsum('bqhs,bqh->bqs', jax.nn.relu(dots), wb.astype(jnp.float32) * w_scale)
        causal = key_pos[None, :] <= t[:, None]
        score = jnp.where(causal[None], score, neg)
        _, sel = lax.top_k(score, topk)
        kg = k[bidx, sel]
        vg = v[bidx, sel]
        logits = jnp.einsum('bqhd,bqkd->bhqk', qb, kg).astype(jnp.float32) * scale
        valid = (sel <= t[None, :, None])[:, None]
        p = jax.nn.softmax(jnp.where(valid, logits, neg), axis=-1)
        return jnp.einsum('bhqk,bqkd->bqhd', p.astype(vg.dtype), vg)

    offs = jnp.arange(nb, dtype=jnp.int32) * BLOCK
    out = lax.map(blk, (to_blocks(q, nb), to_blocks(qi, nb), to_blocks(wi, nb), offs))
    return from_blocks(out)

def retention(q, k, v):
    B, S, H, d = q.shape
    dv = v.shape[-1]
    C = BLOCK
    nc = S // C
    log_g = jnp.log(1.0 - 2.0 ** (-5.0 - jnp.arange(H, dtype=jnp.float32)))
    n = jnp.arange(C, dtype=jnp.float32)
    diff = n[:, None] - n[None, :]
    Dm = jnp.where(diff[None] >= 0, jnp.exp(diff[None] * log_g[:, None, None]), 0.0)
    xi = jnp.exp((n + 1.0)[None, :] * log_g[:, None])
    zeta = jnp.exp((C - 1.0 - n)[None, :] * log_g[:, None])
    gC = jnp.exp(C * log_g)

    def chunks(t):
        return t.reshape(B, nc, C, H, t.shape[-1]).transpose(1, 0, 3, 2, 4)

    def step(R, inp):
        qc, kc, vc = inp
        inner = jnp.einsum('bhnm,bhme->bhne', jnp.einsum('bhnd,bhmd->bhnm', qc, kc) * Dm[None], vc)
        cross = jnp.einsum('bhnd,bhde->bhne', qc, R) * xi[None, :, :, None]
        R = R * gC[None, :, None, None] + jnp.einsum('bhmd,bhme->bhde', kc * zeta[None, :, :, None], vc)
        return R, inner + cross

    R0 = jnp.zeros((B, H, d, dv), jnp.float32)
    _, ys = lax.scan(step, R0, (chunks(q), chunks(k), chunks(v)))
    return ys.transpose(1, 0, 3, 2, 4).reshape(B, S, H, dv)

def head_groupnorm(r, g):
    mu = jnp.mean(r, axis=-1, keepdims=True)
    var = jnp.mean(jnp.square(r - mu), axis=-1, keepdims=True)
    y = (r - mu) * lax.rsqrt(var + EPS)
    return y.reshape(r.shape[0], r.shape[1], -1) * g.astype(jnp.float32)

def sliding_window_gqa(q, k, v, sinks):
    B, S, HQ, d = q.shape
    HKV = k.shape[2]
    G = HQ // HKV
    W = SWA_WINDOW
    nb = S // W
    neg = jnp.finfo(jnp.float32).min
    qb = q.reshape(B, nb, W, HKV, G, d)
    kb = k.reshape(B, nb, W, HKV, d)
    vb = v.reshape(B, nb, W, HKV, d)
    shift = lambda t: jnp.concatenate([jnp.zeros_like(t[:, :1]), t[:, :-1]], axis=1)
    kband = jnp.concatenate([shift(kb), kb], axis=2)
    vband = jnp.concatenate([shift(vb), vb], axis=2)
    logits = jnp.einsum('bnqgrd,bnkgd->bngrqk', qb, kband).astype(jnp.float32) * (d ** -0.5)
    i = jnp.arange(W)[:, None]
    j = jnp.arange(2 * W)[None, :]
    in_band = (j > i) & (j <= i + W)
    kpos = jnp.arange(nb)[:, None, None] * W - W + j[None]
    mask = in_band[None] & (kpos >= 0)
    logits = jnp.where(mask[None, :, None, None], logits, neg)
    sink = sinks.astype(jnp.float32).reshape(HKV, G)[None, None, :, :, None, None]
    m = jnp.maximum(jnp.max(logits, axis=-1, keepdims=True), sink)
    p = jnp.exp(logits - m)
    denom = jnp.sum(p, axis=-1, keepdims=True) + jnp.exp(sink - m)
    out = jnp.einsum('bngrqk,bnkgd->bnqgrd', (p / denom).astype(vband.dtype), vband)
    return out.reshape(B, S, HQ * d)

def causal_dwconv(u, w, b):
    C = u.shape[-1]
    out = lax.conv_general_dilated(u, w.astype(u.dtype)[:, None, :], window_strides=(1,),
                                   padding=[(CONV_WIDTH - 1, 0)],
                                   dimension_numbers=('NWC', 'WIO', 'NWC'),
                                   feature_group_count=C)
    return out + b.astype(u.dtype)

def first_inputs(seed: int = 0) -> dict:
    key = jax.random.key(seed)
    ks = jax.random.split(key, 14)
    nrm = lambda k, shape: jax.random.normal(k, shape, jnp.float32)
    return {
        "x": nrm(ks[0], (BATCH, SEQ, D_MODEL)),
        "attn_norm": 1.0 + 0.02 * nrm(ks[1], (DEPTH, D_MODEL)),
        "w_in": nrm(ks[2], (DEPTH, D_MODEL, N_IN)) * D_MODEL ** -0.5,
        "forget_bias": 3.0 + 0.1 * nrm(ks[3], (DEPTH, FOX_HEADS)),
        "ret_norm": 1.0 + 0.02 * nrm(ks[4], (DEPTH, RET_HEADS * HEAD_DIM)),
        "attn_sinks": 0.1 * nrm(ks[5], (DEPTH, SWA_Q_HEADS)),
        "w_branch": nrm(ks[6], (DEPTH, N_BRANCH, BRANCH_WIDTH, D_MODEL)) * BRANCH_WIDTH ** -0.5,
        "w_out": nrm(ks[7], (DEPTH, D_MODEL, D_MODEL)) * D_MODEL ** -0.5,
        "ffn_norm": 1.0 + 0.02 * nrm(ks[8], (DEPTH, D_MODEL)),
        "w_up": nrm(ks[9], (DEPTH, D_MODEL, 2 * D_FF)) * D_MODEL ** -0.5,
        "conv_w": nrm(ks[10], (DEPTH, CONV_WIDTH, 2 * D_FF)) * CONV_WIDTH ** -0.5,
        "conv_b": 0.01 * nrm(ks[11], (DEPTH, 2 * D_FF)),
        "w_down": nrm(ks[12], (DEPTH, D_FF, D_MODEL)) * D_FF ** -0.5,
        "final_norm": 1.0 + 0.02 * nrm(ks[13], (D_MODEL,)),
    }

def first_block(x, attn_norm, w_in, forget_bias, ret_norm, attn_sinks, w_branch, w_out,
              ffn_norm, w_up, conv_w, conv_b, w_down, final_norm):
    B, S, D = x.shape
    pos = jnp.arange(S, dtype=jnp.float32)
    split_at = np.cumsum(COL_SIZES)[:-1].tolist()
    heads = lambda t, n: t.reshape(B, S, n, -1)
    for l in range(DEPTH):
        h = rmsnorm(x, attn_norm[l])
        z = h @ w_in[l]
        (qA, kA, vA, fA, qB, kB, vB, qI, kI, wI,
         qC, kC, vC, gC, qD, kD, vD, gates) = jnp.split(z, split_at, axis=-1)

        yA = forgetting_attention(heads(qA, FOX_HEADS), heads(kA, FOX_HEADS), heads(vA, FOX_HEADS),
                                  fA, forget_bias[l])
        yB = dsa_attention(rope(heads(qB, DSA_HEADS), pos), rope(kB[:, :, None], pos)[:, :, 0], vB,
                           rope(heads(qI, IDX_HEADS), pos), rope(kI[:, :, None], pos)[:, :, 0], wI)
        r = retention(rope(heads(qC, RET_HEADS), pos).astype(jnp.float32),
                      (rope(heads(kC, RET_HEADS), pos) * HEAD_DIM ** -0.5).astype(jnp.float32),
                      heads(vC, RET_HEADS).astype(jnp.float32))
        yC = (head_groupnorm(r, ret_norm[l]) * jax.nn.silu(gC.astype(jnp.float32))).astype(x.dtype)
        yD = sliding_window_gqa(rope(heads(qD, SWA_Q_HEADS), pos), rope(heads(kD, SWA_KV_HEADS), pos),
                                heads(vD, SWA_KV_HEADS), attn_sinks[l])

        ys = jnp.stack([yA, yB, yC, yD], axis=2)
        branch = jnp.einsum('bsnc,ncd->bsnd', ys, w_branch[l])
        g = jax.nn.sigmoid(gates.reshape(B, S, N_BRANCH, D))
        merged = jnp.sum(g * branch, axis=2)
        x = x + merged @ w_out[l]

        h = rmsnorm(x, ffn_norm[l])
        u = causal_dwconv(h @ w_up[l], conv_w[l], conv_b[l])
        a, b = jnp.split(u, 2, axis=-1)
        x = x + (jax.nn.silu(a) * b) @ w_down[l]
    return rmsnorm(x, final_norm)


DEPTH_2 = 1

GRID_W = 64
CTX_LEN = 256
MIX_W = D_MODEL
F_GROUPS = 4
F_DIM = D_MODEL // 8
FOURIER_W = F_GROUPS * F_DIM
GDN_HEADS = 4
GDN_DK = D_MODEL // 8
GDN_DV = D_MODEL // 8
QK_W = GDN_HEADS * GDN_DK
V_W = GDN_HEADS * GDN_DV
IN_W = FOURIER_W + 2 * QK_W + 2 * V_W + 4 * GDN_HEADS
SHORT_CONV = 3
CHUNK = 64
D_FF_2 = ((8 * D_MODEL // 3 + 127) // 128) * 128


def rmsnorm_2(t, g):
    tf = t.astype(jnp.float32)
    y = tf * lax.rsqrt(jnp.mean(tf * tf, axis=-1, keepdims=True) + EPS)
    return y.astype(t.dtype) * g

def l2norm(t):
    tf = t.astype(jnp.float32)
    return (tf * lax.rsqrt(jnp.sum(tf * tf, axis=-1, keepdims=True) + EPS)).astype(t.dtype)

def modulate(h, shift, scale):
    return h * (1 + scale) + shift

def dwconv1d(t, w):
    k_w = w.shape[0]
    pad = k_w // 2
    length = t.shape[1]
    tp = jnp.pad(t, ((0, 0), (pad, pad), (0, 0)))
    out = tp[:, 0:length] * w[0]
    for j in range(1, k_w):
        out = out + tp[:, j:j + length] * w[j]
    return out

def gated_delta_chunked(q, k, v, beta, g, s0):
    f32 = jnp.float32
    bsz, length, heads, dk = q.shape
    dv = v.shape[-1]
    n_chunks = length // CHUNK

    def chunks(t):
        t = t.astype(f32).reshape(bsz, n_chunks, CHUNK, heads, t.shape[-1])
        return jnp.transpose(t, (1, 0, 3, 2, 4))

    def chunks_s(t):
        t = t.astype(f32).reshape(bsz, n_chunks, CHUNK, heads)
        return jnp.transpose(t, (1, 0, 3, 2))

    qc = chunks(q) * (dk ** -0.5)
    kc = chunks(k)
    vc = chunks(v)
    bc = chunks_s(beta)
    gc = jnp.cumsum(chunks_s(g), axis=-1)
    lower = jnp.tril(jnp.ones((CHUNK, CHUNK), dtype=bool))
    strict = jnp.tril(jnp.ones((CHUNK, CHUNK), dtype=bool), -1)
    diff = gc[..., :, None] - gc[..., None, :]
    decay = jnp.where(lower, jnp.exp(jnp.where(lower, diff, 0.0)), 0.0)

    kb = kc * bc[..., None]
    vb = vc * bc[..., None]
    a_mat = jnp.where(strict, jnp.einsum('nbhid,nbhjd->nbhij', kb, kc) * decay, 0.0)
    eye = jnp.eye(CHUNK, dtype=f32)
    t_inv = lax.linalg.triangular_solve(eye + a_mat, jnp.broadcast_to(eye, a_mat.shape),
                                        left_side=True, lower=True, unit_diagonal=True)
    u_val = jnp.einsum('nbhij,nbhjd->nbhid', t_inv, vb)
    w_key = jnp.einsum('nbhij,nbhjd->nbhid', t_inv, kb * jnp.exp(gc)[..., None])
    attn_intra = jnp.where(lower, jnp.einsum('nbhid,nbhjd->nbhij', qc, kc) * decay, 0.0)
    g_last = gc[..., -1]
    k_dec = kc * jnp.exp(g_last[..., None] - gc)[..., None]
    q_dec = qc * jnp.exp(gc)[..., None]

    def step(s, xs):
        u_i, w_i, a_i, qd_i, kd_i, gl_i = xs
        v_new = u_i - jnp.einsum('bhcd,bhde->bhce', w_i, s)
        o_i = jnp.einsum('bhcd,bhde->bhce', qd_i, s) + jnp.einsum('bhij,bhje->bhie', a_i, v_new)
        s = s * jnp.exp(gl_i)[..., None, None] + jnp.einsum('bhcd,bhce->bhde', kd_i, v_new)
        return s, o_i

    s_final, o = lax.scan(step, s0.astype(f32), (u_val, w_key, attn_intra, q_dec, k_dec, g_last))
    o = jnp.transpose(o, (1, 0, 3, 2, 4)).reshape(bsz, length, heads, dv)
    return o.astype(v.dtype), s_final

def bidir_gdn(q, k, v, beta, g, s0_f, s0_b):
    flip = lambda t: jnp.flip(t, axis=1)
    o_f, s_f = gated_delta_chunked(q, k, v, beta[:, :, 0], g[:, :, 0], s0_f)
    o_b, s_b = gated_delta_chunked(flip(q), flip(k), flip(v), flip(beta[:, :, 1]), flip(g[:, :, 1]), s0_b)
    return o_f + flip(o_b), s_f, s_b

def mixer_inputs(h, w_in_l, conv_l, a_log_l, dt_bias_l):
    bsz, length, _ = h.shape
    p = h @ w_in_l
    o1 = FOURIER_W
    o2 = o1 + 2 * QK_W + V_W
    o3 = o2 + V_W
    u = p[..., :o1]
    qkv = jax.nn.silu(dwconv1d(p[..., o1:o2], conv_l))
    z = p[..., o2:o3]
    ab = p[..., o3:].astype(jnp.float32).reshape(bsz, length, 4, GDN_HEADS)
    q = l2norm(qkv[..., :QK_W].reshape(bsz, length, GDN_HEADS, GDN_DK))
    k = l2norm(qkv[..., QK_W:2 * QK_W].reshape(bsz, length, GDN_HEADS, GDN_DK))
    v = qkv[..., 2 * QK_W:].reshape(bsz, length, GDN_HEADS, GDN_DV)
    beta = jax.nn.sigmoid(ab[:, :, 0:2])
    g = -jnp.exp(a_log_l.astype(jnp.float32)) * jax.nn.softplus(ab[:, :, 2:4] + dt_bias_l.astype(jnp.float32))
    return u, z, q, k, v, beta, g

def fourier_mix(u, w_f):
    bsz, length, _ = u.shape
    ug = u.astype(jnp.float32).reshape(bsz, length, F_GROUPS, F_DIM)
    y = jnp.fft.fft2(ug, axes=(1, 3), norm='ortho').real.astype(u.dtype)
    return jnp.einsum('blgc,gcd->blgd', y, w_f).reshape(bsz, length, FOURIER_W)

def mixer_out(u, o, z, w_f, g_gdn_l, w_out_l):
    bsz, length, _ = z.shape
    y_f = fourier_mix(u, w_f)
    y_d = rmsnorm_2(o, g_gdn_l) * jax.nn.silu(z).reshape(bsz, length, GDN_HEADS, GDN_DV)
    return jnp.concatenate([y_f, y_d.reshape(bsz, length, V_W)], axis=-1) @ w_out_l

def conv_ffn(h, w_up_l, w_dwc_l, w_down_l, on_grid):
    bsz, length, _ = h.shape
    p = h @ w_up_l
    val, gate = p[..., :D_FF_2], p[..., D_FF_2:]
    if on_grid:
        rows = length // GRID_W
        gate = lax.conv_general_dilated(
            gate.reshape(bsz, rows, GRID_W, D_FF_2), w_dwc_l[:, :, None, :],
            window_strides=(1, 1), padding='SAME',
            dimension_numbers=('NHWC', 'HWIO', 'NHWC'),
            feature_group_count=D_FF_2).reshape(bsz, length, D_FF_2)
    else:
        gate = dwconv1d(gate, w_dwc_l[1])
    return (jax.nn.silu(gate) * val) @ w_down_l

def second_inputs(seed: int = 0) -> dict:
    key = jax.random.key(seed)
    ks = jax.random.split(key, 20)
    f32 = jnp.float32

    def nrm(k, shape, s):
        return jax.random.normal(k, shape, f32) * s

    L = DEPTH_2
    x = nrm(ks[0], (BATCH, SEQ, D_MODEL), 1.0)
    c = nrm(ks[1], (BATCH, D_MODEL), 1.0)
    ctx = nrm(ks[2], (BATCH, CTX_LEN, D_MODEL), 1.0)
    c_ctx = nrm(ks[3], (D_MODEL,), 1.0)
    w_ada = nrm(ks[4], (L, D_MODEL, 6 * D_MODEL), 0.5 * D_MODEL ** -0.5)
    b_ada = nrm(ks[5], (L, 6 * D_MODEL), 0.02)
    g_pre_mix = 1.0 + nrm(ks[6], (L, D_MODEL), 0.1)
    g_post_mix = 1.0 + nrm(ks[7], (L, D_MODEL), 0.1)
    g_pre_ffn = 1.0 + nrm(ks[8], (L, D_MODEL), 0.1)
    g_post_ffn = 1.0 + nrm(ks[9], (L, D_MODEL), 0.1)
    w_in = nrm(ks[10], (L, D_MODEL, IN_W), D_MODEL ** -0.5)
    w_qkv_conv = nrm(ks[11], (L, SHORT_CONV, 2 * QK_W + V_W), SHORT_CONV ** -0.5)
    a_log = jnp.log(jax.random.uniform(ks[12], (L, 2, GDN_HEADS), f32, minval=1.0, maxval=16.0))
    dt = jnp.exp(jax.random.uniform(ks[13], (L, 2, GDN_HEADS), f32,
                                    minval=math.log(1e-3), maxval=math.log(1e-1)))
    dt_bias = dt + jnp.log(-jnp.expm1(-dt))
    g_gdn = 1.0 + nrm(ks[14], (L, GDN_DV), 0.1)
    w_fourier = nrm(ks[15], (L, F_GROUPS, F_DIM, F_DIM), F_DIM ** -0.5)
    w_out = nrm(ks[16], (L, MIX_W, D_MODEL), MIX_W ** -0.5)
    w_up = nrm(ks[17], (L, D_MODEL, 2 * D_FF_2), D_MODEL ** -0.5)
    w_dwc = nrm(ks[18], (L, 3, 3, D_FF_2), 1.0 / 3.0)
    w_down = nrm(ks[19], (L, D_FF_2, D_MODEL), D_FF_2 ** -0.5)
    return {"x": x, "c": c, "ctx": ctx, "c_ctx": c_ctx, "w_ada": w_ada, "b_ada": b_ada,
            "g_pre_mix": g_pre_mix, "g_post_mix": g_post_mix, "g_pre_ffn": g_pre_ffn,
            "g_post_ffn": g_post_ffn, "w_in": w_in, "w_qkv_conv": w_qkv_conv, "a_log": a_log,
            "dt_bias": dt_bias, "g_gdn": g_gdn, "w_fourier": w_fourier, "w_out": w_out,
            "w_up": w_up, "w_dwc": w_dwc, "w_down": w_down}

def second_block(x, c, ctx, c_ctx, w_ada, b_ada, g_pre_mix, g_post_mix, g_pre_ffn, g_post_ffn,
              w_in, w_qkv_conv, a_log, dt_bias, g_gdn, w_fourier, w_out, w_up, w_dwc, w_down):
    xl, xc = x, ctx
    bsz = x.shape[0]
    silu_c = jax.nn.silu(c)
    silu_cc = jax.nn.silu(c_ctx)
    for i in range(DEPTH_2):
        update_ctx = i < DEPTH_2 - 1
        mod_l = (silu_c @ w_ada[i] + b_ada[i])[:, None, :]
        mod_c = silu_cc @ w_ada[i] + b_ada[i]
        sh1l, sc1l, gt1l, sh2l, sc2l, gt2l = jnp.split(mod_l, 6, axis=-1)
        sh1c, sc1c, gt1c, sh2c, sc2c, gt2c = jnp.split(mod_c, 6, axis=-1)

        hl = modulate(rmsnorm_2(xl, g_pre_mix[i]), sh1l, sc1l)
        hc = modulate(rmsnorm_2(xc, g_pre_mix[i]), sh1c, sc1c)
        ul, zl, ql, kl, vl, bl, gl = mixer_inputs(hl, w_in[i], w_qkv_conv[i], a_log[i], dt_bias[i])
        uc, zc, qc, kc, vc, bc, gc = mixer_inputs(hc, w_in[i], w_qkv_conv[i], a_log[i], dt_bias[i])
        s_zero = jnp.zeros((bsz, GDN_HEADS, GDN_DK, GDN_DV), jnp.float32)
        oc, s_f, s_b = bidir_gdn(qc, kc, vc, bc, gc, s_zero, s_zero)
        ol, _, _ = bidir_gdn(ql, kl, vl, bl, gl, s_f, s_b)
        yl = mixer_out(ul, ol, zl, w_fourier[i], g_gdn[i], w_out[i])
        xl = xl + gt1l * rmsnorm_2(yl, g_post_mix[i])
        if update_ctx:
            yc = mixer_out(uc, oc, zc, w_fourier[i], g_gdn[i], w_out[i])
            xc = xc + gt1c * rmsnorm_2(yc, g_post_mix[i])

        hl = modulate(rmsnorm_2(xl, g_pre_ffn[i]), sh2l, sc2l)
        xl = xl + gt2l * rmsnorm_2(conv_ffn(hl, w_up[i], w_dwc[i], w_down[i], True), g_post_ffn[i])
        if update_ctx:
            hc = modulate(rmsnorm_2(xc, g_pre_ffn[i]), sh2c, sc2c)
            xc = xc + gt2c * rmsnorm_2(conv_ffn(hc, w_up[i], w_dwc[i], w_down[i], False), g_post_ffn[i])
    return xl


def setup_inputs(seed=0):
    out = dict(first_inputs(seed))
    for name, value in second_inputs(seed + 1).items():
        if name != "x":
            out[name + "_2"] = value
    return out


def reference(
    x, attn_norm, w_in, forget_bias, ret_norm, attn_sinks, w_branch, w_out, ffn_norm, w_up,
    conv_w, conv_b, w_down, final_norm, c_2, ctx_2, c_ctx_2, w_ada_2, b_ada_2, g_pre_mix_2,
    g_post_mix_2, g_pre_ffn_2, g_post_ffn_2, w_in_2, w_qkv_conv_2, a_log_2, dt_bias_2, g_gdn_2,
    w_fourier_2, w_out_2, w_up_2, w_dwc_2, w_down_2,
):
    x = first_block(
        x, attn_norm, w_in, forget_bias, ret_norm, attn_sinks, w_branch, w_out, ffn_norm, w_up,
        conv_w, conv_b, w_down, final_norm,
    )
    return second_block(
        x, c_2, ctx_2, c_ctx_2, w_ada_2, b_ada_2, g_pre_mix_2, g_post_mix_2, g_pre_ffn_2,
        g_post_ffn_2, w_in_2, w_qkv_conv_2, a_log_2, dt_bias_2, g_gdn_2, w_fourier_2, w_out_2,
        w_up_2, w_dwc_2, w_down_2,
    )


_drawn_inputs = setup_inputs


def setup_inputs(seed=0):
    import zlib

    import numpy as np

    out = dict(_drawn_inputs(seed))
    spreads = {}
    factors = {'ret_norm': 4.931,
     'attn_sinks': 35.136,
     'conv_b': 4.493,
     'ctx_2': 4.5,
     'c_ctx_2': 8.0,
     'g_gdn_2': 2.889,
     'forget_bias': 34.28,
     'ffn_norm': 3.412}
    for name, (base, spread) in spreads.items():
        noise = np.random.default_rng([zlib.crc32(name.encode()), seed]).standard_normal(out[name].shape)
        drawn = base * np.exp(spread * noise) if base else spread * noise
        out[name] = __import__('jax').numpy.asarray(drawn.astype(out[name].dtype))
    for name, factor in factors.items():
        out[name] = (out[name] * factor).astype(out[name].dtype)
    return out
```

```python
from contextlib import ExitStack

import numpy as np

import concourse.bass as bass
from concourse import mybir

F32 = mybir.dt.float32
ALU = mybir.AluOpType
ACT = mybir.ActivationFunctionType
AX_X = mybir.AxisListType.X

P = 128
D_MODEL, SEQ, DEPTH = 1024, 512, 2
KC = D_MODEL // P
TB = SEQ // P
HEAD_DIM, HEADS, IDX_HEADS, N_BRANCH = 64, 8, 4, 4
PAIRS = HEADS // 2
D_FF = 2816
FC = D_FF // P
TOPK = min(256, SEQ // 4)
EPS = 1e-6
NEG = -1e30
TAKEN = -3e38
QK_SCALE = HEAD_DIM ** -0.5

LAYER = [
    ("norm1", 1, 0, 1), ("pre", 1, 5, 5), ("A", PAIRS, 5, 5), ("B", PAIRS, 3, 3), ("Dkv", 1, 2, 2),
    ("D", PAIRS, 3, 3), ("C", PAIRS, 7, 6), ("merge", KC, 2, 4), ("out", KC // 2, 2, 2),
    ("norm2", 1, 0, 1), ("up", FC, 2, 2), ("down", 2, 11, 4),
]
TAIL = [
    ("normf", 1, 0, 1), ("ada", 6, 8, 8), ("normL", 1, 0, 1), ("normX", 1, 0, 1), ("ab", 1, 1, 1),
    ("qkv", 12, 1, 2), ("uz", 4, 2, 2), ("four", 1, 5, 14), ("out2", KC // 2, 2, 2), ("norm3", 1, 0, 1),
    ("norm4", 1, 0, 1), ("up2", FC, 2, 2), ("down2", 2, 11, 4), ("norm5", 1, 0, 1),
]
UNBANKED = ("ada",)
CTX = 256
GH, GD, CHUNK = 4, 128, 64
XB = (SEQ + CTX) // P
LEVELS = 6
GRID_W = 64
ORDER = ([4, 5, 0, 1, 2, 3], [5, 4, 3, 2, 1, 0])
UNITS = 6
FIRST_L = 2
ADA_N = 6 * KC
SLOTS = 6
OPEN = 1
BANKS = 2
PV_LAG, TR_LAG = 3, 2
STEPS = 2 * TB
GATE_STEPS = [2, 2, 2, 2, 1, 1, 1, 1, 1, 1, 1]
GATE_TAIL = 2 * KC - sum(GATE_STEPS)
RET_GATES = [2, 2, 2, 2, 1, 1, 1, 1, 0]
GATE0_AT = 5
DECAY_ITEM = 6
TOK_COLS = HEAD_DIM + HEADS + IDX_HEADS
IDX_SCALE = IDX_HEADS ** -0.5 * HEAD_DIM ** -0.5
FFT_SCALE = (SEQ * GD) ** -0.5
INITS = 6
BRANCH = {"A": 0, "B": 1, "C": 2, "D": 3}


def item_result(name, j):
    if name == "merge":
        return 2 * j + 1
    if name == "qkv":
        return 1
    if name == "four":
        return 13 if j else 1
    if name in ("down", "down2"):
        return (KC * j + KC - 1) // FC
    return min(j, RESULTS[name] - 1)


class Plan:

    def __init__(self):
        self.item_base, self.out_base, self.slot_base, self.bank_base, self.items = {}, {}, {}, {}, {}
        for table in (LAYER, TAIL):
            n = m = 0
            slot, bank = [0] * SLOTS, [0] * BANKS
            for name, turns, items, outs in table:
                self.item_base[name], self.out_base[name], self.items[name] = n, m, items
                self.slot_base[name], self.bank_base[name] = list(slot), list(bank)
                for j in range(items):
                    slot[j % SLOTS] += turns
                for j in range(0 if name in UNBANKED else outs):
                    bank[j % BANKS] += turns
                n += turns * items
                m += turns * outs
            if table is LAYER:
                self.layer_items, self.layer_outs, self.layer_slot, self.layer_bank = n, m, slot, bank
            self.tail_items = n
        self.total_items = DEPTH * self.layer_items + self.tail_items
        self.slack, done = {}, {}
        for layer, table in [(l, LAYER) for l in range(DEPTH)] + [(DEPTH, TAIL)]:
            for name, turns, items, _ in table:
                for turn in range(turns):
                    first = self.result(name, layer, turn, 0)
                    for j in range(items):
                        key, s = (name, j), j % SLOTS
                        room = min(first, first - done[s] if s in done else first)
                        self.slack[key] = min(self.slack.get(key, room), room)
                        done[s] = self.result(name, layer, turn, item_result(name, j)) + 1

    def item(self, name, layer, turn, j):
        return layer * self.layer_items + turn * self.items[name] + (self.item_base[name] + j)

    def slot_free(self, name, layer, turn, j):
        return self.result(name, layer, turn, 0) + (OPEN - self.slack[name, j])

    def done(self, name, layer, turn, j):
        return self.result(name, layer, turn, j) + (OPEN + 1)

    def landed(self, name, layer, turn, j):
        s = j % SLOTS
        per = len(range(s, self.items[name], SLOTS))
        return s, (layer * (16 * self.layer_slot[s]) + turn * (16 * per)
                   + 16 * (self.slot_base[name][s] + j // SLOTS + 1))

    def result(self, name, layer, turn, j):
        return layer * self.layer_outs + turn * RESULTS[name] + (self.out_base[name] + j)

    def bank(self, name, layer, turn, j):
        b = j % BANKS
        per = len(range(b, RESULTS[name], BANKS))
        return b, layer * self.layer_bank[b] + turn * per + (self.bank_base[name][b] + j // BANKS + OPEN)


RESULTS = {name: outs for name, _, _, outs in LAYER + TAIL}
PLAN = Plan()


def held_before(name, layer, b):
    return layer * PLAN.layer_bank[b] + (PLAN.bank_base[name][b] + OPEN)


SMALL = {}


def _place_small():
    at = 0
    for name, n in (("attn_norm", DEPTH * KC), ("ffn_norm", DEPTH * KC), ("ret_norm", DEPTH * PAIRS),
                    ("forget_bias", DEPTH * HEADS), ("sinks", DEPTH * HEADS), ("final_norm", KC),
                    ("conv", DEPTH * 2 * FC * 4), ("b_ada", ADA_N), ("g_pre_mix", KC), ("g_post_mix", KC),
                    ("g_pre_ffn", KC), ("g_post_ffn", KC), ("g_gdn", 1), ("a_log", 2 * GH),
                    ("dt_bias", 2 * GH), ("qkv_conv", 12 * 3), ("dwc", FC * 9), ("cond", KC * 2)):
        SMALL[name] = at
        at += n
    return at


SMALL_N = _place_small()
CONSTS = {"cos": 512, "sin": 512, "ident": 128, "causal": 128, "before": 128, "tri": 512,
          "barred": 2 * 128, "upto": 2 * 128, "chunk_ones": 128, "levels": 2 * LEVELS * 128}
CONST_AT = dict(zip(CONSTS, np.cumsum([0] + list(CONSTS.values()))[:-1].tolist()))
CONST_N = sum(CONSTS.values())


def build_program(nc, x_in, stream, small_in, const_in, ctx_in, out):
    with ExitStack() as ctx:
        def sb(name, shape):
            return ctx.enter_context(nc.sbuf_tensor(name, shape, F32))

        def sem(name):
            return ctx.enter_context(nc.semaphore(name))

        xT = sb("xT", [P, KC, SEQ])
        hT = sb("hT", [P, KC, SEQ])
        gates = sb("gates", [P, N_BRANCH * KC, SEQ])
        yT = sb("yT", [P, N_BRANCH * PAIRS, SEQ])
        ring = sb("ring", [P, SLOTS, KC * P])
        small = sb("small_sb", [P, SMALL_N])
        const = sb("const_sb", [P, CONST_N])
        qT, kT = sb("qT", [P, SEQ]), sb("kT", [P, SEQ])
        vt = sb("vt", [P, TB, P])
        kB, kI = sb("kB", [P, SEQ]), sb("kI", [P, SEQ])
        qI = sb("qI", [P, 2, SEQ])
        tok = sb("tok", [P, TB, P])
        swapped, swapped_sin = sb("swapped", [P, SEQ]), sb("swapped_sin", [P, SEQ])
        probs = sb("probs", [P, 2, SEQ])
        probsT = sb("probsT", [P, 2, SEQ])
        Y = sb("Y", [P, SEQ])
        gC = sb("gC", [P, SEQ])
        ones = sb("ones", [P, P])
        halves = sb("halves", [P, HEADS])
        row_max, neg_max = sb("row_max", [P, STEPS]), sb("neg_max", [P, STEPS])
        row_sum, sink_exp = sb("row_sum", [P, STEPS]), sb("sink_exp", [P, STEPS])
        inv_sum = sb("inv_sum", [P, STEPS])
        mean, var, inv_std = sb("mean", [P, STEPS]), sb("var", [P, STEPS]), sb("inv_std", [P, STEPS])
        neg_sink = sb("neg_sink", [P, DEPTH * HEADS])
        half_gain = sb("half_gain", [P, DEPTH * PAIRS])
        top8 = sb("top8", [P, TB, 8])
        logf = sb("logf", [P, 4, TB * HEADS])
        act_T = gates
        negF = gates
        NEGF = BRANCH["C"] * KC
        sel = yT
        SEL = BRANCH["C"] * PAIRS
        cos, sin, ident, causal, before, tri, barred, upto, chunk_ones, levels = (
            const[:, CONST_AT[k]:CONST_AT[k] + CONSTS[k]] for k in CONSTS)

        flat = gates[:].rearrange("p a n -> p (a n)")
        hx = flat[:, 0:KC * XB * P].rearrange("p (k n) -> p k n", k=KC)
        cv_flat = flat[:, KC * XB * P:KC * XB * P + 12 * XB * P]
        cv = cv_flat.rearrange("p (c n) -> p c n", c=12)
        ktok = flat[:, 0:XB * SEQ].rearrange("p (t n) -> p t n", t=XB)
        vtok = flat[:, XB * SEQ:2 * XB * SEQ].rearrange("p (t n) -> p t n", t=XB)
        khT = cv_flat[:, 8 * XB * P:12 * XB * P].rearrange("p (t n) -> p t n", t=XB)
        uT, zT = yT[:, 0:4, :], yT[:, 4:8, :]
        xc = yT[:, 8:12, :].rearrange("p a (b n) -> p (a b) n", n=CTX)
        free = ([hT[:, k, :] for k in range(KC)] + [qT[:], kT[:], vt[:].rearrange("p t n -> p (t n)"), kB[:], kI[:],
                qI[:, 0, :], qI[:, 1, :], tok[:].rearrange("p t n -> p (t n)"), swapped[:], swapped_sin[:],
                probs[:, 0, :], probs[:, 1, :], probsT[:, 0, :], probsT[:, 1, :]]
                + [yT[:, k, :] for k in range(8, 16)] + [gates[:, 30, :], gates[:, 31, :]])
        names = ("decay", "A", "A_level", "T", "TT", "Z", "X", "wT", "u", "kd", "attnT", "vnew", "oscan")
        W2 = {name: (free[2 * i], free[2 * i + 1]) for i, name in enumerate(names)}
        state = (free[26], free[27])
        o2 = free[28:32]
        wc, ws, p1, p2 = W2["A_level"] + W2["Z"]
        mod = sb("mod", [P, ADA_N * 2])
        cond_tanh, cond = sb("cond_tanh", [P, KC * 2]), sb("cond", [P, KC * 2])
        gain = sb("gain", [P, 5, KC])
        dead_at = [0]

        def over_rope(n):
            at = dead_at[0]
            dead_at[0] += n
            assert dead_at[0] <= 2 * SEQ
            return const[:, at:at + n]
        SC = 2 * XB * GH
        abt = over_rope(XB * 16)
        zz, gg, beta, half_beta, gcum, egc, ed, bs, bg, eqs = (over_rope(SC) for _ in range(10))
        tmp_sc = over_rope(2 * SC)
        etot = over_rope(2 * SC)
        decay_rate = over_rope(2 * GH)
        l2s, l2v = over_rope(8 * XB), over_rope(8 * XB)
        qs = over_rope(XB * GH)
        osum, oscale = over_rope(TB * GH), over_rope(TB * GH)
        minus_half = sb("minus_half", [P, 8 * XB])
        half_gdn = sb("half_gdn", [P, 1])

        def psum(name, shape):
            return ctx.enter_context(nc.psum_tensor(name, shape, F32))
        dense = psum("dense", [P, BANKS, SEQ])
        scores = psum("scores", [P, 2, SEQ])
        turned = psum("turned", [P, 2, SEQ])
        O = psum("O", [P, SEQ])
        Yt = psum("Yt", [P, SEQ])

        s_x, s_small, s_const, s_store = sem("x_landed"), sem("small_landed"), sem("const_landed"), sem("stored")
        landed = [sem(f"item_landed{s}") for s in range(SLOTS)]
        dense_done = sem("dense_done")
        evacuated = [sem(f"dense_evacuated{b}") for b in range(BANKS)]
        s_init = sem("init_done")
        squared, square_used, norm_root, norm_inv, h_ready = (
            sem("squared"), sem("square_used"), sem("norm_root"), sem("norm_inv"), sem("h_ready"))
        swap_ready, swap_mul, rope_done = sem("swap_ready"), sem("swap_mul"), sem("rope_done")
        f_sum, f_abs, f_exp, f_ln, f_log, f_bcast, f_copied = (
            sem("f_sum"), sem("f_abs"), sem("f_exp"), sem("f_ln"), sem("f_log"), sem("f_bcast"),
            sem("f_copied"))
        dots_ready, relu_ready, score_step, topk_step = (
            sem("dots_ready"), sem("relu_ready"), sem("score_step"), sem("topk_step"))
        scores_ready, logits_ready, negmax_ready, probs_ready, turned_ready, turned_copied, pv_done = (
            sem("scores_ready"), sem("logits_ready"), sem("negmax_ready"), sem("probs_ready"),
            sem("turned_ready"), sem("turned_copied"), sem("pv_done"))
        settled = sem("wait_taken")
        biased = sem("scores_biased")
        y_sum, y_inv, y_norm, y_turned, y_stored = (
            sem("y_sum"), sem("y_inv"), sem("y_norm"), sem("y_turned"), sem("y_stored"))
        st_ready, st_decayed, rv_done, gc_tanh = (
            sem("st_ready"), sem("st_decayed"), sem("rv_done"), sem("gc_tanh"))
        gn_step, gn_pow, yc_norm, yc_turned, yc_stored = (
            sem("gn_step"), sem("gn_pow"), sem("yc_norm"), sem("yc_turned"), sem("yc_stored"))
        merge_add = sem("merge_add")
        s_ctx, cond_step, mod_step, h_scaled, x_added = (
            sem("ctx_landed"), sem("cond_step"), sem("mod_step"), sem("h_scaled"), sem("x_added"))
        ab_step, ab_act, ab_sums, l2_squared, l2_used, l2_sums, l2_var, l2_ready = (
            sem("ab_step"), sem("ab_act"), sem("ab_sums"), sem("l2_squared"), sem("l2_used"), sem("l2_sums"),
            sem("l2_var"), sem("l2_ready"))
        cq_taps, cq_tanh, cq_done, cq_conv, z_tanh, z_done = (
            sem("cq_taps"), sem("cq_tanh"), sem("cq_done"), sem("cq_conv"), sem("z_tanh"), sem("z_done"))
        v_turned, v_stored, k_turned, k_scaled, kh_turned, kh_stored = (
            sem("v_turned"), sem("v_stored"), sem("k_turned"), sem("k_scaled"), sem("kh_turned"), sem("kh_stored"))
        two = lambda name: (sem(name + "_fwd"), sem(name + "_bwd"))
        u_row, u_diff, u_decay, u_kk, u_a, u_qk, u_x, u_xt, u_attn, u_t0, u_t, u_tt, u_ttc = (
            two(n) for n in ("u_row", "u_diff", "u_decay", "u_kk", "u_a", "u_qk", "u_x", "u_xt", "u_attn", "u_t0",
                             "u_t", "u_tt", "u_ttc"))
        u_as, u_z, u_zc, u_upd, u_lvl, u_kv, u_wu, u_w, u_u = (
            two(n) for n in ("u_as", "u_z", "u_zc", "u_upd", "u_lvl", "u_kv", "u_wu", "u_w", "u_u"))
        c_ws, c_v, c_sd, c_s, c_oi, c_o1, c_o2, c_o3 = (
            two(n) for n in ("c_ws", "c_v", "c_sd", "c_s", "c_oi", "c_o1", "c_o2", "c_o3"))
        p_sq, p_red, p_ms, p_pow, p_on, p_turned, p_y = (
            sem(n) for n in ("p_sq", "p_red", "p_ms", "p_pow", "p_on", "p_turned", "p_y"))
        grid_step = sem("grid_step")
        taps, conv_step, up_tanh, up_gate, hidden_ready = (
            sem("taps"), sem("conv_step"), sem("up_tanh"), sem("up_gate"), sem("hidden_ready"))

        ATT = ("A", "B", "D")
        ROPES = 4 + 4 + 1 + 4 + 8
        ROPE_BASE = {"pre": 0, "B": 4, "Dkv": 8, "D": 9, "C": 13}
        DOTS = (TB - 1) * IDX_HEADS
        TOPK_ROUNDS = TOPK // 8
        TOPK_STEPS = 2 * TOPK_ROUNDS * (TB - 1) + 2 * (TB - 1) + 1
        GN_STEPS = 6

        def att_turn(name, layer, c):
            return layer * (3 * PAIRS) + c + ATT.index(name) * PAIRS

        def rope_no(name, layer, c, j=0):
            per = {"pre": 4, "B": 1, "Dkv": 1, "D": 1, "C": 2}[name]
            return layer * ROPES + c * per + (ROPE_BASE[name] + j)

        def key_range(name, i):
            return (max(0, i - 1) * P if name == "D" else 0), (i + 1) * P

        def gate_index(name, c):
            return 2 * c + BRANCH[name] * KC

        bankA = (scores[:, 0, :], scores[:, 1, :])
        bankB = (turned[:, 0, :], turned[:, 1, :])
        bankC = (O[:], Yt[:])
        N_F, N_L, N_X, N_3, N_4, N_5 = (2 * DEPTH + i for i in range(6))

        SQ4 = W2["A_level"] + W2["Z"]

        def sc3(t, d):
            return t[:, d * XB * GH:(d + 1) * XB * GH].rearrange("p (t h) -> p t h", h=GH)

        def level_mask(d, lev):
            at = (d * LEVELS + lev) * P
            return levels[:, at:at + P].unsqueeze(1).broadcast_to((P, GH, P))

        def heads(t):
            return t.rearrange("p (h n) -> p h n", h=GH)

        def per_head(cols):
            return cols.unsqueeze(2).broadcast_to((cols.shape[0], GH, GD))

        def sc_at(t, d, b):
            at = (d * XB + b) * GH
            return t[:, at:at + GH]

        def etot_at(c, d, b, h):
            at = (c * 2 * XB + d * XB + b) * GH + h
            return etot[:, at:at + 1]

        def chunk_of(d, i):
            c = i if d == 0 else 1 - i
            return c, slice(CHUNK * c, CHUNK * (c + 1))

        def seen(n, i=-1):
            return 2 * (n - FIRST_L) + i + 1

        block = ctx.enter_context(nc.Block())


        def settle(eng):
            eng.sem_inc(settled, 1)

        def softmax_scores(name):
            return QK_SCALE if name == "D" else 1.0

        @block.sync
        def _(sp):
            for freed in (dense_done, swap_mul, rope_done, y_stored, yc_stored, yc_norm, up_gate, hidden_ready,
                          merge_add, cq_done, z_done, *evacuated):
                sp.sem_inc(freed, OPEN)
            sp.dma_start(xT[:], x_in).then_inc(s_x, 16)
            sp.dma_start(small[:], small_in).then_inc(s_small, 16)
            sp.dma_start(const[:], const_in).then_inc(s_const, 16)

            def load(name, l, c):
                for j in range(PLAN.items[name]):
                    s, _ = PLAN.landed(name, l, c, j)
                    at = sp.snap(PLAN.item(name, l, c, j))
                    free = sp.snap(PLAN.slot_free(name, l, c, j))
                    if name in ("C", "merge"):
                        decays = sp.snap(l * PAIRS + (c + OPEN if name == "C" else PAIRS + OPEN))
                    if name in ("C", "merge") and s == DECAY_ITEM % SLOTS:
                        sp.wait_ge(yc_norm, decays)
                        settle(sp)
                    sp.wait_ge(dense_done, free)
                    sp.dma_start(ring[:, s:s + 1, :], stream[bass.ds(at, 1)].rearrange("a p n -> p a n")
                                 ).then_inc(landed[s], 16)

            with sp.Fori(0, DEPTH) as l:
                for name, turns, items, _ in LAYER:
                    if items and turns == 1:
                        load(name, l, 0)
                    elif items:
                        with sp.Fori(0, turns) as c:
                            load(name, l, c)
            sp.wait_ge(dense_done, PLAN.done("merge", DEPTH - 1, KC - 1, N_BRANCH - 1))
            sp.dma_start(xc, ctx_in).then_inc(s_ctx, 16)
            for name, turns, items, _ in TAIL:
                if items and turns == 1:
                    load(name, DEPTH, 0)
                elif items:
                    with sp.Fori(0, turns) as c:
                        load(name, DEPTH, c)
            sp.wait_ge(x_added, 2 * KC)
            sp.dma_start(out, xT[:]).then_inc(s_store, 16)
            sp.wait_ge(s_store, 16)

        @block.tensor
        def _(pe):
            def open_bank(name, l, c, j):
                b, held = PLAN.bank(name, l, c, j)
                pe.wait_ge(evacuated[b], held)
                return b

            def evac_wait(name, l, c, j):
                b, held = PLAN.bank(name, l, c, j)
                pe.wait_ge(evacuated[b], held + 1)

            def part(name, l, c, j, out_j, k, token_major=False, cols=P):
                s, b = j % SLOTS, out_j % BANKS
                if k == 0:
                    open_bank(name, l, c, out_j)
                    pe.wait_ge(landed[s], PLAN.landed(name, l, c, j)[1])
                if token_major:
                    for t in range(TB):
                        last = nc.tensor.matmul(dense[:, b, t * P:t * P + cols], hT[:, k, t * P:(t + 1) * P],
                                                ring[:, s, k * P:k * P + cols], start=(k == 0 and t == 0),
                                                stop=True, skip_group_check=True)
                else:
                    last = nc.tensor.matmul(dense[:, b, :], ring[:, s, k * P:(k + 1) * P], hT[:, k, :],
                                            start=(k == 0), stop=(k == KC - 1))
                if k == KC - 1:
                    last.then_inc(dense_done, 1)

            def product(name, l, c, j, token_major=False, cols=P):
                for k in range(KC):
                    part(name, l, c, j, j, k, token_major, cols)

            def gate_parts(name, l, c, first, done, n):
                for m in range(done, done + n):
                    part(name, l, c, first + m // KC, first + m // KC, m % KC)

            def norm_stats(name, l, number, n=SEQ):
                b = open_bank(name, l, 0, 0)
                for k in range(KC):
                    pe.wait_ge(squared, number * KC + (k + 1))
                    last = nc.tensor.matmul(dense[:, b, 0:n], ones[:], probs[:, k % 2, 0:n],
                                            start=(k == 0), stop=(k == KC - 1))
                    last.then_inc(square_used if k < KC - 1 else dense_done, 1)

            def down(name, l):
                with pe.Fori(0, 2) as c:
                    for j in range(4):
                        b = open_bank(name, l, c, j)
                        for k in range(FC):
                            w = j * FC + k
                            s, count = PLAN.landed(name, l, c, w // KC)
                            if k == 0 or w % KC == 0:
                                pe.wait_ge(landed[s], count)
                            last = nc.tensor.matmul(dense[:, b, :], ring[:, s, (w % KC) * P:(w % KC + 1) * P],
                                                    act_T[:, k, :], start=(k == 0), stop=(k == FC - 1))
                        last.then_inc(dense_done, 1)

            def pre(l):
                pe.wait_ge(h_ready, l * (2 * KC) + KC)
                for j in range(5):
                    product("pre", l, 0, j, token_major=(j == 0), cols=P if j else TOK_COLS)
                pe.wait_ge(f_log, l + 1)
                for h in range(HEADS):
                    if h >= 2:
                        pe.wait_ge(f_copied, l * HEADS + (h - 1))
                    for j in range(TB):
                        last = nc.tensor.matmul(
                            scores[:, h % 2, j * P:SEQ],
                            logf[:, 3, j * HEADS + h:j * HEADS + h + 1].broadcast_to((P, P)),
                            tri[:, 0:SEQ - j * P], start=(j == 0), stop=True, skip_group_check=True)
                    last.then_inc(f_bcast, 1)
                pe.wait_ge(rope_done, rope_no("pre", l, 0, 3) + OPEN)
                for i in range(1, TB):
                    for h in range(IDX_HEADS):
                        u = (i - 1) * IDX_HEADS + h
                        if u < 2:
                            pe.wait_ge(f_copied, (l + 1) * HEADS)
                        else:
                            pe.wait_ge(relu_ready, l * DOTS + (u - 1))
                        half = slice(HEAD_DIM * (h % 2), HEAD_DIM * (h % 2 + 1))
                        n = (i + 1) * P
                        nc.tensor.matmul(scores[:, u % 2, 0:n], qI[half, h // 2, i * P:(i + 1) * P],
                                         kI[half, 0:n], start=True, stop=True).then_inc(dots_ready, 1)

            def attention(name, l, c):
                T = pe.snap(att_turn(name, l, c))
                first_gate = 3 if name == "A" else 1
                keys = {"A": kT, "B": kB, "D": kI}[name]
                values = {"A": vt, "B": tok, "D": qI[:, 0, :].rearrange("p (t n) -> p t n", t=TB)}[name]
                if name == "A":
                    for j in range(3):
                        product("A", l, c, j, token_major=(j == 2))
                    evac_wait("A", l, c, 0)
                    evac_wait("A", l, c, 1)
                    pe.wait_ge(relu_ready, (l + 1) * DOTS)
                else:
                    product(name, l, c, 0)
                    pe.wait_ge(rope_done, rope_no(name, l, c) + (OPEN + 1))

                done = 0
                for k in range(STEPS + PV_LAG):
                    if k < STEPS:
                        i, hh = divmod(k, 2)
                        half = slice(HEAD_DIM * hh, HEAD_DIM * (hh + 1))
                        k0, k1 = key_range(name, i)
                        n = k1 - k0
                        if k >= 2:
                            pe.wait_ge(probs_ready, T * STEPS + (k - 1))
                        last = nc.tensor.matmul(scores[:, k % 2, 0:n], qT[half, i * P:(i + 1) * P],
                                                   keys[half, k0:k1], start=True, stop=True)
                        if name != "B":
                            last = nc.tensor.matmul(scores[:, k % 2, n - P:n], ident, causal, start=False,
                                                       stop=True, skip_group_check=True)
                        if name == "D" and i:
                            last = nc.tensor.matmul(scores[:, k % 2, 0:P], ident, before, start=False,
                                                       stop=True, skip_group_check=True)
                        last.then_inc(scores_ready, 1)
                    if k < len(GATE_STEPS):
                        gate_parts(name, l, c, first_gate, done, GATE_STEPS[k])
                        done += GATE_STEPS[k]
                    s = k - TR_LAG
                    if 0 <= s < STEPS:
                        k0, k1 = key_range(name, s // 2)
                        pe.wait_ge(probs_ready, T * STEPS + (s + 1))
                        if s >= 2:
                            pe.wait_ge(turned_copied, T * STEPS + (s - 1))
                        for m in range((k1 - k0) // P):
                            last = nc.tensor.transpose(turned[:, s % 2, m * P:(m + 1) * P],
                                                       probs[:, s % 2, m * P:(m + 1) * P], ident)
                        last.then_inc(turned_ready, 1)
                    s = k - PV_LAG
                    if 0 <= s < STEPS:
                        i, hh = divmod(s, 2)
                        k0, k1 = key_range(name, i)
                        pe.wait_ge(turned_copied, T * STEPS + (s + 1))
                        if s == 0 and name == "A":
                            evac_wait("A", l, c, 2)
                        if s == 0 and name == "D":
                            evac_wait("Dkv", l, 0, 1)
                        v0 = {"A": HEAD_DIM * hh, "B": 0, "D": HEAD_DIM * hh}[name]
                        for m in range((k1 - k0) // P):
                            last = nc.tensor.matmul(
                                O[:, s * HEAD_DIM:(s + 1) * HEAD_DIM], probsT[:, s % 2, m * P:(m + 1) * P],
                                values[:, k0 // P + m, v0:v0 + HEAD_DIM], start=(m == 0),
                                stop=(m == (k1 - k0) // P - 1))
                        last.then_inc(pv_done, 1)
                gate_parts(name, l, c, first_gate, done, GATE_TAIL)
                pe.wait_ge(y_norm, T + 1)
                pe.wait_ge(y_stored, T + OPEN)
                pe.wait_ge(yc_stored, l * PAIRS + OPEN)
                for t in range(TB):
                    last = nc.tensor.transpose(Yt[:, t * P:(t + 1) * P], Y[:, t * P:(t + 1) * P], ident)
                last.then_inc(y_turned, 1)

            def retention(l, c):
                R = pe.snap(l * PAIRS + c)
                for j in range(4):
                    product("C", l, c, j, token_major=(j == 2))
                pe.wait_ge(rope_done, rope_no("C", l, c, 1) + (OPEN + 1))
                done = 0
                for k in range(STEPS + 1):
                    if k < STEPS:
                        hh, j = divmod(k, TB)
                        half = slice(HEAD_DIM * hh, HEAD_DIM * (hh + 1))
                        if k >= 2:
                            pe.wait_ge(st_decayed, R * STEPS + (k - 1))
                        nc.tensor.matmul(scores[:, k % 2, 0:SEQ - j * P], kT[half, j * P:(j + 1) * P],
                                         qT[half, j * P:SEQ], start=True, stop=True).then_inc(st_ready, 1)
                    gate_parts("C", l, c, 4, done, RET_GATES[k])
                    done += RET_GATES[k]
                    if k:
                        s = k - 1
                        hh, j = divmod(s, TB)
                        pe.wait_ge(st_decayed, R * STEPS + (s + 1))
                        if s == 0:
                            evac_wait("C", l, c, 2)
                        for i in range(j, TB):
                            at = (2 * i + hh) * HEAD_DIM
                            last = nc.tensor.matmul(
                                O[:, at:at + HEAD_DIM], probsT[:, s % 2, (i - j) * P:(i - j + 1) * P],
                                vt[:, j, HEAD_DIM * hh:HEAD_DIM * (hh + 1)], start=(s == 0 and i == 0),
                                stop=True, skip_group_check=True)
                        last.then_inc(rv_done, 1)
                gate_parts("C", l, c, 4, done, 2 * KC - done)
                pe.wait_ge(yc_norm, R + (OPEN + 1))
                pe.wait_ge(y_stored, (l + 1) * (3 * PAIRS) + OPEN)
                pe.wait_ge(yc_stored, R + OPEN)
                for t in range(TB):
                    last = nc.tensor.transpose(Yt[:, t * P:(t + 1) * P], Y[:, t * P:(t + 1) * P], ident)
                last.then_inc(yc_turned, 1)

            pe.wait_ge(s_init, INITS)
            pe.wait_ge(s_const, 16)
            with pe.Fori(0, DEPTH) as l:
                norm_stats("norm1", l, 2 * l)
                pre(l)
                with pe.Fori(0, PAIRS) as c:
                    attention("A", l, c)
                with pe.Fori(0, PAIRS) as c:
                    attention("B", l, c)
                for j in range(2):
                    product("Dkv", l, 0, j, token_major=(j == 1))
                with pe.Fori(0, PAIRS) as c:
                    attention("D", l, c)
                with pe.Fori(0, PAIRS) as c:
                    retention(l, c)
                pe.wait_ge(y_stored, (l + 1) * (3 * PAIRS) + OPEN)
                pe.wait_ge(yc_stored, (l + 1) * PAIRS + OPEN)
                settle(pe)
                with pe.Fori(0, KC) as d:
                    for n in range(N_BRANCH):
                        b = open_bank("merge", l, d, n)
                        s, count = PLAN.landed("merge", l, d, n // 2)
                        pe.wait_ge(landed[s], count)
                        for k in range(PAIRS):
                            w = (n % 2) * PAIRS + k
                            last = nc.tensor.matmul(dense[:, b, :], ring[:, s, w * P:(w + 1) * P],
                                                    yT[:, n * PAIRS + k, :], start=(k == 0), stop=(k == PAIRS - 1))
                        last.then_inc(dense_done, 1)
                pe.wait_ge(merge_add, (l + 1) * (KC * (N_BRANCH - 1)) + OPEN)
                settle(pe)
                with pe.Fori(0, KC // 2) as c:
                    for j in range(2):
                        product("out", l, c, j)
                norm_stats("norm2", l, 2 * l + 1)
                pe.wait_ge(h_ready, (l + 1) * (2 * KC))
                settle(pe)
                with pe.Fori(0, FC) as f:
                    for j in range(2):
                        product("up", l, f, j)
                pe.wait_ge(hidden_ready, (l + 1) * FC + OPEN)
                settle(pe)
                down("down", l)
            norm_stats("normf", DEPTH, N_F)

            L = DEPTH
            pe.wait_ge(cond_step, 3)
            pe.wait_ge(yc_stored, DEPTH * PAIRS + OPEN)
            with pe.Fori(0, 6) as c:
                for j in range(8):
                    s, count = PLAN.landed("ada", L, c, j)
                    pe.wait_ge(landed[s], count)
                    at = pe.snap((c * 8 + j) * 2)
                    for k in range(KC):
                        last = nc.tensor.matmul(Yt[:, bass.ds(at, 2)], ring[:, s, k * P:(k + 1) * P],
                                                cond[:, 2 * k:2 * k + 2], start=(k == 0), stop=(k == KC - 1))
                    last.then_inc(dense_done, 1)
            norm_stats("normL", L, N_L)
            norm_stats("normX", L, N_X, CTX)
            pe.wait_ge(h_ready, (N_X + 1) * KC)
            b = open_bank("ab", L, 0, 0)
            pe.wait_ge(landed[0], PLAN.landed("ab", L, 0, 0)[1])
            for t in range(XB):
                for k in range(KC):
                    last = nc.tensor.matmul(dense[:, b, t * 16:(t + 1) * 16], hx[:, k, t * P:(t + 1) * P],
                                            ring[:, 0, k * P:k * P + 16], start=(k == 0), stop=(k == KC - 1))
            last.then_inc(dense_done, 1)
            with pe.Fori(0, 12) as c:
                for j, (at, n) in enumerate(((0, SEQ), (SEQ, CTX))):
                    b = open_bank("qkv", L, c, j)
                    if j == 0:
                        pe.wait_ge(landed[0], PLAN.landed("qkv", L, c, 0)[1])
                    for k in range(KC):
                        last = nc.tensor.matmul(dense[:, b, 0:n], ring[:, 0, k * P:(k + 1) * P],
                                                hx[:, k, at:at + n], start=(k == 0), stop=(k == KC - 1))
                    last.then_inc(dense_done, 1)
            with pe.Fori(0, 4) as c:
                for j in range(2):
                    b = open_bank("uz", L, c, j)
                    pe.wait_ge(landed[j], PLAN.landed("uz", L, c, j)[1])
                    for k in range(KC):
                        last = nc.tensor.matmul(dense[:, b, :], ring[:, j, k * P:(k + 1) * P], hx[:, k, 0:SEQ],
                                                start=(k == 0), stop=(k == KC - 1))
                    last.then_inc(dense_done, 1)
            pe.wait_ge(ab_step, 7)
            sums = scores[:, 0, :]
            half_sc = XB * GH
            for d in range(2):
                nc.tensor.matmul(sums[:, d * half_sc:(d + 1) * half_sc], upto[:, d * P:(d + 1) * P],
                                 gg[:, d * half_sc:(d + 1) * half_sc], start=True, stop=True)
            nc.tensor.matmul(sums[:, SC:2 * SC], chunk_ones, gg[:], start=True, stop=True)
            for c in range(2):
                last = nc.tensor.matmul(sums[:, (2 + c) * SC:(3 + c) * SC],
                                        chunk_ones[:, c * (P - 1):c * (P - 1) + 1].broadcast_to((P, P)), gg[:],
                                        start=True, stop=True)
            last.then_inc(ab_sums, 1)
            for cc in range(8):
                pe.wait_ge(l2_squared, cc + 1)
                sq = (probs, probsT)[cc % 2][:].rearrange("p a n -> p (a n)")
                for t in range(XB):
                    last = nc.tensor.matmul(scores[:, 1, cc * XB + t:cc * XB + t + 1], sq[:, t * P:(t + 1) * P],
                                            ones[:, 0:1], start=True, stop=True)
                last.then_inc(l2_used if cc < 7 else l2_sums, 1)
            for r in range(2):
                b = open_bank("four", L, 0, r)
                pe.wait_ge(landed[0], PLAN.landed("four", L, 0, 0)[1])
                nc.tensor.matmul(dense[:, b, :], ring[:, 0, (GH + r) * P:(GH + r + 1) * P], ring[:, 0, 0:SEQ],
                                 start=True, stop=True).then_inc(dense_done, 1)
            evac_wait("uz", L, 3, 0)
            for g in range(4):
                for m in range(2):
                    r = 2 + 3 * g + m
                    b = open_bank("four", L, 0, r)
                    if g == 0:
                        evac_wait("four", L, 0, m)
                    for t in range(TB):
                        last = nc.tensor.matmul(dense[:, b, t * P:(t + 1) * P], uT[:, g, t * P:(t + 1) * P],
                                                (wc, ws)[m][:, g * P:(g + 1) * P], start=True, stop=True)
                    last.then_inc(dense_done, 1)
                b = open_bank("four", L, 0, 4 + 3 * g)
                for m in range(2):
                    evac_wait("four", L, 0, 2 + 3 * g + m)
                    for t in range(TB):
                        s = 1 + 2 * m + t // 2
                        pe.wait_ge(landed[s], PLAN.landed("four", L, 0, s)[1])
                        last = nc.tensor.matmul(dense[:, b, :], (p1, p2)[m][:, t * P:(t + 1) * P],
                                                ring[:, s, (t % 2) * SEQ:(t % 2 + 1) * SEQ],
                                                start=(m == 0 and t == 0), stop=(m == 1 and t == TB - 1))
                last.then_inc(dense_done, 1)
            pe.wait_ge(l2_var, 1)
            pe.wait_ge(ab_act, 6)
            pe.wait_ge(ab_step, 10)
            pe.wait_ge(mod_step, 1)
            for t in range(XB):
                if t >= 2:
                    pe.wait_ge(v_stored, t - 1)
                for h in range(GH):
                    last = nc.tensor.transpose(bankB[t % 2][:, h * P:(h + 1) * P], cv[:, 8 + h, t * P:(t + 1) * P],
                                               ident)
                last.then_inc(v_turned, 1)
            for t in range(XB + 1):
                if t < XB:
                    if t >= 2:
                        pe.wait_ge(k_scaled, t - 1)
                    for h in range(GH):
                        last = nc.tensor.transpose(bankA[t % 2][:, h * P:(h + 1) * P],
                                                   cv[:, 4 + h, t * P:(t + 1) * P], ident)
                    last.then_inc(k_turned, 1)
                if t >= 1:
                    pe.wait_ge(k_scaled, t)
                    if t >= 3:
                        pe.wait_ge(kh_stored, t - 2)
                    for h in range(GH):
                        last = nc.tensor.transpose(bankC[(t - 1) % 2][:, h * P:(h + 1) * P],
                                                   ktok[:, t - 1, h * P:(h + 1) * P], ident)
                    last.then_inc(kh_turned, 1)
            pe.wait_ge(kh_stored, XB)
            pe.wait_ge(v_stored, XB)

            def unit(n):
                isl = n >= FIRST_L
                both = [(d, ORDER[d][n]) for d in range(2)]
                hcol = [slice(h * P, (h + 1) * P) for h in range(GH)]
                for d, b in both:
                    if n:
                        pe.wait_ge(c_s[d], 2 * n)
                    for h in range(GH):
                        at = (d * XB + b) * GH + h
                        last = nc.tensor.matmul(bankA[d][:, hcol[h]], gg[:, at:at + 1].broadcast_to((P, P)),
                                                upto[:, d * P:(d + 1) * P], start=True, stop=True)
                    last.then_inc(u_row[d], 1)
                for d, b in both:
                    if n > FIRST_L:
                        pe.wait_ge(c_o2[d], seen(n))
                    for h in range(GH):
                        last = nc.tensor.matmul(bankB[d][:, hcol[h]], cv[:, 4 + h, b * P:(b + 1) * P],
                                                khT[:, b, hcol[h]], start=True, stop=True)
                    last.then_inc(u_kk[d], 1)
                if isl:
                    for d, b in both:
                        if n > FIRST_L:
                            pe.wait_ge(c_o1[d], seen(n))
                        for h in range(GH):
                            last = nc.tensor.matmul(bankC[d][:, hcol[h]], cv[:, h, b * P:(b + 1) * P],
                                                    khT[:, b, hcol[h]], start=True, stop=True)
                        last.then_inc(u_qk[d], 1)
                    for d, b in both:
                        pe.wait_ge(u_x[d], n - FIRST_L + 1)
                        for h in range(GH):
                            last = nc.tensor.transpose(bankC[d][:, hcol[h]], W2["X"][d][:, hcol[h]], ident)
                        last.then_inc(u_xt[d], 1)
                for d, b in both:
                    pe.wait_ge(u_t[d], n + 1)
                    for h in range(GH):
                        last = nc.tensor.transpose(bankB[d][:, hcol[h]], W2["T"][d][:, hcol[h]], ident)
                    last.then_inc(u_tt[d], 1)
                for lev in range(1, LEVELS):
                    step = n * (LEVELS - 1) + lev
                    for d, b in both:
                        pe.wait_ge(u_as[d], step)
                        if lev == 1:
                            pe.wait_ge(u_ttc[d], n + 1)
                        else:
                            pe.wait_ge(u_lvl[d], step - 1)
                        for h in range(GH):
                            last = nc.tensor.matmul(bankB[d][:, hcol[h]], W2["A_level"][d][:, hcol[h]],
                                                    W2["TT"][d][:, hcol[h]], start=True, stop=True)
                        last.then_inc(u_z[d], 1)
                    for d, b in both:
                        pe.wait_ge(u_zc[d], step)
                        if lev == 1 and isl:
                            pe.wait_ge(u_attn[d], n - FIRST_L + 1)
                        for h in range(GH):
                            if lev < LEVELS - 1:
                                nc.tensor.matmul(bankA[d][:, hcol[h]], W2["Z"][d][:, hcol[h]],
                                                 W2["T"][d][:, hcol[h]], start=True, stop=True)
                            last = nc.tensor.matmul(bankC[d][:, hcol[h]], W2["T"][d][:, hcol[h]],
                                                    W2["Z"][d][:, hcol[h]], start=True, stop=True)
                        last.then_inc(u_upd[d], 1)
                for d, b in both:
                    pe.wait_ge(u_lvl[d], (n + 1) * (LEVELS - 1))
                    pe.wait_ge(u_kv[d], 3 * n + 3)
                    for h in range(GH):
                        nc.tensor.matmul(bankA[d][:, hcol[h]], W2["decay"][d][:, hcol[h]], W2["TT"][d][:, hcol[h]],
                                         start=True, stop=True)
                        last = nc.tensor.matmul(bankC[d][:, hcol[h]], W2["TT"][d][:, hcol[h]],
                                                W2["X"][d][:, hcol[h]], start=True, stop=True)
                    last.then_inc(u_wu[d], 1)

            def scan(n):
                isl = n >= FIRST_L
                for i in range(2):
                    for d in range(2):
                        b = ORDER[d][n]
                        c, hs = chunk_of(d, i)
                        if i == 0:
                            pe.wait_ge(u_w[d], n + 1)
                            pe.wait_ge(u_u[d], n + 1)
                        if n or i:
                            pe.wait_ge(c_s[d], 2 * n + i)
                        else:
                            pe.wait_ge(ab_step, 14)
                        if isl and i:
                            pe.wait_ge(c_o2[d], seen(n, 0))
                        for h in range(GH):
                            hc = slice(h * P, (h + 1) * P)
                            last = nc.tensor.matmul(bankB[d][hs, hc], W2["wT"][d][:, h * P + CHUNK * c:h * P + CHUNK * (c + 1)],
                                                    state[d][:, hc], start=True, stop=True)
                            if isl:
                                last = nc.tensor.matmul(bankC[d][hs, hc], cv[:, h, b * P + CHUNK * c:b * P + CHUNK * (c + 1)],
                                                        state[d][:, hc], start=True, stop=True)
                        last.then_inc(c_ws[d], 1)
                    for d in range(2):
                        c, hs = chunk_of(d, i)
                        pe.wait_ge(c_v[d], 2 * n + i + 1)
                        for h in range(GH):
                            hc = slice(h * P, (h + 1) * P)
                            last = nc.tensor.matmul(bankA[d][:, hc], W2["kd"][d][hs, hc], W2["vnew"][d][hs, hc],
                                                    start=True, stop=True)
                        last.then_inc(c_sd[d], 1)
                        if isl:
                            for h in range(GH):
                                hc = slice(h * P, (h + 1) * P)
                                last = nc.tensor.matmul(
                                    bankB[d][hs, hc], W2["attnT"][d][hs, h * P + CHUNK * c:h * P + CHUNK * (c + 1)],
                                    W2["vnew"][d][hs, hc], start=True, stop=True)
                            last.then_inc(c_oi[d], 1)

            for n in range(UNITS):
                unit(n)
                scan(n)
            for t in range(TB):
                pe.wait_ge(p_on, t + 1)
                for h in range(GH):
                    last = nc.tensor.transpose((bankA + bankB)[t][:, h * P:(h + 1) * P], o2[t][:, h * P:(h + 1) * P],
                                               ident)
                last.then_inc(p_turned, 1)
            pe.wait_ge(p_y, TB)
            evac_wait("four", L, 0, 13)
            settle(pe)
            with pe.Fori(0, KC // 2) as c:
                for j in range(2):
                    b = open_bank("out2", L, c, j)
                    pe.wait_ge(landed[j], PLAN.landed("out2", L, c, j)[1])
                    for k in range(KC):
                        last = nc.tensor.matmul(dense[:, b, :], ring[:, j, k * P:(k + 1) * P], yT[:, k, :],
                                                start=(k == 0), stop=(k == KC - 1))
                    last.then_inc(dense_done, 1)
            norm_stats("norm3", L, N_3)
            norm_stats("norm4", L, N_4)
            pe.wait_ge(h_ready, (N_4 + 1) * KC)
            with pe.Fori(0, FC) as f:
                for j in range(2):
                    product("up2", L, f, j)
            pe.wait_ge(hidden_ready, (DEPTH + 1) * FC + OPEN)
            down("down2", L)
            norm_stats("norm5", L, N_5)

        @block.scalar
        def _(act):
            def result_in(name, l, c, j):
                act.wait_ge(dense_done, PLAN.done(name, l, c, j))
                b, held = PLAN.bank(name, l, c, j)
                return b, held

            def norm(name, l, number, src=xT, n=SEQ):
                for b in range(BANKS):
                    act.wait_ge(evacuated[b], held_before(name, l, b))
                for k in range(KC):
                    if k >= 2:
                        act.wait_ge(square_used, number * (KC - 1) + (k - 1))
                    nc.scalar.activation(probs[:, k % 2, 0:n], src[:, k, 0:n], ACT.Square).then_inc(squared, 1)
                act.wait_ge(evacuated[0], held_before(name, l, 0) + 1)
                nc.scalar.activation(gC[:, 0:n], Y[:, 0:n], ACT.Sqrt).then_inc(norm_root, 1)

            def swap(name, l, c, j, r):
                b, _ = result_in(name, l, c, j)
                act.wait_ge(swap_mul, r + OPEN)
                for q in range(4):
                    last = nc.scalar.activation(swapped[32 * q:32 * q + 32, :],
                                                dense[32 * (q ^ 1):32 * (q ^ 1) + 32, b, :], ACT.Copy)
                last.then_inc(swap_ready, 1)

            def copy(name, l, c, j, dst, scale=1.0, cols=P, blocks=TB):
                b, _ = result_in(name, l, c, j)
                src = dense[:, b, :]
                if name == "ab":
                    src = dense[:, b, 0:blocks * cols].rearrange("p (t n) -> p t n", t=blocks)
                elif cols < P:
                    src = src.rearrange("p (t n) -> p t n", t=TB)[:, :, 0:cols]
                nc.scalar.activation(dst, src, ACT.Copy, scale=scale).then_inc(evacuated[b], 1)

            def gate(name, l, c, j, g):
                at = act.snap(gate_index(name, c) + g)
                b, _ = result_in(name, l, c, j)
                settle(act)
                nc.scalar.activation(gates[:, bass.ds(at, 1), :], dense[:, b:b + 1, :], ACT.Tanh,
                                     scale=0.5).then_inc(evacuated[b], 1)

            def pre(l):
                copy("pre", l, 0, 0, tok[:, :, 0:TOK_COLS], cols=TOK_COLS)
                swap("pre", l, 0, 1, rope_no("pre", l, 0, 0))
                act.wait_ge(f_abs, l + 1)
                nc.scalar.activation(logf[:, 2, :], logf[:, 1, :], ACT.Exp, scale=-1.0).then_inc(f_exp, 1)
                act.wait_ge(f_exp, l + 1)
                nc.scalar.activation(logf[:, 2, :], logf[:, 2, :], ACT.Ln, bias=1.0).then_inc(f_ln, 1)
                for j in range(2, 5):
                    swap("pre", l, 0, j, rope_no("pre", l, 0, j - 1))
                for h in range(HEADS):
                    act.wait_ge(f_bcast, l * HEADS + (h + 1))
                    nc.scalar.activation(negF[:, NEGF + h, :], scores[:, h % 2, :], ACT.Copy,
                                         scale=-1.0).then_inc(f_copied, 1)
                for i in range(1, TB):
                    for h in range(IDX_HEADS):
                        u = (i - 1) * IDX_HEADS + h
                        n = (i + 1) * P
                        act.wait_ge(dots_ready, l * DOTS + (u + 1))
                        if u >= 2:
                            act.wait_ge(score_step, l * DOTS + (u - 1))
                        nc.scalar.activation(probs[:, u % 2, 0:n], scores[:, u % 2, 0:n], ACT.Relu,
                                             scale=IDX_SCALE).then_inc(relu_ready, 1)

            def attention(name, l, c):
                T = act.snap(att_turn(name, l, c))
                if name == "A":
                    copy("A", l, c, 0, qT[:], scale=QK_SCALE)
                    copy("A", l, c, 1, kT[:])
                    copy("A", l, c, 2, vt[:].rearrange("p t n -> p (t n)"))
                else:
                    swap(name, l, c, 0, rope_no(name, l, c))
                first_gate = 3 if name == "A" else 1
                for k in range(STEPS + TR_LAG):
                    if k < STEPS:
                        k0, k1 = key_range(name, k // 2)
                        n = k1 - k0
                        act.wait_ge(negmax_ready, T * STEPS + (k + 1))
                        src = probs[:, k % 2, 0:n]
                        if name == "D":
                            h = act.snap(l * HEADS + c + (k % 2) * PAIRS)
                            settle(act)
                            nc.scalar.activation(sink_exp[:, k:k + 1], small[:, bass.ds(h + SMALL["sinks"], 1)],
                                                 ACT.Exp, bias=neg_max[:, k:k + 1])
                            src = scores[:, k % 2, 0:n]
                        nc.scalar.activation(probs[:, k % 2, 0:n], src, ACT.Exp, bias=neg_max[:, k:k + 1],
                                             scale=softmax_scores(name),
                                             accum_out=row_sum[:, k:k + 1]).then_inc(probs_ready, 1)
                    s = k - TR_LAG
                    if s >= 0:
                        k0, k1 = key_range(name, s // 2)
                        act.wait_ge(turned_ready, T * STEPS + (s + 1))
                        if s >= 2:
                            act.wait_ge(pv_done, T * STEPS + (s - 1))
                        nc.scalar.activation(probsT[:, s % 2, 0:k1 - k0], turned[:, s % 2, 0:k1 - k0],
                                             ACT.Copy).then_inc(turned_copied, 1)
                    if k == GATE0_AT:
                        gate(name, l, c, first_gate, 0)
                gate(name, l, c, first_gate + 1, 1)
                at = act.snap(PAIRS * BRANCH[name] + c)
                act.wait_ge(y_turned, T + 1)
                settle(act)
                nc.scalar.activation(yT[:, bass.ds(at, 1), :], Yt[:].rearrange("p (a n) -> p a n", a=1),
                                     ACT.Copy).then_inc(y_stored, 1)

            def retention(l, c):
                R = act.snap(l * PAIRS + c)
                swap("C", l, c, 0, rope_no("C", l, c, 0))
                swap("C", l, c, 1, rope_no("C", l, c, 1))
                copy("C", l, c, 2, vt[:].rearrange("p t n -> p (t n)"))
                b, _ = result_in("C", l, c, 3)
                act.wait_ge(yc_stored, R + OPEN)
                nc.scalar.activation(gC[:], dense[:, b, :], ACT.Tanh, scale=0.5).then_inc(gc_tanh, 1)
                for g in range(2):
                    gate("C", l, c, 4 + g, g)

            act.wait_ge(s_x, 16)
            act.wait_ge(s_small, 16)
            nc.scalar.activation(cond_tanh[:], small[:, SMALL["cond"]:SMALL["cond"] + 2 * KC], ACT.Tanh, scale=0.5
                                 ).then_inc(cond_step, 1)
            with act.Fori(0, DEPTH) as l:
                norm("norm1", l, 2 * l)
                pre(l)
                with act.Fori(0, PAIRS) as c:
                    attention("A", l, c)
                with act.Fori(0, PAIRS) as c:
                    attention("B", l, c)
                swap("Dkv", l, 0, 0, rope_no("Dkv", l, 0))
                copy("Dkv", l, 0, 1, qI[:, 0, :])
                with act.Fori(0, PAIRS) as c:
                    attention("D", l, c)
                with act.Fori(0, PAIRS) as c:
                    retention(l, c)
                norm("norm2", l, 2 * l + 1)
                with act.Fori(0, FC) as f:
                    F = act.snap(l * FC + f)
                    act.wait_ge(up_gate, F + OPEN)
                    act.wait_ge(hidden_ready, F + OPEN)
                    for j in range(2):
                        b, _ = result_in("up", l, f, j)
                        at = act.snap((l * (2 * FC) + f + j * FC) * 4 + SMALL["conv"])
                        settle(act)
                        nc.scalar.activation(probs[:, j, :], dense[:, b, :], ACT.Identity,
                                             scale=small[:, bass.ds(at + 2, 1)],
                                             bias=small[:, bass.ds(at + 3, 1)]).then_inc(taps, 1)
                    _, held = PLAN.bank("up", l, f, 0)
                    act.wait_ge(evacuated[0], held + 1)
                    nc.scalar.activation(probsT[:, 0, :], probs[:, 0, :], ACT.Tanh, scale=0.5).then_inc(up_tanh, 1)
            norm("normf", DEPTH, N_F)

            L = DEPTH
            act.wait_ge(h_ready, (N_F + 1) * KC)
            norm("normL", L, N_L)
            act.wait_ge(s_ctx, 16)
            norm("normX", L, N_X, xc, CTX)
            copy("ab", L, 0, 0, abt[:].rearrange("p (t n) -> p t n", t=XB), cols=16, blocks=XB)
            with act.Fori(0, 12) as c:
                act.wait_ge(cq_done, c + OPEN)
                at = act.snap(c * 3 + SMALL["qkv_conv"])
                for j, (lo, n) in enumerate(((0, SEQ), (SEQ, CTX))):
                    b, _ = result_in("qkv", L, c, j)
                    settle(act)
                    nc.scalar.activation(cv[:, bass.ds(c, 1), lo:lo + n], dense[:, b:b + 1, 0:n], ACT.Identity,
                                         scale=small[:, bass.ds(at + 1, 1)]).then_inc(cq_taps, 1)
                for j in range(2):
                    act.wait_ge(evacuated[j], PLAN.bank("qkv", L, c, j)[1] + 1)
                settle(act)
                nc.scalar.activation(probsT[:].rearrange("p a n -> p (a n)")[:, 0:XB * P].rearrange("p (a n) -> p a n", a=1),
                                     cv[:, bass.ds(c, 1), :], ACT.Tanh, scale=0.5).then_inc(cq_tanh, 1)
            with act.Fori(0, 4) as c:
                b, _ = result_in("uz", L, c, 0)
                settle(act)
                nc.scalar.activation(yT[:, bass.ds(c, 1), :], dense[:, b:b + 1, :], ACT.Copy).then_inc(evacuated[b], 1)
                act.wait_ge(z_done, c + OPEN)
                b, _ = result_in("uz", L, c, 1)
                nc.scalar.activation(gC[:], dense[:, b, :], ACT.Tanh, scale=0.5).then_inc(z_tanh, 1)
            act.wait_ge(ab_step, 3)
            nc.scalar.activation(tmp_sc[:, SC:2 * SC], tmp_sc[:, 0:SC], ACT.Exp, scale=-1.0).then_inc(ab_act, 1)
            act.wait_ge(ab_act, 1)
            nc.scalar.activation(tmp_sc[:, SC:2 * SC], tmp_sc[:, SC:2 * SC], ACT.Ln, bias=1.0).then_inc(ab_act, 1)
            nc.scalar.activation(decay_rate[:], small[:, SMALL["a_log"]:SMALL["a_log"] + 2 * GH], ACT.Exp
                                 ).then_inc(ab_act, 1)
            ab = abt[:].rearrange("p (t g h) -> p t g h", t=XB, h=GH)
            for d in range(2):
                nc.scalar.activation(sc3(beta, d), ab[:, :, d, :], ACT.Tanh, scale=0.5).then_inc(ab_act, 1)
            act.wait_ge(ab_sums, 1)
            nc.scalar.activation(gcum[:], scores[:, 0, 0:SC], ACT.Copy)
            nc.scalar.activation(egc[:], scores[:, 0, 0:SC], ACT.Exp)
            nc.scalar.activation(etot[:], scores[:, 0, 2 * SC:4 * SC], ACT.Exp).then_inc(ab_act, 1)
            act.wait_ge(ab_step, 10)
            nc.scalar.activation(ed[:], tmp_sc[:, 0:SC], ACT.Exp).then_inc(ab_act, 1)
            for cc in range(8):
                if cc >= 2:
                    act.wait_ge(l2_used, cc - 1)
                sq = (probs, probsT)[cc % 2][:].rearrange("p a n -> p (a n)")
                nc.scalar.activation(sq[:, 0:XB * P], cv[:, cc, :], ACT.Square).then_inc(l2_squared, 1)
            for r in range(2):
                b, _ = result_in("four", L, 0, r)
                nc.scalar.activation((wc, ws)[r], dense[:, b, :], ACT.Copy, scale=FFT_SCALE).then_inc(evacuated[b], 1)
            for g in range(4):
                copy("four", L, 0, 2 + 3 * g, p1)
                copy("four", L, 0, 3 + 3 * g, p2)
                copy("four", L, 0, 4 + 3 * g, yT[:, g, :])
            for t in range(XB):
                act.wait_ge(v_turned, t + 1)
                nc.scalar.activation(vtok[:, t, :], bankB[t % 2], ACT.Copy).then_inc(v_stored, 1)
            for t in range(XB):
                act.wait_ge(kh_turned, t + 1)
                nc.scalar.activation(khT[:, t, :], bankC[t % 2], ACT.Copy).then_inc(kh_stored, 1)
            for n in range(UNITS):
                isl = n >= FIRST_L
                for d in range(2):
                    act.wait_ge(u_diff[d], n + 1)
                    nc.scalar.activation(W2["decay"][d], W2["decay"][d], ACT.Exp, scale=-1.0).then_inc(u_decay[d], 1)
                if isl:
                    for d in range(2):
                        act.wait_ge(u_xt[d], n - FIRST_L + 1)
                        nc.scalar.activation(W2["attnT"][d], bankC[d], ACT.Copy).then_inc(u_attn[d], 1)
                for d in range(2):
                    act.wait_ge(u_tt[d], n + 1)
                    nc.scalar.activation(W2["TT"][d], bankB[d], ACT.Copy).then_inc(u_ttc[d], 1)
                for lev in range(1, LEVELS):
                    for d in range(2):
                        act.wait_ge(u_z[d], n * (LEVELS - 1) + lev)
                        nc.scalar.activation(W2["Z"][d], bankB[d], ACT.Copy).then_inc(u_zc[d], 1)
                for d in range(2):
                    act.wait_ge(u_wu[d], n + 1)
                    nc.scalar.activation(W2["wT"][d], bankA[d], ACT.Copy).then_inc(u_w[d], 1)
            for t in range(TB):
                d = int(t < 2)
                act.wait_ge(c_o3[d], 4)
                nc.scalar.activation(SQ4[t], o2[t], ACT.Square).then_inc(p_sq, 1)
            with act.Fori(0, KC // 2) as c:
                for j in range(2):
                    at = act.snap(c * 2 + j)
                    b, _ = result_in("out2", L, c, j)
                    settle(act)
                    nc.scalar.activation(hT[:, bass.ds(at, 1), :], dense[:, b:b + 1, :], ACT.Copy
                                         ).then_inc(evacuated[b], 1)
            norm("norm3", L, N_3, hT)
            act.wait_ge(x_added, KC)
            norm("norm4", L, N_4)
            with act.Fori(0, FC) as f:
                act.wait_ge(up_gate, f + (DEPTH * FC + OPEN))
                act.wait_ge(hidden_ready, f + (DEPTH * FC + OPEN))
                b, _ = result_in("up2", L, f, 0)
                nc.scalar.activation(probs[:, 0, :], dense[:, b, :], ACT.Copy).then_inc(evacuated[b], 1)
                at = act.snap(f * 9 + SMALL["dwc"])
                b, _ = result_in("up2", L, f, 1)
                settle(act)
                nc.scalar.activation(probs[:, 1, :], dense[:, b, :], ACT.Identity,
                                     scale=small[:, bass.ds(at + 4, 1)]).then_inc(taps, 1)
                act.wait_ge(evacuated[1], PLAN.bank("up2", L, f, 1)[1] + 1)
                nc.scalar.activation(probsT[:, 0, :], probs[:, 1, :], ACT.Tanh, scale=0.5).then_inc(up_tanh, 1)
            with act.Fori(0, 2) as c:
                for j in range(4):
                    at = act.snap(c * 4 + j)
                    b, _ = result_in("down2", L, c, j)
                    settle(act)
                    nc.scalar.activation(hT[:, bass.ds(at, 1), :], dense[:, b:b + 1, :], ACT.Copy, scale=0.5
                                         ).then_inc(evacuated[b], 1)
            norm("norm5", L, N_5, hT)

        @block.vector
        def _(dve):
            def result_in(name, l, c, j):
                dve.wait_ge(dense_done, PLAN.done(name, l, c, j))
                return PLAN.bank(name, l, c, j)

            def norm(name, l, number, gain, dst, src=xT, n=SEQ, sem=h_ready):
                b, held = result_in(name, l, 0, 0)
                nc.vector.tensor_scalar(Y[:, 0:n], dense[:, b, 0:n], 1.0 / D_MODEL, EPS, ALU.mult, ALU.add
                                        ).then_inc(evacuated[b], 1)
                dve.wait_ge(norm_root, number + 1)
                nc.vector.reciprocal(Y[:, 0:n], gC[:, 0:n]).then_inc(norm_inv, 1)
                dve.wait_ge(norm_inv, number + 1)
                for k in range(KC):
                    nc.vector.scalar_tensor_tensor(out=dst[:, k, 0:n], in0=src[:, k, 0:n], scalar=gain(k),
                                                   in1=Y[:, 0:n], op0=ALU.mult, op1=ALU.mult).then_inc(sem, 1)

            def rope(name, l, c, j, r, dst):
                b, held = result_in(name, l, c, j)
                dve.wait_ge(swap_ready, r + 1)
                nc.vector.tensor_tensor(dst, dense[:, b, :], cos, ALU.mult).then_inc(evacuated[b], 1)
                dve.wait_ge(evacuated[b], held + 1)
                dve.wait_ge(swap_mul, r + (OPEN + 1))
                nc.vector.tensor_tensor(dst, dst, swapped_sin[:], ALU.add).then_inc(rope_done, 1)

            def pre(l):
                b, held = PLAN.bank("pre", l, 0, 0)
                dve.wait_ge(evacuated[b], held + 1)
                z = logf[:, 0, :].rearrange("p (t h) -> p t h", t=TB)
                at = dve.snap(l * HEADS + SMALL["forget_bias"])
                bias = small[:, bass.ds(at, HEADS)].unsqueeze(1).broadcast_to((P, TB, HEADS))
                nc.vector.tensor_tensor(z, tok[:, :, HEAD_DIM:HEAD_DIM + HEADS], bias, ALU.add).then_inc(f_sum, 1)
                dve.wait_ge(f_sum, l + 1)
                nc.vector.scalar_tensor_tensor(out=logf[:, 1, :], in0=logf[:, 0, :], scalar=-1.0,
                                               in1=logf[:, 0, :], op0=ALU.mult, op1=ALU.max).then_inc(f_abs, 1)
                rope("pre", l, 0, 1, rope_no("pre", l, 0, 0), kI[:])
                dve.wait_ge(f_ln, l + 1)
                nc.vector.scalar_tensor_tensor(out=logf[:, 3, :], in0=logf[:, 0, :], scalar=0.0,
                                               in1=logf[:, 2, :], op0=ALU.min, op1=ALU.subtract).then_inc(f_log, 1)
                rope("pre", l, 0, 2, rope_no("pre", l, 0, 1), qI[:, 0, :])
                rope("pre", l, 0, 3, rope_no("pre", l, 0, 2), qI[:, 1, :])
                rope("pre", l, 0, 4, rope_no("pre", l, 0, 3), kB[:])
                for i in range(1, TB):
                    for h in range(IDX_HEADS):
                        u = (i - 1) * IDX_HEADS + h
                        n = (i + 1) * P
                        dst = sel[:, SEL + i, 0:n]
                        w = tok[:, i, HEAD_DIM + HEADS + h:HEAD_DIM + HEADS + h + 1]
                        dve.wait_ge(relu_ready, l * DOTS + (u + 1))
                        if h == 0:
                            nc.vector.tensor_scalar(dst, probs[:, u % 2, 0:n], w, None, ALU.mult
                                                    ).then_inc(score_step, 1)
                        else:
                            dve.wait_ge(score_step, l * DOTS + u)
                            nc.vector.scalar_tensor_tensor(out=dst, in0=probs[:, u % 2, 0:n], scalar=w, in1=dst,
                                                           op0=ALU.mult, op1=ALU.add).then_inc(score_step, 1)
                step = 0
                base = dve.snap(l * TOPK_STEPS)
                dve.wait_ge(score_step, (l + 1) * DOTS)
                nc.vector.tensor_copy(sel[:, SEL, 0:P], causal).then_inc(topk_step, 1)
                step += 1
                for i in range(1, TB):
                    diag = sel[:, SEL + i, i * P:(i + 1) * P]
                    nc.vector.tensor_tensor(diag, diag, causal, ALU.add).then_inc(topk_step, 1)
                    step += 1
                for _ in range(TOPK_ROUNDS):
                    for i in range(1, TB):
                        dve.wait_ge(topk_step, base + (step - (TB - 2)))
                        settle(dve)
                        nc.vector.max(top8[:, i, :], sel[:, SEL + i, 0:(i + 1) * P]).then_inc(topk_step, 1)
                        step += 1
                    for i in range(1, TB):
                        work = sel[:, SEL + i, 0:(i + 1) * P]
                        dve.wait_ge(topk_step, base + (step - (TB - 2)))
                        settle(dve)
                        nc.vector.match_replace(out=work, in_to_replace=top8[:, i, :], in_values=work,
                                                imm_value=TAKEN).then_inc(topk_step, 1)
                        step += 1
                for i in range(1, TB):
                    work = sel[:, SEL + i, 0:(i + 1) * P]
                    dve.wait_ge(topk_step, base + (step - (TB - 2)))
                    nc.vector.tensor_scalar(work, work, TAKEN / 2, NEG, ALU.is_gt, ALU.mult
                                            ).then_inc(topk_step, 1)
                    step += 1
                assert step == TOPK_STEPS
                dve.wait_ge(topk_step, (l + 1) * TOPK_STEPS)
                dve.wait_ge(f_copied, (l + 1) * HEADS)
                settle(dve)

            def attention(name, l, c):
                T = dve.snap(att_turn(name, l, c))
                if name != "A":
                    rope(name, l, c, 0, rope_no(name, l, c), qT[:])
                for s in range(STEPS):
                    i, hh = divmod(s, 2)
                    k0, k1 = key_range(name, i)
                    n = k1 - k0
                    dve.wait_ge(scores_ready, T * STEPS + (s + 1))
                    if s >= 2:
                        dve.wait_ge(turned_ready, T * STEPS + (s - 1))
                    mx = row_max[:, s:s + 1]
                    if name == "D":
                        nc.vector.tensor_reduce(mx, scores[:, s % 2, 0:n], AX_X, ALU.max).then_inc(logits_ready, 1)
                    elif name == "B":
                        settle(dve)
                        nc.vector.tensor_tensor_reduce(
                            probs[:, s % 2, 0:n], scores[:, s % 2, 0:n], sel[:, SEL + i, 0:n], QK_SCALE, TAKEN,
                            ALU.add, ALU.max, mx).then_inc(logits_ready, 1)
                    else:
                        at = dve.snap(c * 2 + (NEGF + hh))
                        nc.vector.tensor_tensor(probs[:, s % 2:s % 2 + 1, 0:n], scores[:, s % 2:s % 2 + 1, 0:n],
                                                negF[:, bass.ds(at, 1), 0:n], ALU.add).then_inc(biased, 1)
                        dve.wait_ge(biased, (l * PAIRS + c) * STEPS + (s + 1))
                        nc.vector.tensor_reduce(mx, probs[:, s % 2, 0:n], AX_X, ALU.max).then_inc(logits_ready, 1)
                    dve.wait_ge(logits_ready, T * STEPS + (s + 1))
                    if name == "D":
                        h = dve.snap(l * HEADS + c + hh * PAIRS)
                        nc.vector.tensor_scalar(neg_max[:, s:s + 1], mx, -QK_SCALE, neg_sink[:, bass.ds(h, 1)],
                                                ALU.mult, ALU.min).then_inc(negmax_ready, 1)
                    else:
                        nc.vector.tensor_scalar(neg_max[:, s:s + 1], mx, -1.0, None, ALU.mult
                                                ).then_inc(negmax_ready, 1)
                dve.wait_ge(pv_done, T * STEPS + STEPS)
                if name == "D":
                    nc.vector.tensor_tensor(row_sum[:], row_sum[:], sink_exp[:], ALU.add).then_inc(y_sum, 1)
                    dve.wait_ge(y_sum, l * PAIRS + c + 1)
                nc.vector.reciprocal(inv_sum[:], row_sum[:]).then_inc(y_inv, 1)
                dve.wait_ge(y_inv, T + 1)
                nc.vector.tensor_tensor(by_head(Y), by_head(O), bcast(inv_sum), ALU.mult).then_inc(y_norm, 1)

            def by_head(t):
                return t[:].rearrange("p (s e) -> p s e", e=HEAD_DIM)

            def bcast(t):
                return t[:].unsqueeze(2).broadcast_to((P, STEPS, HEAD_DIM))

            def retention(l, c):
                R = dve.snap(l * PAIRS + c)
                rope("C", l, c, 0, rope_no("C", l, c, 0), qT[:])
                rope("C", l, c, 1, rope_no("C", l, c, 1), kT[:])
                b, held = result_in("C", l, c, 3)
                dve.wait_ge(gc_tanh, R + 1)
                nc.vector.scalar_tensor_tensor(out=gC[:], in0=gC[:], scalar=1.0, in1=dense[:, b, :], op0=ALU.add,
                                               op1=ALU.mult).then_inc(evacuated[b], 1)
                slot, count = PLAN.landed("C", l, c, DECAY_ITEM)
                dve.wait_ge(landed[slot], count)
                for s in range(STEPS):
                    hh, j = divmod(s, TB)
                    n = SEQ - j * P
                    dve.wait_ge(st_ready, R * STEPS + (s + 1))
                    if s >= 2:
                        dve.wait_ge(rv_done, R * STEPS + (s - 1))
                    nc.vector.tensor_tensor(probsT[:, s % 2, 0:n], scores[:, s % 2, 0:n],
                                            ring[:, slot, hh * SEQ:hh * SEQ + n], ALU.mult).then_inc(st_decayed, 1)
                dve.wait_ge(rv_done, R * STEPS + STEPS)
                nc.vector.tensor_reduce(mean[:], by_head(O), AX_X, ALU.add).then_inc(gn_step, 1)
                dve.wait_ge(gn_step, R * GN_STEPS + 1)
                nc.vector.tensor_scalar(mean[:], mean[:], 1.0 / HEAD_DIM, None, ALU.mult).then_inc(gn_step, 1)
                dve.wait_ge(gn_step, R * GN_STEPS + 2)
                nc.vector.tensor_tensor(by_head(Y), by_head(O), bcast(mean), ALU.subtract).then_inc(gn_step, 1)
                dve.wait_ge(gn_step, R * GN_STEPS + 3)
                nc.vector.tensor_tensor(probs[:, 0, :], Y[:], Y[:], ALU.mult).then_inc(gn_step, 1)
                dve.wait_ge(gn_step, R * GN_STEPS + 4)
                nc.vector.tensor_reduce(var[:], probs[:, 0, :].rearrange("p (s e) -> p s e", e=HEAD_DIM), AX_X,
                                        ALU.add).then_inc(gn_step, 1)
                dve.wait_ge(gn_step, R * GN_STEPS + 5)
                nc.vector.tensor_scalar(var[:], var[:], 1.0 / HEAD_DIM, EPS, ALU.mult, ALU.add).then_inc(gn_step, 1)
                dve.wait_ge(gn_pow, R + 1)
                nc.vector.tensor_tensor(by_head(Y), by_head(Y), bcast(inv_std), ALU.mult).then_inc(yc_norm, 1)
                at = dve.snap(PAIRS * BRANCH["C"] + c)
                dve.wait_ge(yc_turned, R + 1)
                nc.vector.scalar_tensor_tensor(out=yT[:, bass.ds(at, 1), :], in0=Yt[:].rearrange("p (a n) -> p a n", a=1),
                                               scalar=half_gain[:, bass.ds(R, 1)],
                                               in1=gC[:].rearrange("p (a n) -> p a n", a=1),
                                               op0=ALU.mult, op1=ALU.mult).then_inc(yc_stored, 1)

            nc.vector.memset(ones[:], 1.0).then_inc(s_init, 1)
            nc.vector.memset(halves[:], -0.5).then_inc(s_init, 1)
            dve.wait_ge(s_x, 16)
            dve.wait_ge(s_const, 16)
            dve.wait_ge(s_small, 16)
            nc.vector.tensor_scalar(neg_sink[:], small[:, SMALL["sinks"]:SMALL["sinks"] + DEPTH * HEADS], -1.0, None,
                                    ALU.mult).then_inc(s_init, 1)
            nc.vector.tensor_scalar(half_gain[:], small[:, SMALL["ret_norm"]:SMALL["ret_norm"] + DEPTH * PAIRS],
                                    0.5, None, ALU.mult).then_inc(s_init, 1)
            nc.vector.tensor_scalar(half_gdn[:], small[:, SMALL["g_gdn"]:SMALL["g_gdn"] + 1], 0.5, None, ALU.mult
                                    ).then_inc(s_init, 1)
            nc.vector.memset(minus_half[:], -0.5).then_inc(s_init, 1)
            dve.wait_ge(cond_step, 1)
            nc.vector.scalar_tensor_tensor(out=cond[:], in0=cond_tanh[:], scalar=1.0,
                                           in1=small[:, SMALL["cond"]:SMALL["cond"] + 2 * KC], op0=ALU.add,
                                           op1=ALU.mult).then_inc(cond_step, 1)
            dve.wait_ge(cond_step, 2)
            nc.vector.tensor_scalar(cond[:], cond[:], 0.5, None, ALU.mult).then_inc(cond_step, 1)
            dve.wait_ge(s_init, INITS)
            with dve.Fori(0, DEPTH) as l:
                norm("norm1", l, 2 * l, lambda k: small[:, bass.ds(l * KC + (SMALL["attn_norm"] + k), 1)], hT)
                pre(l)
                with dve.Fori(0, PAIRS) as c:
                    attention("A", l, c)
                with dve.Fori(0, PAIRS) as c:
                    attention("B", l, c)
                rope("Dkv", l, 0, 0, rope_no("Dkv", l, 0), kI[:])
                with dve.Fori(0, PAIRS) as c:
                    attention("D", l, c)
                with dve.Fori(0, PAIRS) as c:
                    retention(l, c)
                for b in range(BANKS):
                    dve.wait_ge(evacuated[b], held_before("merge", l, b))
                settle(dve)
                with dve.Fori(0, KC) as d:
                    for n in range(N_BRANCH):
                        b, held = result_in("merge", l, d, n)
                        g = dve.snap(d + KC * n)
                        tmp = hT[:, bass.ds(d, 1), :] if n == 0 else (Y if n % 2 else gC)[:].rearrange("p (a n) -> p a n", a=1)
                        nc.vector.scalar_tensor_tensor(out=tmp, in0=gates[:, bass.ds(g, 1), :], scalar=1.0,
                                                       in1=dense[:, b:b + 1, :], op0=ALU.add, op1=ALU.mult
                                                       ).then_inc(evacuated[b], 1)
                        dve.wait_ge(evacuated[b], held + 1)
                        if n:
                            dve.wait_ge(merge_add, l * (3 * KC) + d * 3 + (n - 1 + OPEN))
                            nc.vector.tensor_tensor(hT[:, bass.ds(d, 1), :], hT[:, bass.ds(d, 1), :], tmp, ALU.add
                                                    ).then_inc(merge_add, 1)
                with dve.Fori(0, KC // 2) as c:
                    for j in range(2):
                        b, held = result_in("out", l, c, j)
                        x = xT[:, bass.ds(c * 2 + j, 1), :]
                        nc.vector.scalar_tensor_tensor(out=x, in0=dense[:, b:b + 1, :], scalar=0.5, in1=x,
                                                       op0=ALU.mult, op1=ALU.add).then_inc(evacuated[b], 1)
                norm("norm2", l, 2 * l + 1, lambda k: small[:, bass.ds(l * KC + (SMALL["ffn_norm"] + k), 1)], hT)
                with dve.Fori(0, FC) as f:
                    F = dve.snap(l * FC + f)
                    for j in range(2):
                        b, held = result_in("up", l, f, j)
                        at = dve.snap((l * (2 * FC) + f + j * FC) * 4 + SMALL["conv"])
                        dve.wait_ge(taps, F * 2 + (j + 1))
                        for shift, tap, done in ((1, 1, conv_step), (2, 0, evacuated[b])):
                            u = probs[:, j, shift:SEQ]
                            nc.vector.scalar_tensor_tensor(out=u, in0=dense[:, b, 0:SEQ - shift],
                                                           scalar=small[:, bass.ds(at + tap, 1)], in1=u,
                                                           op0=ALU.mult, op1=ALU.add).then_inc(done, 1)
                            if shift == 1:
                                dve.wait_ge(conv_step, F * 2 + (j + 1))
                    dve.wait_ge(up_tanh, F + 1)
                    dve.wait_ge(hidden_ready, F + OPEN)
                    nc.vector.scalar_tensor_tensor(out=probsT[:, 1, :], in0=probsT[:, 0, :], scalar=1.0,
                                                   in1=probs[:, 0, :], op0=ALU.add, op1=ALU.mult).then_inc(up_gate, 1)
                with dve.Fori(0, 2) as c:
                    for j in range(4):
                        b, held = result_in("down", l, c, j)
                        x = xT[:, bass.ds(c * 4 + j, 1), :]
                        nc.vector.scalar_tensor_tensor(out=x, in0=dense[:, b:b + 1, :], scalar=0.5, in1=x,
                                                       op0=ALU.mult, op1=ALU.add).then_inc(evacuated[b], 1)
            norm("normf", DEPTH, N_F, lambda k: small[:, SMALL["final_norm"] + k:SMALL["final_norm"] + k + 1], xT)

            L = DEPTH
            sm = lambda name, at=0, n=1: small[:, SMALL[name] + at:SMALL[name] + at + n]
            m4 = mod[:].rearrange("p (s k w) -> p s k w", s=6, w=2)
            dve.wait_ge(dense_done, PLAN.done("ada", L, 5, 7))
            nc.vector.tensor_tensor(mod[:].rearrange("p (s w) -> p s w", w=2),
                                    Yt[:, 0:2 * ADA_N].rearrange("p (s w) -> p s w", w=2),
                                    sm("b_ada", 0, ADA_N).unsqueeze(2).broadcast_to((P, ADA_N, 2)), ALU.add
                                    ).then_inc(mod_step, 1)
            dve.wait_ge(mod_step, 1)
            for r, (part, w, name) in enumerate(((1, 0, "g_pre_mix"), (1, 1, "g_pre_mix"), (2, 0, "g_post_mix"),
                                                 (4, 0, "g_pre_ffn"), (5, 0, "g_post_ffn"))):
                add = 1.0 if part in (1, 4) else 0.0
                nc.vector.scalar_tensor_tensor(out=gain[:, r, :], in0=m4[:, part, :, w], scalar=add,
                                               in1=sm(name, 0, KC), op0=ALU.add, op1=ALU.mult).then_inc(mod_step, 1)
            dve.wait_ge(mod_step, 6)

            def shifted(number, dst, part, w, n, before):
                dve.wait_ge(h_scaled, before + KC)
                for k in range(KC):
                    nc.vector.tensor_scalar(dst[:, k, 0:n], dst[:, k, 0:n], m4[:, part, k, w:w + 1], None, ALU.add
                                            ).then_inc(h_ready, 1)

            def residual(number):
                dve.wait_ge(h_ready, (number + 1) * KC)
                for k in range(KC):
                    nc.vector.tensor_tensor(xT[:, k, :], xT[:, k, :], hT[:, k, :], ALU.add).then_inc(x_added, 1)

            dve.wait_ge(h_ready, (N_F + 1) * KC)
            norm("normL", L, N_L, lambda k: gain[:, 0, k:k + 1], hx, sem=h_scaled)
            shifted(N_L, hx, 0, 0, SEQ, 0)
            hctx = hx[:, :, SEQ:SEQ + CTX]
            norm("normX", L, N_X, lambda k: gain[:, 1, k:k + 1], hctx, src=xc, n=CTX, sem=h_scaled)
            shifted(N_X, hctx, 0, 1, CTX, KC)

            with dve.Fori(0, 12) as c:
                at = dve.snap(c * 3 + SMALL["qkv_conv"])
                for j, (lo, n) in enumerate(((0, SEQ), (SEQ, CTX))):
                    b, held = result_in("qkv", L, c, j)
                    dve.wait_ge(cq_taps, c * 2 + (j + 1))
                    u = cv[:, bass.ds(c, 1), lo + 1:lo + n]
                    nc.vector.scalar_tensor_tensor(out=u, in0=dense[:, b:b + 1, 0:n - 1],
                                                   scalar=small[:, bass.ds(at, 1)], in1=u, op0=ALU.mult,
                                                   op1=ALU.add).then_inc(cq_conv, 1)
                    dve.wait_ge(cq_conv, c * 2 + (j + 1))
                    u = cv[:, bass.ds(c, 1), lo:lo + n - 1]
                    nc.vector.scalar_tensor_tensor(out=u, in0=dense[:, b:b + 1, 1:n],
                                                   scalar=small[:, bass.ds(at + 2, 1)], in1=u, op0=ALU.mult,
                                                   op1=ALU.add).then_inc(evacuated[b], 1)
                dve.wait_ge(cq_tanh, c + 1)
                u = cv[:, bass.ds(c, 1), :]
                nc.vector.scalar_tensor_tensor(
                    out=u, in0=probsT[:].rearrange("p a n -> p (a n)")[:, 0:XB * P].rearrange("p (a n) -> p a n", a=1),
                    scalar=1.0, in1=u, op0=ALU.add, op1=ALU.mult).then_inc(cq_done, 1)
            with dve.Fori(0, 4) as c:
                b, held = result_in("uz", L, c, 1)
                dve.wait_ge(z_tanh, c + 1)
                nc.vector.scalar_tensor_tensor(out=yT[:, bass.ds(c + 4, 1), :], in0=gC[:].rearrange("p (a n) -> p a n", a=1),
                                               scalar=1.0, in1=dense[:, b:b + 1, :], op0=ALU.add, op1=ALU.mult
                                               ).then_inc(evacuated[b], 1)
                dve.wait_ge(evacuated[b], held + 1)
                dve.sem_inc(z_done, 1)
            dve.wait_ge(evacuated[0], PLAN.bank("ab", L, 0, 0)[1] + 1)
            ab = abt[:].rearrange("p (t g h) -> p t g h", t=XB, h=GH)
            rows = lambda t, d: t[:, d * GH:(d + 1) * GH].unsqueeze(1).broadcast_to((P, XB, GH))
            dtb = sm("dt_bias", 0, 2 * GH)
            for d in range(2):
                nc.vector.tensor_tensor(sc3(zz, d), ab[:, :, 2 + d, :], rows(dtb, d), ALU.add).then_inc(ab_step, 1)
            dve.wait_ge(ab_step, 2)
            nc.vector.scalar_tensor_tensor(out=tmp_sc[:, 0:SC], in0=zz[:], scalar=-1.0, in1=zz[:], op0=ALU.mult,
                                           op1=ALU.max).then_inc(ab_step, 1)
            dve.wait_ge(ab_act, 5)
            nc.vector.scalar_tensor_tensor(out=zz[:], in0=zz[:], scalar=0.0, in1=tmp_sc[:, SC:2 * SC], op0=ALU.max,
                                           op1=ALU.add).then_inc(ab_step, 1)
            nc.vector.tensor_scalar(half_beta[:], beta[:], 0.25, 0.25, ALU.mult, ALU.add).then_inc(ab_step, 1)
            dve.wait_ge(ab_step, 5)
            for d in range(2):
                nc.vector.scalar_tensor_tensor(out=sc3(gg, d), in0=sc3(zz, d), scalar=-1.0, in1=rows(decay_rate[:], d),
                                               op0=ALU.mult, op1=ALU.mult).then_inc(ab_step, 1)
            nc.vector.tensor_scalar(beta[:], beta[:], 0.5, 0.5, ALU.mult, ALU.add).then_inc(ab_step, 1)
            dve.wait_ge(ab_act, 6)
            dve.wait_ge(ab_step, 8)
            nc.vector.tensor_tensor(bg[:], beta[:], egc[:], ALU.mult).then_inc(ab_step, 1)
            nc.vector.tensor_tensor(tmp_sc[:, 0:SC], scores[:, 0, SC:2 * SC], gcum[:], ALU.subtract
                                    ).then_inc(ab_step, 1)
            dve.wait_ge(l2_sums, 1)
            nc.vector.tensor_scalar(l2v[:], scores[:, 1, 0:8 * XB], 4 * EPS, None, ALU.add).then_inc(l2_var, 1)
            dve.wait_ge(l2_ready, 1)
            lq = l2s[:, 0:GH * XB].rearrange("p (h t) -> p t h", t=XB)
            lk = l2s[:, GH * XB:2 * GH * XB].rearrange("p (h t) -> p t h", t=XB)
            nc.vector.tensor_scalar(qs[:].rearrange("p (t h) -> p t h", h=GH), lq, GD ** -0.5, None, ALU.mult
                                    ).then_inc(ab_step, 1)
            dve.wait_ge(ab_step, 11)
            q3 = qs[:].rearrange("p (t h) -> p t h", h=GH)
            for d in range(2):
                nc.vector.tensor_tensor(sc3(bs, d), sc3(beta, d), lk, ALU.mult)
                last = nc.vector.tensor_tensor(sc3(eqs, d), sc3(egc, d), q3, ALU.mult)
            last.then_inc(ab_step, 1)
            for t in range(XB):
                dve.wait_ge(k_turned, t + 1)
                nc.vector.tensor_tensor(heads(ktok[:, t, :]), heads(bankA[t % 2]), per_head(lk[:, t, :]), ALU.mult
                                        ).then_inc(k_scaled, 1)
            for d in range(2):
                nc.vector.memset(state[d], 0.0).then_inc(ab_step, 1)
            dve.wait_ge(ab_step, 14)

            for n in range(UNITS):
                isl = n >= FIRST_L
                both = [(d, ORDER[d][n]) for d in range(2)]
                hcol = [slice(h * P, (h + 1) * P) for h in range(GH)]
                for d, b in both:
                    dve.wait_ge(u_row[d], n + 1)
                    for h in range(GH):
                        last = nc.vector.scalar_tensor_tensor(
                            out=W2["decay"][d][:, hcol[h]], in0=bankA[d][:, hcol[h]], scalar=sc_at(gcum, d, b)[:, h:h + 1],
                            in1=barred[:, d * P:(d + 1) * P], op0=ALU.subtract, op1=ALU.add)
                    last.then_inc(u_diff[d], 1)
                for d, b in both:
                    dve.wait_ge(u_kk[d], n + 1)
                    dve.wait_ge(u_decay[d], n + 1)
                    for h in range(GH):
                        last = nc.vector.scalar_tensor_tensor(
                            out=W2["A"][d][:, hcol[h]], in0=bankB[d][:, hcol[h]], scalar=sc_at(bs, d, b)[:, h:h + 1],
                            in1=W2["decay"][d][:, hcol[h]], op0=ALU.mult, op1=ALU.mult)
                    last.then_inc(u_a[d], 1)
                if isl:
                    for d, b in both:
                        dve.wait_ge(u_qk[d], n - FIRST_L + 1)
                        for h in range(GH):
                            last = nc.vector.scalar_tensor_tensor(
                                out=W2["X"][d][:, hcol[h]], in0=bankC[d][:, hcol[h]],
                                scalar=qs[:, b * GH + h:b * GH + h + 1], in1=W2["decay"][d][:, hcol[h]],
                                op0=ALU.mult, op1=ALU.mult)
                        last.then_inc(u_x[d], 1)
                for d, b in both:
                    dve.wait_ge(u_a[d], n + 1)
                    nc.vector.tensor_tensor(heads(W2["A_level"][d]), heads(W2["A"][d]), level_mask(d, 0), ALU.mult
                                            ).then_inc(u_t0[d], 1)
                for d, b in both:
                    dve.wait_ge(u_t0[d], n + 1)
                    nc.vector.tensor_tensor(heads(W2["T"][d]), ident.unsqueeze(1).broadcast_to((P, GH, P)),
                                            heads(W2["A_level"][d]), ALU.subtract).then_inc(u_t[d], 1)
                for lev in range(1, LEVELS):
                    for d, b in both:
                        dve.wait_ge(u_upd[d], n * (LEVELS - 1) + lev)
                        if lev < LEVELS - 1:
                            nc.vector.tensor_tensor(W2["T"][d], W2["T"][d], bankA[d], ALU.subtract)
                        nc.vector.tensor_tensor(W2["TT"][d], W2["TT"][d], bankC[d], ALU.subtract).then_inc(u_lvl[d], 1)
                for d, b in both:
                    dve.wait_ge(u_wu[d], n + 1)
                    nc.vector.tensor_copy(W2["u"][d], bankC[d]).then_inc(u_u[d], 1)
                for i in range(2):
                    for d, b in both:
                        c, hs = chunk_of(d, i)
                        dve.wait_ge(c_ws[d], 2 * n + i + 1)
                        nc.vector.tensor_tensor(W2["vnew"][d][hs, :], W2["u"][d][hs, :], bankB[d][hs, :], ALU.subtract
                                                ).then_inc(c_v[d], 1)
                    for d, b in both:
                        c, hs = chunk_of(d, i)
                        dve.wait_ge(c_sd[d], 2 * n + i + 1)
                        for h in range(GH):
                            last = nc.vector.scalar_tensor_tensor(
                                out=state[d][:, hcol[h]], in0=state[d][:, hcol[h]], scalar=etot_at(c, d, b, h),
                                in1=bankA[d][:, hcol[h]], op0=ALU.mult, op1=ALU.add)
                        last.then_inc(c_s[d], 1)
                        if isl:
                            if n >= 4 and (n, i) != (4, 0):
                                dve.wait_ge(c_o3[d], 2 * (n - 4) + i)
                            nc.vector.tensor_tensor(heads(W2["oscan"][d][hs, :]), heads(bankC[d][hs, :]),
                                                    per_head(sc_at(eqs, d, b)[hs, :]), ALU.mult).then_inc(c_o1[d], 1)
                            dve.wait_ge(c_oi[d], seen(n, i))
                            dve.wait_ge(c_o1[d], seen(n, i))
                            dst = o2[b] if n < 4 else W2["oscan"][d]
                            nc.vector.tensor_tensor(dst[hs, :], W2["oscan"][d][hs, :], bankB[d][hs, :], ALU.add
                                                    ).then_inc(c_o2[d], 1)
            for t in range(TB):
                dve.wait_ge(p_sq, t + 1)
                nc.vector.tensor_reduce(osum[:, t * GH:(t + 1) * GH], heads(SQ4[t]), AX_X, ALU.add).then_inc(p_red, 1)
            dve.wait_ge(p_red, TB)
            nc.vector.tensor_scalar(osum[:], osum[:], 1.0 / GD, EPS, ALU.mult, ALU.add).then_inc(p_ms, 1)
            dve.wait_ge(p_pow, 1)
            for t in range(TB):
                nc.vector.tensor_tensor(heads(o2[t]), heads(o2[t]), per_head(oscale[:, t * GH:(t + 1) * GH]), ALU.mult
                                        ).then_inc(p_on, 1)
            for t in range(TB):
                dve.wait_ge(p_turned, t + 1)
                z = zT[:, :, t * P:(t + 1) * P]
                nc.vector.scalar_tensor_tensor(out=z, in0=heads((bankA + bankB)[t]), scalar=half_gdn[:, 0:1], in1=z,
                                               op0=ALU.mult, op1=ALU.mult).then_inc(p_y, 1)
            norm("norm3", L, N_3, lambda k: gain[:, 2, k:k + 1], hT, src=hT)
            residual(N_3)
            dve.wait_ge(x_added, KC)
            norm("norm4", L, N_4, lambda k: gain[:, 3, k:k + 1], hT, sem=h_scaled)
            shifted(N_4, hT, 3, 0, SEQ, 2 * KC)
            rows8 = SEQ // GRID_W
            grid = lambda t: t.rearrange("p (r c) -> p r c", c=GRID_W)
            others = [(dy, dx) for dy in (-1, 0, 1) for dx in (-1, 0, 1) if (dy, dx) != (0, 0)]
            with dve.Fori(0, FC) as f:
                b, held = result_in("up2", L, f, 1)
                at = dve.snap(f * 9 + SMALL["dwc"])
                dve.wait_ge(taps, f + (2 * DEPTH * FC + 1))
                for m, (dy, dx) in enumerate(others):
                    r0, r1, c0, c1 = max(0, -dy), rows8 - max(0, dy), max(0, -dx), GRID_W - max(0, dx)
                    u = grid(probs[:, 1, :])[:, r0:r1, c0:c1]
                    v = grid(dense[:, b, :])[:, r0 + dy:r1 + dy, c0 + dx:c1 + dx]
                    if m:
                        dve.wait_ge(grid_step, f * 7 + m)
                    nc.vector.scalar_tensor_tensor(out=u, in0=v, scalar=small[:, bass.ds(at + (3 * (dy + 1) + dx + 1), 1)],
                                                   in1=u, op0=ALU.mult, op1=ALU.add
                                                   ).then_inc(grid_step if m < 7 else evacuated[b], 1)
                dve.wait_ge(up_tanh, f + (DEPTH * FC + 1))
                nc.vector.scalar_tensor_tensor(out=probsT[:, 1, :], in0=probsT[:, 0, :], scalar=1.0,
                                               in1=probs[:, 1, :], op0=ALU.add, op1=ALU.mult).then_inc(up_gate, 1)
            norm("norm5", L, N_5, lambda k: gain[:, 4, k:k + 1], hT, src=hT)
            residual(N_5)

        @block.gpsimd
        def _(pool):
            def swap_sin(r):
                pool.wait_ge(swap_ready, r + 1)
                pool.wait_ge(rope_done, r + OPEN)
                nc.gpsimd.tensor_tensor(swapped_sin[:], swapped[:], sin, ALU.mult).then_inc(swap_mul, 1)

            pool.wait_ge(s_const, 16)
            pool.wait_ge(s_init, INITS)
            with pool.Fori(0, DEPTH) as l:
                with pool.Fori(0, ROPES - 2 * PAIRS) as r:
                    swap_sin(l * ROPES + r)
                with pool.Fori(0, PAIRS) as c:
                    R = pool.snap(l * PAIRS + c)
                    for j in range(2):
                        swap_sin(rope_no("C", l, c, j))
                    pool.wait_ge(gn_step, R * GN_STEPS + GN_STEPS)
                    nc.gpsimd.tensor_tensor(inv_std[:], var[:], halves[:], ALU.pow).then_inc(gn_pow, 1)
                with pool.Fori(0, FC) as f:
                    F = pool.snap(l * FC + f)
                    pool.wait_ge(up_gate, F + (OPEN + 1))
                    _, held = PLAN.bank("up", l, f, 1)
                    pool.wait_ge(evacuated[1], held + 1)
                    nc.gpsimd.tensor_tensor(act_T[:, bass.ds(f, 1), :], probsT[:, 1:2, :], probs[:, 1:2, :],
                                            ALU.mult).then_inc(hidden_ready, 1)

            pool.wait_ge(l2_var, 1)
            nc.gpsimd.tensor_tensor(l2s[:], l2v[:], minus_half[:], ALU.pow).then_inc(l2_ready, 1)
            pool.wait_ge(kh_stored, XB)
            for n in range(UNITS):
                isl = n >= FIRST_L
                both = [(d, ORDER[d][n]) for d in range(2)]
                for lev in range(1, LEVELS):
                    for d, b in both:
                        if lev == 1:
                            pool.wait_ge(u_t[d], n + 1)
                        else:
                            pool.wait_ge(u_z[d], n * (LEVELS - 1) + lev - 1)
                        nc.gpsimd.tensor_tensor(heads(W2["A_level"][d]), heads(W2["A"][d]), level_mask(d, lev), ALU.mult
                                                ).then_inc(u_as[d], 1)
                    if lev == 2:
                        for d, b in both:
                            if n:
                                pool.wait_ge(c_sd[d], 2 * n)
                            if isl:
                                pool.wait_ge(u_xt[d], n - FIRST_L + 1)
                            for dst, src, scale in (("decay", ktok, bg), ("X", vtok, half_beta), ("kd", ktok, ed)):
                                nc.gpsimd.tensor_tensor(heads(W2[dst][d]), heads(src[:, b, :]), per_head(sc_at(scale, d, b)),
                                                        ALU.mult).then_inc(u_kv[d], 1)
                if n >= 4:
                    for i in range(2):
                        for d, b in both:
                            c, hs = chunk_of(d, i)
                            pool.wait_ge(c_o2[d], seen(n, i))
                            pool.wait_ge(c_o2[1 - d], seen(7 - n, 1))
                            nc.gpsimd.tensor_tensor(o2[b][hs, :], o2[b][hs, :], W2["oscan"][d][hs, :], ALU.add
                                                    ).then_inc(c_o3[d], 1)
                    for d in range(2):
                        pool.wait_ge(c_o3[d], 2 * (n - 4) + 2)
            pool.wait_ge(p_ms, 1)
            nc.gpsimd.tensor_tensor(oscale[:], osum[:], minus_half[:, 0:TB * GH], ALU.pow).then_inc(p_pow, 1)
            with pool.Fori(0, FC) as f:
                pool.wait_ge(up_gate, f + (DEPTH * FC + OPEN + 1))
                _, held = PLAN.bank("up2", DEPTH, f, 0)
                pool.wait_ge(evacuated[0], held + 1)
                nc.gpsimd.tensor_tensor(act_T[:, bass.ds(f, 1), :], probsT[:, 1:2, :], probs[:, 0:1, :],
                                        ALU.mult).then_inc(hidden_ready, 1)


def _blocks(w, cols=P):
    return w.reshape(-1, P, P).transpose(1, 0, 2).reshape(P, -1)


def _columns():
    sizes = dict(qA=512, kA=512, vA=512, fA=8, qB=512, kB=64, vB=64, qI=256, kI=64, wI=4, qC=512, kC=512,
                 vC=512, gC=512, qD=512, kD=128, vD=128, gates=4096)
    return dict(zip(sizes, np.cumsum([0] + list(sizes.values()))[:-1].tolist()))


AT = _columns()


def _layer_items(a, l):
    w = a["w_in"][l]
    col = lambda name, j, n=P: w[:, AT[name] + j:AT[name] + j + n]
    gate = lambda branch, c: [_blocks(col("gates", BRANCH[branch] * D_MODEL + (2 * c + g) * P)) for g in range(2)]
    items = []
    tok = np.concatenate([col("vB", 0, 64), col("fA", 0, 8), col("wI", 0, 4),
                          np.zeros((D_MODEL, P - TOK_COLS), w.dtype)], axis=1)
    items += [_blocks(tok), _blocks(np.concatenate([col("kI", 0, 64)] * 2, 1)), _blocks(col("qI", 0)),
              _blocks(col("qI", P)), _blocks(np.concatenate([col("kB", 0, 64)] * 2, 1))]
    for c in range(PAIRS):
        items += [_blocks(col(n, c * P)) for n in ("qA", "kA", "vA")] + gate("A", c)
    for c in range(PAIRS):
        items += [_blocks(col("qB", c * P))] + gate("B", c)
    items += [_blocks(col("kD", 0)), _blocks(col("vD", 0))]
    for c in range(PAIRS):
        pair = np.concatenate([col("qD", c * 64, 64), col("qD", (c + PAIRS) * 64, 64)], 1)
        items += [_blocks(pair)] + gate("D", c)
    for c in range(PAIRS):
        items += [_blocks(col(n, c * P)) for n in ("qC", "kC", "vC", "gC")] + gate("C", c) + [DECAYS[c]]
    wb = a["w_branch"][l].copy()
    wb[3] = wb[3].reshape(2, PAIRS, 64, D_MODEL).transpose(1, 0, 2, 3).reshape(512, D_MODEL)
    for d in range(KC):
        for n in (0, 2):
            items.append(np.concatenate([_blocks(wb[n + m][:, d * P:(d + 1) * P]) for m in range(2)], 1))
    items += [_blocks(a["w_out"][l][:, d * P:(d + 1) * P]) for d in range(KC)]
    for f in range(FC):
        items += [_blocks(a["w_up"][l][:, j * D_FF + f * P:j * D_FF + (f + 1) * P]) for j in range(2)]
    down = np.concatenate([_blocks(a["w_down"][l][:, d * P:(d + 1) * P]) for d in range(KC)], 1)
    items += [down[:, i * KC * P:(i + 1) * KC * P] for i in range(FC)]
    return items


def _decays():
    g = np.log(1.0 - 2.0 ** (-5.0 - np.arange(HEADS)))
    dist = np.arange(SEQ)[None, :] - np.arange(P)[:, None]
    full = np.where(dist >= 0, np.exp(np.maximum(dist, 0)[None] * g[:, None, None]), 0.0) * QK_SCALE
    full = full.astype(np.float32)
    return [np.concatenate([full[2 * c], full[2 * c + 1]], 1) for c in range(PAIRS)]


DECAYS = _decays()


def _tail_items(a):
    w_ada, w_in, w_out, w_up, w_down = (a[k][0] for k in ("w_ada_2", "w_in_2", "w_out_2", "w_up_2", "w_down_2"))
    items = [_blocks(w_ada[:, j * P:(j + 1) * P]) for j in range(ADA_N)]
    items.append(_blocks(np.concatenate([w_in[:, 2560:2576], np.zeros((D_MODEL, P - 16), w_in.dtype)], 1)))
    items += [_blocks(w_in[:, 512 + j * P:512 + (j + 1) * P]) for j in range(12)]
    for c in range(4):
        items += [_blocks(w_in[:, c * P:(c + 1) * P]), _blocks(w_in[:, 2048 + c * P:2048 + (c + 1) * P])]
    ch = np.arange(GD)
    angle = 2 * np.pi * (np.outer(ch, ch) % GD) / GD
    wf = a["w_fourier_2"][0].transpose(1, 0, 2).reshape(GD, 4 * GD)
    items.append(np.concatenate([wf, np.cos(angle).astype(np.float32), np.sin(angle).astype(np.float32),
                                 np.zeros((P, 2 * P), np.float32)], 1))
    at = np.arange(SEQ)
    angle = 2 * np.pi * (np.outer(at, at) % SEQ) / SEQ
    for m in (np.cos(angle), -np.sin(angle)):
        m = m.astype(np.float32).reshape(2, 2, P, SEQ).transpose(0, 2, 1, 3).reshape(2, P, 2 * SEQ)
        items += [m[0], m[1]]
    items += [_blocks(w_out[:, d * P:(d + 1) * P]) for d in range(KC)]
    for f in range(FC):
        items += [_blocks(w_up[:, j * D_FF + f * P:j * D_FF + (f + 1) * P]) for j in range(2)]
    down = np.concatenate([_blocks(w_down[:, d * P:(d + 1) * P]) for d in range(KC)], 1)
    items += [down[:, i * KC * P:(i + 1) * KC * P] for i in range(FC)]
    return items


def _consts2():
    i, j = np.arange(P)[:, None], np.arange(P)[None, :]
    same = i // CHUNK == j // CHUNK
    barred = [np.where(same & see, 0.0, -NEG) for see in (j <= i, j >= i)]
    upto = [same & (i <= j), same & (i >= j)]
    lev = []
    for s in (1 << n for n in range(LEVELS)):
        lev.append((i // (2 * s) == j // (2 * s)) & (i % (2 * s) >= s) & (j % (2 * s) < s))
    return [*barred, *upto, same, *lev, *[m.T for m in lev]]


def _consts():
    half = HEAD_DIM // 2
    inv = (1.0 / (np.float32(10000.0) ** (np.arange(half, dtype=np.float32) * 2.0 / HEAD_DIM))).astype(np.float32)
    ang = (np.arange(SEQ, dtype=np.float32)[None, :] * inv[:, None]).astype(np.float32)
    c, s = np.cos(ang), np.sin(ang)
    i = np.arange(P)
    return np.concatenate([
        np.concatenate([c] * 4), np.concatenate([-s, s] * 2), np.eye(P),
        np.where(i[None, :] <= i[:, None], 0.0, NEG), np.where(i[None, :] > i[:, None], 0.0, NEG),
        (np.arange(SEQ)[None, :] >= i[:, None]), *_consts2(),
    ], axis=1).astype(np.float32)


def _feature_major(v, n):
    v = np.asarray(v)
    return v.reshape(-1, n, P).transpose(2, 0, 1).reshape(P, -1)


def _small(a):
    rows = lambda v: np.broadcast_to(np.asarray(v).reshape(1, -1), (P, np.asarray(v).size))
    conv = np.concatenate([a["conv_w"], a["conv_b"][:, None]], 1)
    conv = conv.reshape(DEPTH, 4, 2 * FC, P).transpose(3, 0, 2, 1).reshape(P, -1)
    return np.concatenate([
        _feature_major(a["attn_norm"], KC), _feature_major(a["ffn_norm"], KC),
        _feature_major(a["ret_norm"], PAIRS), rows(a["forget_bias"]), rows(a["attn_sinks"]),
        _feature_major(a["final_norm"], KC), conv, _feature_major(a["b_ada_2"][0], ADA_N),
        *[_feature_major(a[n][0], KC) for n in ("g_pre_mix_2", "g_post_mix_2", "g_pre_ffn_2", "g_post_ffn_2")],
        a["g_gdn_2"].reshape(P, 1), rows(a["a_log_2"]), rows(a["dt_bias_2"]),
        a["w_qkv_conv_2"][0].reshape(3, 12, P).transpose(2, 1, 0).reshape(P, -1),
        a["w_dwc_2"][0].reshape(9, FC, P).transpose(2, 1, 0).reshape(P, -1),
        np.stack([a["c_2"][0], a["c_ctx_2"]], -1).reshape(KC, P, 2).transpose(1, 0, 2).reshape(P, -1),
    ], axis=1)


def kernel(**inputs):
    import concourse.bacc as bacc
    from concourse.bass_utils import run_bass_kernel_spmd

    a = {k: np.asarray(v) for k, v in inputs.items()}
    items = []
    for l in range(DEPTH):
        items += _layer_items(a, l)
    items += _tail_items(a)
    assert len(items) == PLAN.total_items, (len(items), PLAN.total_items)
    arrays = {
        "x_in": np.ascontiguousarray(a["x"][0].reshape(SEQ, KC, P).transpose(2, 1, 0)),
        "stream": np.stack(items),
        "small": np.ascontiguousarray(_small(a)),
        "consts": _consts(),
        "ctx": np.ascontiguousarray(a["ctx_2"][0].reshape(CTX, KC, P).transpose(2, 1, 0)),
    }
    nc = bacc.Bacc("TRN2", target_bir_lowering=False, num_devices=1)
    args = [nc.dram_tensor(k, v.shape, F32, kind="ExternalInput").ap() for k, v in arrays.items()]
    out = nc.dram_tensor("out", (P, KC, SEQ), F32, kind="ExternalOutput").ap()
    build_program(nc, *args, out)
    r = run_bass_kernel_spmd(nc, [arrays], core_ids=[0])
    y = np.asarray(r.results[0]["out"])
    return y.transpose(2, 1, 0).reshape(1, SEQ, D_MODEL)
```

```python
from contextlib import ExitStack

import numpy as np

import concourse.bass as bass
from concourse import mybir

F32 = mybir.dt.float32
F32R = mybir.dt.float32r
ALU = mybir.AluOpType
ACT = mybir.ActivationFunctionType
AX_X = mybir.AxisListType.X

P = 128
D_MODEL, SEQ, DEPTH = 1024, 512, 2
KC = D_MODEL // P
TB = SEQ // P
HEAD_DIM, HEADS, IDX_HEADS, N_BRANCH = 64, 8, 4, 4
PAIRS = HEADS // 2
D_FF = 2816
FC = D_FF // P
TOPK = min(256, SEQ // 4)
EPS = 1e-6
NEG = -1e30
TAKEN = -3e38
QK_SCALE = HEAD_DIM ** -0.5

LAYER = [
    ("norm1", 1, 0, 1), ("pre", 1, 5, 5), ("A", PAIRS, 5, 5), ("B", PAIRS, 3, 3), ("Dkv", 1, 2, 2),
    ("D", PAIRS, 3, 3), ("C", PAIRS, 7, 6), ("merge", KC, 5, 4), ("out", KC // 2, 2, 2),
    ("norm2", 1, 0, 1), ("up", FC // 2, 4, 4), ("down", 2, 11, 4),
]
TAIL = [
    ("normf", 1, 0, 1), ("normX", 1, 0, 1), ("normL", 1, 0, 1), ("ab", 1, 1, 1),
    ("qkv", 4, 3, 6), ("uz", 4, 2, 2), ("four", 1, 5, 14), ("out2", KC // 2, 2, 2), ("norm3", 1, 0, 1),
    ("norm4", 1, 0, 1), ("up2", FC // 2, 4, 4), ("down2", 2, 11, 4), ("norm5", 1, 0, 1),
]
CTX = 256
GH, GD, CHUNK = 4, 128, 64
XB = (SEQ + CTX) // P
LEVELS = 6
GRID_W = 64
ORDER = ([4, 5, 0, 1, 2, 3], [5, 4, 3, 2, 1, 0])
UNITS = 6
FIRST_L = 2
ADA_N = 6 * KC
ADA_L, ADA_T = ADA_N // DEPTH, ADA_N // DEPTH // KC
MERGE_ITEM = (0, 0, 3, 3)
ADA_ITEM = (1, 2, 4)
SLOTS = 6
HI_SLOTS = 3
FFN_ITEMS = 3 * FC
HIDDEN_OPEN = 2
OPEN = 1
BANKS = 2
PV_LAG, TR_LAG = 3, 2
STEPS = 2 * TB
GATES_FIRST = {"A": 0, "B": 5, "D": 5}
GATE_STEPS = {"A": [2, 2, 2, 2, 1, 1, 1, 1, 1, 1, 1], "B": [1] * 9 + [0] * 2, "D": [1] * 9 + [0] * 2}
RET_GATES = [1] * 8 + [0]
GATE0_AT = {"A": 5, "B": 3, "D": 3}
DECAY_ITEM = 6
TOK_COLS = HEAD_DIM + HEADS + IDX_HEADS
IDX_SCALE = IDX_HEADS ** -0.5 * HEAD_DIM ** -0.5
FFT_SCALE = (SEQ * GD) ** -0.5
INITS = 6
BRANCH = {"A": 0, "B": 1, "C": 2, "D": 3}


def item_result(name, j):
    if name == "merge":
        return (1, 1, 2, 3, 3)[j]
    if name == "qkv":
        return 2 * j + 1
    if name == "four":
        return 13 if j else 1
    if name in ("down", "down2"):
        return (KC * j + KC - 1) // FC
    return min(j, RESULTS[name] - 1)


class Plan:

    def __init__(self):
        self.item_base, self.out_base, self.slot_base, self.bank_base, self.items = {}, {}, {}, {}, {}
        for table in (LAYER, TAIL):
            n = m = 0
            slot, bank = [0] * SLOTS, [0] * BANKS
            for name, turns, items, outs in table:
                self.item_base[name], self.out_base[name], self.items[name] = n, m, items
                self.slot_base[name], self.bank_base[name] = list(slot), list(bank)
                for j in range(items):
                    slot[j % SLOTS] += turns
                for j in range(outs):
                    bank[j % BANKS] += turns
                n += turns * items
                m += turns * outs
            if table is LAYER:
                self.layer_items, self.layer_outs, self.layer_slot, self.layer_bank = n, m, slot, bank
            self.tail_items = n
        self.total_items = DEPTH * self.layer_items + self.tail_items
        self.slack, done = {}, {}
        for layer, table in [(l, LAYER) for l in range(DEPTH)] + [(DEPTH, TAIL)]:
            for name, turns, items, _ in table:
                for turn in range(turns):
                    first = self.result(name, layer, turn, 0)
                    for j in range(items):
                        key, s = (name, j, turn > 0), j % SLOTS
                        room = min(first, first - done[s] if s in done else first)
                        self.slack[key] = min(self.slack.get(key, room), room)
                        done[s] = self.result(name, layer, turn, item_result(name, j)) + 1

    def item(self, name, layer, turn, j):
        return layer * self.layer_items + turn * self.items[name] + (self.item_base[name] + j)

    def slot_free(self, name, layer, turn, j, later):
        return self.result(name, layer, turn, 0) + (OPEN - self.slack[name, j, later])

    def done(self, name, layer, turn, j):
        return self.result(name, layer, turn, j) + (OPEN + 1)

    def landed(self, name, layer, turn, j):
        s = j % SLOTS
        per = len(range(s, self.items[name], SLOTS))
        return s, (layer * (16 * self.layer_slot[s]) + turn * (16 * per)
                   + 16 * (self.slot_base[name][s] + j // SLOTS + 1))

    def result(self, name, layer, turn, j):
        return layer * self.layer_outs + turn * RESULTS[name] + (self.out_base[name] + j)

    def bank(self, name, layer, turn, j):
        b = j % BANKS
        per = len(range(b, RESULTS[name], BANKS))
        return b, layer * self.layer_bank[b] + turn * per + (self.bank_base[name][b] + j // BANKS + OPEN)


RESULTS = {name: outs for name, _, _, outs in LAYER + TAIL}
PLAN = Plan()


def held_before(name, layer, b):
    return layer * PLAN.layer_bank[b] + (PLAN.bank_base[name][b] + OPEN)


SMALL = {}


def _place_small():
    at = 0
    for name, n in (("attn_norm", DEPTH * KC), ("ffn_norm", DEPTH * KC), ("ret_norm", DEPTH * PAIRS),
                    ("forget_bias", DEPTH * HEADS), ("sinks", DEPTH * HEADS), ("final_norm", KC),
                    ("conv", DEPTH * 2 * FC * 4), ("b_ada", ADA_N), ("g_pre_mix", KC), ("g_post_mix", KC),
                    ("g_pre_ffn", KC), ("g_post_ffn", KC), ("g_gdn", 1), ("a_log", 2 * GH),
                    ("dt_bias", 2 * GH), ("qkv_conv", 12 * 3), ("dwc", FC * 9), ("cond", KC * 2)):
        SMALL[name] = at
        at += n
    return at


SMALL_N = _place_small()
CONSTS = {"cos": 512, "sin": 512, "ident": 128, "causal": 128, "before": 128, "tri": 512,
          "barred": 2 * 128, "upto": 2 * 128, "chunk_ones": 128, "levels": 2 * LEVELS * 128}
CONST_AT = dict(zip(CONSTS, np.cumsum([0] + list(CONSTS.values()))[:-1].tolist()))
CONST_N = sum(CONSTS.values())


def build_program(nc, x_in, stream, small_in, const_in, ctx_in, out):
    with ExitStack() as ctx:
        place = {}

        def sb(name, shape):
            place[name] = nc.sbuf_base
            return ctx.enter_context(nc.sbuf_tensor(name, shape, F32))

        def sem(name):
            return ctx.enter_context(nc.semaphore(name))

        xT = sb("xT", [P, KC, SEQ])
        hT = sb("hT", [P, KC, SEQ])
        wide = sb("wide", [P, 58, SEQ])
        gates = wide[:, 0:32, :]
        yT = wide[:, 32:48, :]
        ring = sb("ring", [P, SLOTS, KC * P])
        small = sb("small_sb", [P, SMALL_N])
        const = sb("const_sb", [P, CONST_N])
        qT, kT, kB, kI = (wide[:, 48 + n, :] for n in range(4))
        vt = wide[:, 52, :].rearrange("p (t n) -> p t n", t=TB)
        tok = wide[:, 53, :].rearrange("p (t n) -> p t n", t=TB)
        qI = wide[:, 54:56, :]
        swapped, swapped_sin = wide[:, 56, :], wide[:, 57, :]
        def same_place(name, at, shape, dtype=F32R):
            return nc.alloc_sbuf_tensor_at(f"{name}_{at}_as_{dtype}", shape, dtype, offset=place[name] + at * SEQ * 4)
        hT_lo = same_place("hT", 0, [P, KC, SEQ])
        ring_lo = same_place("ring", 0, [P, SLOTS, KC * P])
        hidden, hidden_lo = same_place("wide", 0, [P, FC, SEQ], F32), same_place("wide", 0, [P, FC, SEQ])
        hidden_hi = same_place("wide", FC, [P, FC, SEQ])
        hT_hi = same_place("wide", 2 * FC, [P, KC, SEQ])
        ring_hi = same_place("wide", 52, [P, HI_SLOTS, KC * P])
        probs = sb("probs", [P, 2, SEQ])
        probsT = sb("probsT", [P, 2, SEQ])
        Y = sb("Y", [P, SEQ])
        gC = sb("gC", [P, SEQ])
        ones = sb("ones", [P, P])
        masks = ctx.enter_context(nc.sbuf_tensor("masks", [P, 3 * P], mybir.dt.bfloat16))
        ident_16, causal_16, before_16 = (masks[:, n * P:(n + 1) * P] for n in range(3))
        halves = sb("halves", [P, HEADS])
        row_max, neg_max = sb("row_max", [P, STEPS]), sb("neg_max", [P, STEPS])
        row_sum, sink_exp = sb("row_sum", [P, STEPS]), sb("sink_exp", [P, STEPS])
        inv_sum = sb("inv_sum", [P, STEPS])
        mean, var, inv_std = sb("mean", [P, STEPS]), sb("var", [P, STEPS]), sb("inv_std", [P, STEPS])
        neg_sink = sb("neg_sink", [P, DEPTH * HEADS])
        half_gain = sb("half_gain", [P, DEPTH * PAIRS])
        top8 = sb("top8", [P, TB, 8])
        logf = sb("logf", [P, 4, TB * HEADS])
        negF = gates
        NEGF = BRANCH["C"] * KC
        sel = yT
        SEL = BRANCH["C"] * PAIRS
        cos, sin, ident, causal, before, tri, barred, upto, chunk_ones, levels = (
            const[:, CONST_AT[k]:CONST_AT[k] + CONSTS[k]] for k in CONSTS)

        flat = gates[:].rearrange("p a n -> p (a n)")
        hx = flat[:, 0:KC * XB * P].rearrange("p (k n) -> p k n", k=KC)
        cv_flat = flat[:, KC * XB * P:KC * XB * P + 12 * XB * P]
        cv = cv_flat.rearrange("p (c n) -> p c n", c=12)
        ktok = flat[:, 0:XB * SEQ].rearrange("p (t n) -> p t n", t=XB)
        vtok = flat[:, XB * SEQ:2 * XB * SEQ].rearrange("p (t n) -> p t n", t=XB)
        khT = cv_flat[:, 8 * XB * P:12 * XB * P].rearrange("p (t n) -> p t n", t=XB)
        uT, zT = yT[:, 0:4, :], yT[:, 4:8, :]
        xc = yT[:, 8:12, :].rearrange("p a (b n) -> p (a b) n", n=CTX)
        free = ([hT[:, k, :] for k in range(KC)] + [qT[:], kT[:], vt[:].rearrange("p t n -> p (t n)"), kB[:], kI[:],
                qI[:, 0, :], qI[:, 1, :], tok[:].rearrange("p t n -> p (t n)"), swapped[:], swapped_sin[:],
                probs[:, 0, :], probs[:, 1, :], probsT[:, 0, :], probsT[:, 1, :]]
                + [yT[:, k, :] for k in range(8, 16)] + [gates[:, 30, :], gates[:, 31, :]])
        names = ("decay", "A", "A_level", "T", "TT", "Z", "X", "wT", "u", "kd", "attnT", "vnew", "oscan")
        W2 = {name: (free[2 * i], free[2 * i + 1]) for i, name in enumerate(names)}
        state = (free[26], free[27])
        o2 = free[28:32]
        wc, ws, p1, p2 = W2["A_level"] + W2["Z"]
        mod = sb("mod", [P, ADA_N * 2])
        cond_tanh, cond = sb("cond_tanh", [P, KC * 2]), sb("cond", [P, KC * 2])
        gain = sb("gain", [P, 5, KC])
        dead_at = [0]

        def over_rope(n):
            at = dead_at[0]
            dead_at[0] += n
            assert dead_at[0] <= 2 * SEQ
            return const[:, at:at + n]
        SC = 2 * XB * GH
        abt = over_rope(XB * 16)
        zz, gg, beta, half_beta, gcum, egc, ed, bs, bg, eqs = (over_rope(SC) for _ in range(10))
        tmp_sc = over_rope(2 * SC)
        etot = over_rope(2 * SC)
        decay_rate = over_rope(2 * GH)
        l2s, l2v = over_rope(8 * XB), over_rope(8 * XB)
        qs = over_rope(XB * GH)
        osum, oscale = over_rope(TB * GH), over_rope(TB * GH)
        minus_half = sb("minus_half", [P, 8 * XB])
        half_gdn = sb("half_gdn", [P, 1])

        def psum(name, shape):
            return ctx.enter_context(nc.psum_tensor(name, shape, F32))
        dense = psum("dense", [P, BANKS, SEQ])
        scores = psum("scores", [P, 2, SEQ])
        turned = psum("turned", [P, 2, SEQ])
        O = psum("O", [P, SEQ])
        Yt = psum("Yt", [P, SEQ])

        side_a, side_b = (probs[:, 0, :], Y[:]), (probs[:, 1, :], gC[:])
        grid_in = (swapped, swapped_sin)

        s_x, s_small, s_const = sem("x_landed"), sem("small_landed"), sem("const_landed")
        landed = [sem(f"item_landed{s}") for s in range(SLOTS)]
        dense_done = sem("dense_done")
        evacuated = [sem(f"dense_evacuated{b}") for b in range(BANKS)]
        s_init = sem("init_done")
        squared, square_used, norm_root, norm_inv, h_ready = (
            sem("squared"), sem("square_used"), sem("norm_root"), sem("norm_inv"), sem("h_ready"))
        swap_ready, swap_mul, rope_done = sem("swap_ready"), sem("swap_mul"), sem("rope_done")
        f_dve, f_act, f_bcast, f_copied = (sem("f_dve"), sem("f_act"), sem("f_bcast"), sem("f_copied"))
        dots_ready, relu_ready, score_step, topk_step = (
            sem("dots_ready"), sem("relu_ready"), sem("score_step"), sem("topk_step"))
        scores_ready, logits_ready, negmax_ready, probs_ready, turned_ready, turned_copied, pv_done = (
            sem("scores_ready"), sem("logits_ready"), sem("negmax_ready"), sem("probs_ready"),
            sem("turned_ready"), sem("turned_copied"), sem("pv_done"))
        settled = sem("wait_taken")
        biased = sem("scores_biased")
        y_sum, y_inv, y_norm, y_turned, y_stored = (
            sem("y_sum"), sem("y_inv"), sem("y_norm"), sem("y_turned"), sem("y_stored"))
        st_ready, st_decayed, rv_done, gc_tanh = (
            sem("st_ready"), sem("st_decayed"), sem("rv_done"), sem("gc_tanh"))
        gn_step, gn_pow, yc_norm, yc_turned, yc_stored = (
            sem("gn_step"), sem("gn_pow"), sem("yc_norm"), sem("yc_turned"), sem("yc_stored"))
        merge_add, masks_ready = sem("merge_add"), sem("masks_ready")
        s_io, cond_step, mod_step, h_scaled, x_added = (
            sem("ctx_landed_out_stored"), sem("cond_step"), sem("mod_step"), sem("h_scaled"), sem("x_added"))
        ab_step, ab_act, ab_sums, l2_squared, l2_used, l2_sums, l2_var, l2_ready = (
            sem("ab_step"), sem("ab_act"), sem("ab_sums"), sem("l2_squared"), sem("l2_used"), sem("l2_sums"),
            sem("l2_var"), sem("l2_ready"))
        cq_taps, cq_tanh, cq_done, cq_conv, z_tanh, z_done = (
            sem("cq_taps"), sem("cq_tanh"), sem("cq_done"), sem("cq_conv"), sem("z_tanh"), sem("z_done"))
        v_turned, v_stored, k_turned, k_scaled, kh_turned, kh_stored = (
            sem("v_turned"), sem("v_stored"), sem("k_turned"), sem("k_scaled"), sem("kh_turned"), sem("kh_stored"))
        two = lambda name: (sem(name + "_fwd"), sem(name + "_bwd"))
        u_row, u_diff, u_decay, u_kk, u_a, u_qk, u_x, u_xt, u_attn, u_t0, u_t, u_tt, u_ttc = (
            two(n) for n in ("u_row", "u_diff", "u_decay", "u_kk", "u_a", "u_qk", "u_x", "u_xt", "u_attn", "u_t0",
                             "u_t", "u_tt", "u_ttc"))
        u_as, u_z, u_zc, u_upd, u_lvl, u_kv, u_wu, u_w, u_u = (
            two(n) for n in ("u_as", "u_z", "u_zc", "u_upd", "u_lvl", "u_kv", "u_wu", "u_w", "u_u"))
        c_ws, c_v, c_sd, c_s, c_oi, c_o1, c_o2, c_o3 = (
            two(n) for n in ("c_ws", "c_v", "c_sd", "c_s", "c_oi", "c_o1", "c_o2", "c_o3"))
        p_sq, p_dve, p_pow, p_turned = (sem(n) for n in ("p_sq", "p_dve", "p_pow", "p_turned"))
        P_SUMS, P_MEANS, P_SCALED, P_GATED = TB, TB + 1, 2 * TB + 1, 3 * TB + 1
        weights_hi, weights_lo, weights_used, hidden_hi_ready, hidden_lo_ready, h_hi, h_lo_even, h_lo_odd = (
            sem(n) for n in ("weights_hi", "weights_lo", "weights_used", "hidden_hi_ready", "hidden_lo_ready",
                             "h_hi", "h_lo_even", "h_lo_odd"))
        taps, conv_step, up_tanh, up_gate, hidden_ready = (
            sem("taps"), sem("conv_step"), sem("up_tanh"), sem("up_gate"), sem("hidden_ready"))

        ATT = ("A", "B", "D")
        ROPES = 4 + 4 + 1 + 4 + 8
        ROPE_BASE = {"pre": 0, "B": 4, "Dkv": 8, "D": 9, "C": 13}
        DOTS = (TB - 1) * IDX_HEADS
        TOPK_ROUNDS = TOPK // 8
        assert 2 * TOPK_ROUNDS == PAIRS * STEPS
        TOPK_STEPS = 2 * TOPK_ROUNDS * (TB - 1) + 2 * (TB - 1) + 1
        GN_STEPS = 6

        def att_turn(name, layer, c):
            return layer * (3 * PAIRS) + c + ATT.index(name) * PAIRS

        def rope_no(name, layer, c, j=0):
            per = {"pre": 4, "B": 1, "Dkv": 1, "D": 1, "C": 2}[name]
            return layer * ROPES + c * per + (ROPE_BASE[name] + j)

        def key_range(name, i):
            return (max(0, i - 1) * P if name == "D" else 0), (i + 1) * P

        def gate_index(name, c):
            return 2 * c + BRANCH[name] * KC

        bankA = (scores[:, 0, :], scores[:, 1, :])
        bankB = (turned[:, 0, :], turned[:, 1, :])
        bankC = (O[:], Yt[:])
        N_F, N_X, N_L, N_3, N_4, N_5 = (2 * DEPTH + i for i in range(6))

        SQ4 = W2["A_level"] + W2["Z"]

        def sc3(t, d):
            return t[:, d * XB * GH:(d + 1) * XB * GH].rearrange("p (t h) -> p t h", h=GH)

        def level_mask(d, lev):
            at = (d * LEVELS + lev) * P
            return levels[:, at:at + P].unsqueeze(1).broadcast_to((P, GH, P))

        def heads(t):
            return t.rearrange("p (h n) -> p h n", h=GH)

        def per_head(cols):
            return cols.unsqueeze(2).broadcast_to((cols.shape[0], GH, GD))

        def sc_at(t, d, b):
            at = (d * XB + b) * GH
            return t[:, at:at + GH]

        def etot_at(c, d, b, h):
            at = (c * 2 * XB + d * XB + b) * GH + h
            return etot[:, at:at + 1]

        def chunk_of(d, i):
            c = i if d == 0 else 1 - i
            return c, slice(CHUNK * c, CHUNK * (c + 1))

        def seen(n, i=-1):
            return 2 * (n - FIRST_L) + i + 1

        block = ctx.enter_context(nc.Block())


        def weights_no(name, l, c, j):
            return l * FFN_ITEMS + (c * 4 + j if name.startswith("up") else c * (FC // 2) + (j + 2 * FC))

        def settle(eng):
            eng.sem_inc(settled, 1)

        def softmax_scores(name):
            return QK_SCALE if name == "D" else 1.0

        @block.sync
        def _(sp):
            for freed in (dense_done, swap_mul, rope_done, y_stored, yc_stored, yc_norm, up_gate,
                          merge_add, cq_done, z_done, weights_used, *evacuated):
                sp.sem_inc(freed, OPEN)
            sp.sem_inc(hidden_ready, HIDDEN_OPEN)
            sp.dma_start(xT[:], x_in).then_inc(s_x, 16)
            sp.dma_start(small[:], small_in).then_inc(s_small, 16)
            sp.dma_start(const[:], const_in).then_inc(s_const, 16)

            def load(name, l, c, later=False):
                for j in range(PLAN.items[name]):
                    s, _ = PLAN.landed(name, l, c, j)
                    at = sp.snap(PLAN.item(name, l, c, j))
                    free = sp.snap(PLAN.slot_free(name, l, c, j, later))
                    if name in ("C", "merge"):
                        decays = sp.snap(l * PAIRS + (c + OPEN if name == "C" else PAIRS + OPEN))
                    if name in ("C", "merge") and s == DECAY_ITEM % SLOTS:
                        sp.wait_ge(yc_norm, decays)
                        settle(sp)
                    sp.wait_ge(dense_done, free)
                    sp.dma_start(ring[:, s:s + 1, :], stream[bass.ds(at, 1)].rearrange("a p n -> p a n")
                                 ).then_inc(landed[s], 16)

            with sp.Fori(0, DEPTH) as l:
                for name, turns, items, _ in LAYER:
                    if items:
                        load(name, l, 0)
                    if items and turns > 1:
                        with sp.Fori(1, turns) as c:
                            load(name, l, c, later=True)
            for name, turns, items, _ in TAIL:
                if name == "qkv":
                    sp.wait_ge(dense_done, PLAN.done("down", DEPTH - 1, 1, 3))
                    sp.dma_start(xc, ctx_in).then_inc(s_io, 16)
                if items:
                    load(name, DEPTH, 0)
                if items and turns > 1:
                    with sp.Fori(1, turns) as c:
                        load(name, DEPTH, c, later=True)
            for k in range(0, KC, 2):
                sp.wait_ge(x_added, KC + k + 2)
                sp.dma_start(out[:, k:k + 2, :], xT[:, k:k + 2, :]).then_inc(s_io, 16)
            sp.wait_ge(s_io, 16 + 16 * (KC // 2))

        @block.tensor
        def _(pe):
            def open_bank(name, l, c, j):
                b, held = PLAN.bank(name, l, c, j)
                pe.wait_ge(evacuated[b], held)
                return b

            def evac_wait(name, l, c, j):
                b, held = PLAN.bank(name, l, c, j)
                pe.wait_ge(evacuated[b], held + 1)

            def part(name, l, c, j, out_j, k, token_major=False, cols=P):
                s, b = j % SLOTS, out_j % BANKS
                if k == 0:
                    open_bank(name, l, c, out_j)
                    pe.wait_ge(landed[s], PLAN.landed(name, l, c, j)[1])
                if token_major:
                    for t in range(TB):
                        last = nc.tensor.matmul(dense[:, b, t * P:t * P + cols], hT[:, k, t * P:(t + 1) * P],
                                                ring[:, s, k * P:k * P + cols], start=(k == 0 and t == 0),
                                                stop=True, skip_group_check=True)
                else:
                    last = nc.tensor.matmul(dense[:, b, :], ring[:, s, k * P:(k + 1) * P], hT[:, k, :],
                                            start=(k == 0), stop=(k == KC - 1))
                if k == KC - 1:
                    last.then_inc(dense_done, 1)

            def product(name, l, c, j, token_major=False, cols=P):
                for k in range(KC):
                    part(name, l, c, j, j, k, token_major, cols)

            def gate_parts(name, l, c, first, done, n):
                for m in range(done, done + n):
                    part(name, l, c, first + m // KC, first + m // KC, m % KC)

            def norm_stats(name, l, number, n=SEQ):
                b = open_bank(name, l, 0, 0)
                for k in range(KC):
                    pe.wait_ge(squared, number * KC + (k + 1))
                    last = nc.tensor.matmul(dense[:, b, 0:n], ones[:], probs[:, k % 2, 0:n],
                                            start=(k == 0), stop=(k == KC - 1))
                    last.then_inc(square_used if k < KC - 1 else dense_done, 1)

            def three_passes(b, w_lo, w_hi, x_lo, x_hi, first, final):
                nc.tensor.matmul(dense[:, b, :], w_hi, x_hi, start=first, stop=False)
                nc.tensor.matmul(dense[:, b, :], w_hi, x_lo, start=False, stop=False)
                return nc.tensor.matmul(dense[:, b, :], w_lo, x_hi, start=False, stop=final)

            def up(name, l):
                with pe.Fori(0, FC // 2) as c:
                    for j in range(4):
                        b = open_bank(name, l, c, j)
                        pe.wait_ge(weights_lo, weights_no(name, l, c, j) + 1)
                        for k in range(KC):
                            cols = slice(k * P, (k + 1) * P)
                            if j == 0:
                                pe.wait_ge(h_lo_odd if k % 2 else h_lo_even, l * (KC // 2) + (k // 2 + 1))
                            last = three_passes(b, ring_lo[:, j, cols], ring_hi[:, j % 2, cols], hT_lo[:, k, :],
                                                hT_hi[:, k, :], k == 0, k == KC - 1)
                        last.then_inc(dense_done, 1)

            def down(name, l):
                with pe.Fori(0, 2) as c:
                    for j in range(4):
                        b = open_bank(name, l, c, j)
                        for k in range(FC):
                            item, m = divmod(j * FC + k, KC)
                            if m == 0:
                                pe.wait_ge(weights_lo, weights_no(name, l, c, item) + 1)
                            if j == 0 and k in (0, FC - 2, FC - 1):
                                pe.wait_ge(hidden_lo_ready, l * FC + max(k + 1, FC - 2))
                            cols = slice(m * P, (m + 1) * P)
                            last = three_passes(b, ring_lo[:, item % SLOTS, cols], ring_hi[:, item % HI_SLOTS, cols],
                                                hidden_lo[:, k, :], hidden_hi[:, k, :], k == 0, k == FC - 1)
                            if m == KC - 1 and item < FC // 2 - 1:
                                last.then_inc(weights_used, 1)
                        last.then_inc(dense_done, 1)

            def pre(l):
                pe.wait_ge(s_const, 16)
                pe.wait_ge(masks_ready, l + 1)
                for k in range(KC):
                    pe.wait_ge(h_ready, l * (2 * KC) + (k + 1))
                    part("pre", l, 0, 0, 0, k, token_major=True, cols=TOK_COLS)
                for j in range(1, 5):
                    product("pre", l, 0, j)
                pe.wait_ge(f_dve, l * 3 + 3)
                for h in range(HEADS):
                    if h >= 2:
                        pe.wait_ge(f_copied, l * HEADS + (h - 1))
                    for j in range(TB):
                        last = nc.tensor.matmul(
                            scores[:, h % 2, j * P:SEQ],
                            logf[:, 3, j * HEADS + h:j * HEADS + h + 1].broadcast_to((P, P)),
                            tri[:, 0:SEQ - j * P], start=(j == 0), stop=True, skip_group_check=True)
                    last.then_inc(f_bcast, 1)
                pe.wait_ge(rope_done, rope_no("pre", l, 0, 3) + OPEN)
                for i in range(1, TB):
                    for h in range(IDX_HEADS):
                        u = (i - 1) * IDX_HEADS + h
                        if u < 2:
                            pe.wait_ge(f_copied, (l + 1) * HEADS)
                        else:
                            pe.wait_ge(relu_ready, l * DOTS + (u - 1))
                        half = slice(HEAD_DIM * (h % 2), HEAD_DIM * (h % 2 + 1))
                        n = (i + 1) * P
                        nc.tensor.matmul(scores[:, u % 2, 0:n], qI[half, h // 2, i * P:(i + 1) * P],
                                         kI[half, 0:n], start=True, stop=True).then_inc(dots_ready, 1)

            def attention(name, l, c):
                T = pe.snap(att_turn(name, l, c))
                first_gate = 3 if name == "A" else 1
                keys = {"A": kT, "B": kB, "D": kI}[name]
                values = {"A": vt, "B": tok, "D": qI[:, 0, :].rearrange("p (t n) -> p t n", t=TB)}[name]
                if name == "A":
                    for j in range(3):
                        product("A", l, c, j, token_major=(j == 2))
                    evac_wait("A", l, c, 0)
                    evac_wait("A", l, c, 1)
                    pe.wait_ge(relu_ready, (l + 1) * DOTS)
                else:
                    product(name, l, c, 0)
                done = GATES_FIRST[name]
                gate_parts(name, l, c, first_gate, 0, done)
                if name != "A":
                    pe.wait_ge(rope_done, rope_no(name, l, c) + (OPEN + 1))
                for k in range(STEPS + PV_LAG):
                    if k < STEPS:
                        i, hh = divmod(k, 2)
                        half = slice(HEAD_DIM * hh, HEAD_DIM * (hh + 1))
                        k0, k1 = key_range(name, i)
                        n = k1 - k0
                        if k >= 2:
                            pe.wait_ge(probs_ready, T * STEPS + (k - 1))
                        last = nc.tensor.matmul(scores[:, k % 2, 0:n], qT[half, i * P:(i + 1) * P],
                                                   keys[half, k0:k1], start=True, stop=True)
                        if name != "B":
                            last = nc.tensor.matmul(scores[:, k % 2, n - P:n], ident_16, causal_16, start=False,
                                                       stop=True, skip_group_check=True)
                        if name == "D" and i:
                            last = nc.tensor.matmul(scores[:, k % 2, 0:P], ident_16, before_16, start=False,
                                                       stop=True, skip_group_check=True)
                        last.then_inc(scores_ready, 1)
                    gate_parts(name, l, c, first_gate, done, GATE_STEPS[name][k])
                    done += GATE_STEPS[name][k]
                    s = k - TR_LAG
                    if 0 <= s < STEPS:
                        k0, k1 = key_range(name, s // 2)
                        pe.wait_ge(probs_ready, T * STEPS + (s + 1))
                        if s >= 2:
                            pe.wait_ge(turned_copied, T * STEPS + (s - 1))
                        for m in range((k1 - k0) // P):
                            last = nc.tensor.transpose(turned[:, s % 2, m * P:(m + 1) * P],
                                                       probs[:, s % 2, m * P:(m + 1) * P], ident)
                        last.then_inc(turned_ready, 1)
                    s = k - PV_LAG
                    if 0 <= s < STEPS:
                        i, hh = divmod(s, 2)
                        k0, k1 = key_range(name, i)
                        pe.wait_ge(turned_copied, T * STEPS + (s + 1))
                        if s == 0 and name == "A":
                            evac_wait("A", l, c, 2)
                        if s == 0 and name == "D":
                            evac_wait("Dkv", l, 0, 1)
                        v0 = {"A": HEAD_DIM * hh, "B": 0, "D": HEAD_DIM * hh}[name]
                        for m in range((k1 - k0) // P):
                            last = nc.tensor.matmul(
                                O[:, s * HEAD_DIM:(s + 1) * HEAD_DIM], probsT[:, s % 2, m * P:(m + 1) * P],
                                values[:, k0 // P + m, v0:v0 + HEAD_DIM], start=(m == 0),
                                stop=(m == (k1 - k0) // P - 1))
                        last.then_inc(pv_done, 1)
                gate_parts(name, l, c, first_gate, done, 2 * KC - done)
                pe.wait_ge(y_norm, T + 1)
                pe.wait_ge(y_stored, T + OPEN)
                pe.wait_ge(yc_stored, l * PAIRS + OPEN)
                for t in range(TB):
                    last = nc.tensor.transpose(Yt[:, t * P:(t + 1) * P], Y[:, t * P:(t + 1) * P], ident)
                last.then_inc(y_turned, 1)

            def retention(l, c):
                R = pe.snap(l * PAIRS + c)
                for j in range(4):
                    product("C", l, c, j, token_major=(j == 2))
                pe.wait_ge(rope_done, rope_no("C", l, c, 1) + (OPEN + 1))
                done = 0
                for k in range(STEPS + 1):
                    if k < STEPS:
                        hh, j = divmod(k, TB)
                        half = slice(HEAD_DIM * hh, HEAD_DIM * (hh + 1))
                        if k >= 2:
                            pe.wait_ge(st_decayed, R * STEPS + (k - 1))
                        nc.tensor.matmul(scores[:, k % 2, 0:SEQ - j * P], kT[half, j * P:(j + 1) * P],
                                         qT[half, j * P:SEQ], start=True, stop=True).then_inc(st_ready, 1)
                    gate_parts("C", l, c, 4, done, RET_GATES[k])
                    done += RET_GATES[k]
                    if k:
                        s = k - 1
                        hh, j = divmod(s, TB)
                        pe.wait_ge(st_decayed, R * STEPS + (s + 1))
                        if s == 0:
                            evac_wait("C", l, c, 2)
                        for i in range(j, TB):
                            at = (2 * i + hh) * HEAD_DIM
                            last = nc.tensor.matmul(
                                O[:, at:at + HEAD_DIM], probsT[:, s % 2, (i - j) * P:(i - j + 1) * P],
                                vt[:, j, HEAD_DIM * hh:HEAD_DIM * (hh + 1)], start=(s == 0 and i == 0),
                                stop=True, skip_group_check=True)
                        last.then_inc(rv_done, 1)
                gate_parts("C", l, c, 4, done, 2 * KC - done)
                pe.wait_ge(yc_norm, R + (OPEN + 1))
                pe.wait_ge(y_stored, (l + 1) * (3 * PAIRS) + OPEN)
                pe.wait_ge(yc_stored, R + OPEN)
                for t in range(TB):
                    last = nc.tensor.transpose(Yt[:, t * P:(t + 1) * P], Y[:, t * P:(t + 1) * P], ident)
                last.then_inc(yc_turned, 1)

            pe.wait_ge(s_init, INITS)
            with pe.Fori(0, DEPTH) as l:
                norm_stats("norm1", l, 2 * l)
                pre(l)
                with pe.Fori(0, PAIRS) as c:
                    attention("A", l, c)
                with pe.Fori(0, PAIRS) as c:
                    attention("B", l, c)
                for j in range(2):
                    product("Dkv", l, 0, j, token_major=(j == 1))
                with pe.Fori(0, PAIRS) as c:
                    attention("D", l, c)
                with pe.Fori(0, PAIRS) as c:
                    retention(l, c)
                pe.wait_ge(y_stored, (l + 1) * (3 * PAIRS) + OPEN)
                pe.wait_ge(yc_stored, (l + 1) * PAIRS + OPEN)
                settle(pe)
                pe.wait_ge(cond_step, 3)
                with pe.Fori(0, KC) as d:
                    for n in range(N_BRANCH):
                        b = open_bank("merge", l, d, n)
                        s, count = PLAN.landed("merge", l, d, MERGE_ITEM[n])
                        pe.wait_ge(landed[s], count)
                        for k in range(PAIRS):
                            w = (n % 2) * PAIRS + k
                            last = nc.tensor.matmul(dense[:, b, :], ring[:, s, w * P:(w + 1) * P],
                                                    yT[:, n * PAIRS + k, :], start=(k == 0), stop=(k == PAIRS - 1))
                        last.then_inc(dense_done, 1)
                        if n < ADA_T:
                            s, count = PLAN.landed("merge", l, d, ADA_ITEM[n])
                            at = pe.snap((d * ADA_T + n) * 2)
                            pe.wait_ge(landed[s], count)
                            for k in range(KC):
                                nc.tensor.matmul(Yt[:, bass.ds(at, 2)], ring[:, s, k * P:(k + 1) * P],
                                                 cond[:, 2 * k:2 * k + 2], start=(k == 0), stop=(k == KC - 1))
                pe.wait_ge(merge_add, (l + 1) * (KC * (N_BRANCH - 1)) + OPEN)
                settle(pe)
                with pe.Fori(0, KC // 2) as c:
                    for j in range(2):
                        product("out", l, c, j)
                norm_stats("norm2", l, 2 * l + 1)
                settle(pe)
                up("up", l)
                down("down", l)
            norm_stats("normf", DEPTH, N_F)

            L = DEPTH
            norm_stats("normX", L, N_X, CTX)
            norm_stats("normL", L, N_L)
            pe.wait_ge(h_ready, (N_L + 1) * KC)
            b = open_bank("ab", L, 0, 0)
            pe.wait_ge(landed[0], PLAN.landed("ab", L, 0, 0)[1])
            for t in range(XB):
                for k in range(KC):
                    last = nc.tensor.matmul(dense[:, b, t * 16:(t + 1) * 16], hx[:, k, t * P:(t + 1) * P],
                                            ring[:, 0, k * P:k * P + 16], start=(k == 0), stop=(k == KC - 1))
            last.then_inc(dense_done, 1)
            with pe.Fori(0, 4) as c:
                for u in range(3):
                    for j, (at, n) in enumerate(((0, SEQ), (SEQ, CTX))):
                        b = open_bank("qkv", L, c, 2 * u + j)
                        if j == 0:
                            pe.wait_ge(landed[u], PLAN.landed("qkv", L, c, u)[1])
                        for k in range(KC):
                            last = nc.tensor.matmul(dense[:, b, 0:n], ring[:, u, k * P:(k + 1) * P],
                                                    hx[:, k, at:at + n], start=(k == 0), stop=(k == KC - 1))
                        last.then_inc(dense_done, 1)
            with pe.Fori(0, 4) as c:
                for j in range(2):
                    b = open_bank("uz", L, c, j)
                    pe.wait_ge(landed[j], PLAN.landed("uz", L, c, j)[1])
                    for k in range(KC):
                        last = nc.tensor.matmul(dense[:, b, :], ring[:, j, k * P:(k + 1) * P], hx[:, k, 0:SEQ],
                                                start=(k == 0), stop=(k == KC - 1))
                    last.then_inc(dense_done, 1)
            for cc in range(8):
                pe.wait_ge(l2_squared, cc + 1)
                sq = (probs, probsT)[cc % 2][:].rearrange("p a n -> p (a n)")
                for t in range(XB):
                    last = nc.tensor.matmul(scores[:, 1, cc * XB + t:cc * XB + t + 1], sq[:, t * P:(t + 1) * P],
                                            ones[:, 0:1], start=True, stop=True)
                last.then_inc(l2_used if cc < 7 else l2_sums, 1)
            for r in range(2):
                b = open_bank("four", L, 0, r)
                pe.wait_ge(landed[0], PLAN.landed("four", L, 0, 0)[1])
                nc.tensor.matmul(dense[:, b, :], ring[:, 0, (GH + r) * P:(GH + r + 1) * P], ring[:, 0, 0:SEQ],
                                 start=True, stop=True).then_inc(dense_done, 1)
            evac_wait("uz", L, 3, 0)
            for g in range(4):
                for m in range(2):
                    r = 2 + 3 * g + m
                    b = open_bank("four", L, 0, r)
                    if g == 0:
                        evac_wait("four", L, 0, m)
                    for t in range(TB):
                        last = nc.tensor.matmul(dense[:, b, t * P:(t + 1) * P], uT[:, g, t * P:(t + 1) * P],
                                                (wc, ws)[m][:, g * P:(g + 1) * P], start=True, stop=True)
                    last.then_inc(dense_done, 1)
                b = open_bank("four", L, 0, 4 + 3 * g)
                for m in range(2):
                    evac_wait("four", L, 0, 2 + 3 * g + m)
                    for t in range(TB):
                        s = 1 + 2 * m + t // 2
                        pe.wait_ge(landed[s], PLAN.landed("four", L, 0, s)[1])
                        last = nc.tensor.matmul(dense[:, b, :], (p1, p2)[m][:, t * P:(t + 1) * P],
                                                ring[:, s, (t % 2) * SEQ:(t % 2 + 1) * SEQ],
                                                start=(m == 0 and t == 0), stop=(m == 1 and t == TB - 1))
                last.then_inc(dense_done, 1)
            pe.wait_ge(ab_step, 7)
            sums = scores[:, 0, :]
            half_sc = XB * GH
            for d in range(2):
                nc.tensor.matmul(sums[:, d * half_sc:(d + 1) * half_sc], upto[:, d * P:(d + 1) * P],
                                 gg[:, d * half_sc:(d + 1) * half_sc], start=True, stop=True)
            nc.tensor.matmul(sums[:, SC:2 * SC], chunk_ones, gg[:], start=True, stop=True)
            for c in range(2):
                last = nc.tensor.matmul(sums[:, (2 + c) * SC:(3 + c) * SC],
                                        chunk_ones[:, c * (P - 1):c * (P - 1) + 1].broadcast_to((P, P)), gg[:],
                                        start=True, stop=True)
            last.then_inc(ab_sums, 1)
            pe.wait_ge(l2_var, 1)
            pe.wait_ge(ab_act, 6)
            pe.wait_ge(ab_step, 10)
            pe.wait_ge(mod_step, DEPTH)
            for t in range(XB):
                if t >= 2:
                    pe.wait_ge(v_stored, t - 1)
                for h in range(GH):
                    last = nc.tensor.transpose(bankB[t % 2][:, h * P:(h + 1) * P], cv[:, 8 + h, t * P:(t + 1) * P],
                                               ident)
                last.then_inc(v_turned, 1)
            for t in range(XB + 1):
                if t < XB:
                    if t >= 2:
                        pe.wait_ge(k_scaled, t - 1)
                    for h in range(GH):
                        last = nc.tensor.transpose(bankA[t % 2][:, h * P:(h + 1) * P],
                                                   cv[:, 4 + h, t * P:(t + 1) * P], ident)
                    last.then_inc(k_turned, 1)
                if t >= 1:
                    pe.wait_ge(k_scaled, t)
                    if t >= 3:
                        pe.wait_ge(kh_stored, t - 2)
                    for h in range(GH):
                        last = nc.tensor.transpose(bankC[(t - 1) % 2][:, h * P:(h + 1) * P],
                                                   ktok[:, t - 1, h * P:(h + 1) * P], ident)
                    last.then_inc(kh_turned, 1)
            pe.wait_ge(kh_stored, XB)
            pe.wait_ge(v_stored, XB)

            def unit(n):
                isl = n >= FIRST_L
                both = [(d, ORDER[d][n]) for d in range(2)]
                hcol = [slice(h * P, (h + 1) * P) for h in range(GH)]
                for d, b in both:
                    if n:
                        pe.wait_ge(c_s[d], 2 * n)
                    for h in range(GH):
                        at = (d * XB + b) * GH + h
                        last = nc.tensor.matmul(bankA[d][:, hcol[h]], gg[:, at:at + 1].broadcast_to((P, P)),
                                                upto[:, d * P:(d + 1) * P], start=True, stop=True)
                    last.then_inc(u_row[d], 1)
                for d, b in both:
                    if n > FIRST_L:
                        pe.wait_ge(c_o2[d], seen(n))
                    for h in range(GH):
                        last = nc.tensor.matmul(bankB[d][:, hcol[h]], cv[:, 4 + h, b * P:(b + 1) * P],
                                                khT[:, b, hcol[h]], start=True, stop=True)
                    last.then_inc(u_kk[d], 1)
                if isl:
                    for d, b in both:
                        if n > FIRST_L:
                            pe.wait_ge(c_o1[d], seen(n))
                        for h in range(GH):
                            last = nc.tensor.matmul(bankC[d][:, hcol[h]], cv[:, h, b * P:(b + 1) * P],
                                                    khT[:, b, hcol[h]], start=True, stop=True)
                        last.then_inc(u_qk[d], 1)
                    for d, b in both:
                        pe.wait_ge(u_x[d], n - FIRST_L + 1)
                        for h in range(GH):
                            last = nc.tensor.transpose(bankC[d][:, hcol[h]], W2["X"][d][:, hcol[h]], ident)
                        last.then_inc(u_xt[d], 1)
                for d, b in both:
                    pe.wait_ge(u_t[d], n + 1)
                    for h in range(GH):
                        last = nc.tensor.transpose(bankB[d][:, hcol[h]], W2["T"][d][:, hcol[h]], ident)
                    last.then_inc(u_tt[d], 1)
                for lev in range(1, LEVELS):
                    step = n * (LEVELS - 1) + lev
                    for d, b in both:
                        pe.wait_ge(u_as[d], step)
                        if lev == 1:
                            pe.wait_ge(u_ttc[d], n + 1)
                        else:
                            pe.wait_ge(u_lvl[d], step - 1)
                        for h in range(GH):
                            last = nc.tensor.matmul(bankB[d][:, hcol[h]], W2["A_level"][d][:, hcol[h]],
                                                    W2["TT"][d][:, hcol[h]], start=True, stop=True)
                        last.then_inc(u_z[d], 1)
                    for d, b in both:
                        pe.wait_ge(u_zc[d], step)
                        if lev == 1 and isl:
                            pe.wait_ge(u_attn[d], n - FIRST_L + 1)
                        for h in range(GH):
                            if lev < LEVELS - 1:
                                nc.tensor.matmul(bankA[d][:, hcol[h]], W2["Z"][d][:, hcol[h]],
                                                 W2["T"][d][:, hcol[h]], start=True, stop=True)
                            last = nc.tensor.matmul(bankC[d][:, hcol[h]], W2["T"][d][:, hcol[h]],
                                                    W2["Z"][d][:, hcol[h]], start=True, stop=True)
                        last.then_inc(u_upd[d], 1)
                for d, b in both:
                    pe.wait_ge(u_lvl[d], (n + 1) * (LEVELS - 1))
                    pe.wait_ge(u_kv[d], 3 * n + 3)
                    for h in range(GH):
                        nc.tensor.matmul(bankA[d][:, hcol[h]], W2["decay"][d][:, hcol[h]], W2["TT"][d][:, hcol[h]],
                                         start=True, stop=True)
                        last = nc.tensor.matmul(bankC[d][:, hcol[h]], W2["TT"][d][:, hcol[h]],
                                                W2["X"][d][:, hcol[h]], start=True, stop=True)
                    last.then_inc(u_wu[d], 1)

            def scan(n):
                isl = n >= FIRST_L
                for i in range(2):
                    for d in range(2):
                        b = ORDER[d][n]
                        c, hs = chunk_of(d, i)
                        if i == 0:
                            pe.wait_ge(u_w[d], n + 1)
                            pe.wait_ge(u_u[d], n + 1)
                        if n or i:
                            pe.wait_ge(c_s[d], 2 * n + i)
                        else:
                            pe.wait_ge(ab_step, 14)
                        if isl and i:
                            pe.wait_ge(c_o2[d], seen(n, 0))
                        for h in range(GH):
                            hc = slice(h * P, (h + 1) * P)
                            last = nc.tensor.matmul(bankB[d][hs, hc], W2["wT"][d][:, h * P + CHUNK * c:h * P + CHUNK * (c + 1)],
                                                    state[d][:, hc], start=True, stop=True)
                            if isl:
                                last = nc.tensor.matmul(bankC[d][hs, hc], cv[:, h, b * P + CHUNK * c:b * P + CHUNK * (c + 1)],
                                                        state[d][:, hc], start=True, stop=True)
                        last.then_inc(c_ws[d], 1)
                    for d in range(2):
                        c, hs = chunk_of(d, i)
                        pe.wait_ge(c_v[d], 2 * n + i + 1)
                        for h in range(GH):
                            hc = slice(h * P, (h + 1) * P)
                            last = nc.tensor.matmul(bankA[d][:, hc], W2["kd"][d][hs, hc], W2["vnew"][d][hs, hc],
                                                    start=True, stop=True)
                        last.then_inc(c_sd[d], 1)
                        if isl:
                            for h in range(GH):
                                hc = slice(h * P, (h + 1) * P)
                                last = nc.tensor.matmul(
                                    bankB[d][hs, hc], W2["attnT"][d][hs, h * P + CHUNK * c:h * P + CHUNK * (c + 1)],
                                    W2["vnew"][d][hs, hc], start=True, stop=True)
                            last.then_inc(c_oi[d], 1)

            for n in range(UNITS):
                unit(n)
                scan(n)
            for t in range(TB):
                pe.wait_ge(p_dve, P_MEANS + t + 1)
                for h in range(GH):
                    last = nc.tensor.transpose((bankA + bankB)[t][:, h * P:(h + 1) * P], o2[t][:, h * P:(h + 1) * P],
                                               ident)
                last.then_inc(p_turned, 1)
            pe.wait_ge(p_dve, P_GATED)
            evac_wait("four", L, 0, 13)
            settle(pe)
            with pe.Fori(0, KC // 2) as c:
                for j in range(2):
                    b = open_bank("out2", L, c, j)
                    pe.wait_ge(landed[j], PLAN.landed("out2", L, c, j)[1])
                    for k in range(KC):
                        last = nc.tensor.matmul(dense[:, b, :], ring[:, j, k * P:(k + 1) * P], yT[:, k, :],
                                                start=(k == 0), stop=(k == KC - 1))
                    last.then_inc(dense_done, 1)
            norm_stats("norm3", L, N_3)
            norm_stats("norm4", L, N_4)
            up("up2", L)
            down("down2", L)
            norm_stats("norm5", L, N_5)

        @block.scalar
        def _(act):
            def result_in(name, l, c, j):
                act.wait_ge(dense_done, PLAN.done(name, l, c, j))
                b, held = PLAN.bank(name, l, c, j)
                return b, held

            def norm(name, l, number, src=xT, n=SEQ):
                for b in range(BANKS):
                    act.wait_ge(evacuated[b], held_before(name, l, b))
                for k in range(KC):
                    if k >= 2:
                        act.wait_ge(square_used, number * (KC - 1) + (k - 1))
                    nc.scalar.activation(probs[:, k % 2, 0:n], src[:, k, 0:n], ACT.Square).then_inc(squared, 1)
                act.wait_ge(evacuated[0], held_before(name, l, 0) + 1)
                nc.scalar.activation(gC[:, 0:n], Y[:, 0:n], ACT.Sqrt).then_inc(norm_root, 1)

            def swap(name, l, c, j, r):
                b, _ = result_in(name, l, c, j)
                act.wait_ge(swap_mul, r + OPEN)
                for q in range(4):
                    last = nc.scalar.activation(swapped[32 * q:32 * q + 32, :],
                                                dense[32 * (q ^ 1):32 * (q ^ 1) + 32, b, :], ACT.Copy)
                last.then_inc(swap_ready, 1)

            def copy(name, l, c, j, dst, scale=1.0, cols=P, blocks=TB):
                b, _ = result_in(name, l, c, j)
                src = dense[:, b, :]
                if name == "ab":
                    src = dense[:, b, 0:blocks * cols].rearrange("p (t n) -> p t n", t=blocks)
                elif cols < P:
                    src = src.rearrange("p (t n) -> p t n", t=TB)[:, :, 0:cols]
                nc.scalar.activation(dst, src, ACT.Copy, scale=scale).then_inc(evacuated[b], 1)

            def gate(name, l, c, j, g):
                at = act.snap(gate_index(name, c) + g)
                b, _ = result_in(name, l, c, j)
                settle(act)
                nc.scalar.activation(gates[:, bass.ds(at, 1), :], dense[:, b:b + 1, :], ACT.Tanh,
                                     scale=0.5).then_inc(evacuated[b], 1)

            def pre(l):
                copy("pre", l, 0, 0, tok[:, :, 0:TOK_COLS], cols=TOK_COLS)
                swap("pre", l, 0, 1, rope_no("pre", l, 0, 0))
                act.wait_ge(f_dve, l * 3 + 2)
                nc.scalar.activation(logf[:, 2, :], logf[:, 1, :], ACT.Exp, scale=-1.0).then_inc(f_act, 1)
                act.wait_ge(f_act, l * 2 + 1)
                nc.scalar.activation(logf[:, 2, :], logf[:, 2, :], ACT.Ln, bias=1.0).then_inc(f_act, 1)
                for j in range(2, 5):
                    swap("pre", l, 0, j, rope_no("pre", l, 0, j - 1))
                for h in range(HEADS):
                    act.wait_ge(f_bcast, l * HEADS + (h + 1))
                    nc.scalar.activation(negF[:, NEGF + h, :], scores[:, h % 2, :], ACT.Copy,
                                         scale=-1.0).then_inc(f_copied, 1)
                for i in range(1, TB):
                    for h in range(IDX_HEADS):
                        u = (i - 1) * IDX_HEADS + h
                        n = (i + 1) * P
                        act.wait_ge(dots_ready, l * DOTS + (u + 1))
                        if u >= 2:
                            act.wait_ge(score_step, l * DOTS + (u - 1))
                        nc.scalar.activation(probs[:, u % 2, 0:n], scores[:, u % 2, 0:n], ACT.Relu,
                                             scale=IDX_SCALE).then_inc(relu_ready, 1)

            def attention(name, l, c):
                T = act.snap(att_turn(name, l, c))
                if name == "A":
                    copy("A", l, c, 0, qT[:], scale=QK_SCALE)
                    copy("A", l, c, 1, kT[:])
                    copy("A", l, c, 2, vt[:].rearrange("p t n -> p (t n)"))
                else:
                    swap(name, l, c, 0, rope_no(name, l, c))
                first_gate = 3 if name == "A" else 1
                if GATE0_AT[name] < 0:
                    gate(name, l, c, first_gate, 0)
                for k in range(STEPS + TR_LAG):
                    if k < STEPS:
                        k0, k1 = key_range(name, k // 2)
                        n = k1 - k0
                        act.wait_ge(negmax_ready, T * STEPS + (k + 1))
                        src = probs[:, k % 2, 0:n]
                        if name == "D":
                            h = act.snap(l * HEADS + c + (k % 2) * PAIRS)
                            settle(act)
                            nc.scalar.activation(sink_exp[:, k:k + 1], small[:, bass.ds(h + SMALL["sinks"], 1)],
                                                 ACT.Exp, bias=neg_max[:, k:k + 1])
                            src = scores[:, k % 2, 0:n]
                        nc.scalar.activation(probs[:, k % 2, 0:n], src, ACT.Exp, bias=neg_max[:, k:k + 1],
                                             scale=softmax_scores(name),
                                             accum_out=row_sum[:, k:k + 1]).then_inc(probs_ready, 1)
                    s = k - TR_LAG
                    if s >= 0:
                        k0, k1 = key_range(name, s // 2)
                        act.wait_ge(turned_ready, T * STEPS + (s + 1))
                        if s >= 2:
                            act.wait_ge(pv_done, T * STEPS + (s - 1))
                        nc.scalar.activation(probsT[:, s % 2, 0:k1 - k0], turned[:, s % 2, 0:k1 - k0],
                                             ACT.Copy).then_inc(turned_copied, 1)
                    if k == GATE0_AT[name]:
                        gate(name, l, c, first_gate, 0)
                gate(name, l, c, first_gate + 1, 1)
                at = act.snap(PAIRS * BRANCH[name] + c)
                act.wait_ge(y_turned, T + 1)
                settle(act)
                nc.scalar.activation(yT[:, bass.ds(at, 1), :], Yt[:].rearrange("p (a n) -> p a n", a=1),
                                     ACT.Copy).then_inc(y_stored, 1)

            def retention(l, c):
                R = act.snap(l * PAIRS + c)
                swap("C", l, c, 0, rope_no("C", l, c, 0))
                swap("C", l, c, 1, rope_no("C", l, c, 1))
                copy("C", l, c, 2, vt[:].rearrange("p t n -> p (t n)"))
                b, _ = result_in("C", l, c, 3)
                act.wait_ge(yc_stored, R + OPEN)
                nc.scalar.activation(gC[:], dense[:, b, :], ACT.Tanh, scale=0.5).then_inc(gc_tanh, 1)
                for g in range(2):
                    gate("C", l, c, 4 + g, g)

            act.wait_ge(s_x, 16)
            act.wait_ge(s_small, 16)
            nc.scalar.activation(cond_tanh[:], small[:, SMALL["cond"]:SMALL["cond"] + 2 * KC], ACT.Tanh, scale=0.5
                                 ).then_inc(cond_step, 1)
            with act.Fori(0, DEPTH) as l:
                norm("norm1", l, 2 * l)
                pre(l)
                with act.Fori(0, PAIRS) as c:
                    attention("A", l, c)
                with act.Fori(0, PAIRS) as c:
                    attention("B", l, c)
                swap("Dkv", l, 0, 0, rope_no("Dkv", l, 0))
                copy("Dkv", l, 0, 1, qI[:, 0, :])
                with act.Fori(0, PAIRS) as c:
                    attention("D", l, c)
                with act.Fori(0, PAIRS) as c:
                    retention(l, c)
                norm("norm2", l, 2 * l + 1)
                with act.Fori(0, FC // 2) as c:
                    for half in range(2):
                        F = act.snap(l * FC + c * 2 + half)
                        act.wait_ge(hidden_ready, F + (HIDDEN_OPEN - 1))
                        for j in range(2):
                            b, _ = result_in("up", l, c, 2 * half + j)
                            at = act.snap((l * (2 * FC) + c * 2 + (half + j * FC)) * 4 + SMALL["conv"])
                            settle(act)
                            nc.scalar.activation((side_a, side_b)[j][half], dense[:, b, :], ACT.Identity,
                                                 scale=small[:, bass.ds(at + 2, 1)],
                                                 bias=small[:, bass.ds(at + 3, 1)]).then_inc(taps, 1)
                        _, held = PLAN.bank("up", l, c, 2 * half)
                        act.wait_ge(evacuated[0], held + 1)
                        act.wait_ge(up_gate, F + OPEN)
                        nc.scalar.activation(probsT[:, 0, :], side_a[half], ACT.Tanh, scale=0.5
                                             ).then_inc(up_tanh, 1)
            norm("normf", DEPTH, N_F)

            L = DEPTH
            act.wait_ge(s_io, 16)
            norm("normX", L, N_X, xc, CTX)
            act.wait_ge(h_ready, (N_F + 1) * KC)
            norm("normL", L, N_L)
            copy("ab", L, 0, 0, abt[:].rearrange("p (t n) -> p t n", t=XB), cols=16, blocks=XB)
            with act.Fori(0, 4) as c3:
                for third in range(3):
                    c = act.snap(c3 * 3 + third)
                    act.wait_ge(cq_done, c + OPEN)
                    at = act.snap(c * 3 + SMALL["qkv_conv"])
                    for j, (lo, n) in enumerate(((0, SEQ), (SEQ, CTX))):
                        b, _ = result_in("qkv", L, c3, 2 * third + j)
                        settle(act)
                        nc.scalar.activation(cv[:, bass.ds(c, 1), lo:lo + n], dense[:, b:b + 1, 0:n], ACT.Identity,
                                             scale=small[:, bass.ds(at + 1, 1)]).then_inc(cq_taps, 1)
                    for j in range(2):
                        act.wait_ge(evacuated[j], PLAN.bank("qkv", L, c3, 2 * third + j)[1] + 1)
                    settle(act)
                    tanh = probsT[:].rearrange("p a n -> p (a n)")[:, 0:XB * P].rearrange("p (a n) -> p a n", a=1)
                    nc.scalar.activation(tanh, cv[:, bass.ds(c, 1), :], ACT.Tanh, scale=0.5).then_inc(cq_tanh, 1)
            with act.Fori(0, 4) as c:
                b, _ = result_in("uz", L, c, 0)
                settle(act)
                nc.scalar.activation(yT[:, bass.ds(c, 1), :], dense[:, b:b + 1, :], ACT.Copy).then_inc(evacuated[b], 1)
                act.wait_ge(z_done, c + OPEN)
                b, _ = result_in("uz", L, c, 1)
                nc.scalar.activation(gC[:], dense[:, b, :], ACT.Tanh, scale=0.5).then_inc(z_tanh, 1)
            act.wait_ge(ab_step, 3)
            nc.scalar.activation(tmp_sc[:, SC:2 * SC], tmp_sc[:, 0:SC], ACT.Exp, scale=-1.0).then_inc(ab_act, 1)
            act.wait_ge(ab_act, 1)
            nc.scalar.activation(tmp_sc[:, SC:2 * SC], tmp_sc[:, SC:2 * SC], ACT.Ln, bias=1.0).then_inc(ab_act, 1)
            nc.scalar.activation(decay_rate[:], small[:, SMALL["a_log"]:SMALL["a_log"] + 2 * GH], ACT.Exp
                                 ).then_inc(ab_act, 1)
            ab = abt[:].rearrange("p (t g h) -> p t g h", t=XB, h=GH)
            for d in range(2):
                nc.scalar.activation(sc3(beta, d), ab[:, :, d, :], ACT.Tanh, scale=0.5).then_inc(ab_act, 1)
            for cc in range(8):
                if cc >= 2:
                    act.wait_ge(l2_used, cc - 1)
                sq = (probs, probsT)[cc % 2][:].rearrange("p a n -> p (a n)")
                nc.scalar.activation(sq[:, 0:XB * P], cv[:, cc, :], ACT.Square).then_inc(l2_squared, 1)
            for r in range(2):
                b, _ = result_in("four", L, 0, r)
                nc.scalar.activation((wc, ws)[r], dense[:, b, :], ACT.Copy, scale=FFT_SCALE).then_inc(evacuated[b], 1)
            for g in range(4):
                copy("four", L, 0, 2 + 3 * g, p1)
                copy("four", L, 0, 3 + 3 * g, p2)
                copy("four", L, 0, 4 + 3 * g, yT[:, g, :])
            act.wait_ge(ab_sums, 1)
            nc.scalar.activation(gcum[:], scores[:, 0, 0:SC], ACT.Copy)
            nc.scalar.activation(egc[:], scores[:, 0, 0:SC], ACT.Exp)
            nc.scalar.activation(etot[:], scores[:, 0, 2 * SC:4 * SC], ACT.Exp).then_inc(ab_act, 1)
            act.wait_ge(ab_step, 10)
            nc.scalar.activation(ed[:], tmp_sc[:, 0:SC], ACT.Exp).then_inc(ab_act, 1)
            for t in range(XB):
                act.wait_ge(v_turned, t + 1)
                nc.scalar.activation(vtok[:, t, :], bankB[t % 2], ACT.Copy).then_inc(v_stored, 1)
            for t in range(XB):
                act.wait_ge(kh_turned, t + 1)
                nc.scalar.activation(khT[:, t, :], bankC[t % 2], ACT.Copy).then_inc(kh_stored, 1)
            for n in range(UNITS):
                isl = n >= FIRST_L
                for d in range(2):
                    act.wait_ge(u_diff[d], n + 1)
                    nc.scalar.activation(W2["decay"][d], W2["decay"][d], ACT.Exp, scale=-1.0).then_inc(u_decay[d], 1)
                if isl:
                    for d in range(2):
                        act.wait_ge(u_xt[d], n - FIRST_L + 1)
                        nc.scalar.activation(W2["attnT"][d], bankC[d], ACT.Copy).then_inc(u_attn[d], 1)
                for d in range(2):
                    act.wait_ge(u_tt[d], n + 1)
                    nc.scalar.activation(W2["TT"][d], bankB[d], ACT.Copy).then_inc(u_ttc[d], 1)
                for lev in range(1, LEVELS):
                    for d in range(2):
                        act.wait_ge(u_z[d], n * (LEVELS - 1) + lev)
                        nc.scalar.activation(W2["Z"][d], bankB[d], ACT.Copy).then_inc(u_zc[d], 1)
                for d in range(2):
                    act.wait_ge(u_wu[d], n + 1)
                    nc.scalar.activation(W2["wT"][d], bankA[d], ACT.Copy).then_inc(u_w[d], 1)
            for t in range(TB):
                d = int(t < 2)
                act.wait_ge(c_o3[d], 4)
                nc.scalar.activation(SQ4[t], o2[t], ACT.Square).then_inc(p_sq, 1)
            with act.Fori(0, KC // 2) as c:
                for j in range(2):
                    at = act.snap(c * 2 + j)
                    b, _ = result_in("out2", L, c, j)
                    settle(act)
                    nc.scalar.activation(hT[:, bass.ds(at, 1), :], dense[:, b:b + 1, :], ACT.Copy
                                         ).then_inc(evacuated[b], 1)
            norm("norm3", L, N_3, hT)
            act.wait_ge(x_added, KC)
            norm("norm4", L, N_4)

            def up_split(c, j):
                slot, count = PLAN.landed("up2", L, c + j // 2, (j + 2) % 4)
                act.wait_ge(landed[slot], count)
                nc.scalar.activation(ring_hi[:, j % 2, :], ring[:, slot, :], ACT.Copy).then_inc(weights_hi, 1)

            with act.Fori(0, FC // 2) as c:
                for half in range(2):
                    f = act.snap(c * 2 + half)
                    act.wait_ge(hidden_ready, f + (DEPTH * FC + HIDDEN_OPEN - 1))
                    b, _ = result_in("up2", L, c, 2 * half)
                    nc.scalar.activation(side_a[half], dense[:, b, :], ACT.Copy).then_inc(evacuated[b], 1)
                    up_split(c, 2 * half)
                    at = act.snap(f * 9 + SMALL["dwc"])
                    b, held = result_in("up2", L, c, 2 * half + 1)
                    settle(act)
                    nc.scalar.activation(side_b[half], dense[:, b, :], ACT.Identity,
                                         scale=small[:, bass.ds(at + 4, 1)]).then_inc(taps, 1)
                    nc.scalar.activation(grid_in[half], dense[:, b, :], ACT.Copy).then_inc(evacuated[b], 1)
                    up_split(c, 2 * half + 1)
                    act.wait_ge(conv_step, f * 8 + (2 * DEPTH * FC + 8))
                    act.wait_ge(up_gate, f + (DEPTH * FC + OPEN))
                    nc.scalar.activation(probsT[:, 0, :], side_b[half], ACT.Tanh, scale=0.5).then_inc(up_tanh, 1)
            with act.Fori(0, 2) as c:
                for j in range(4):
                    at = act.snap(c * 4 + j)
                    b, _ = result_in("down2", L, c, j)
                    settle(act)
                    nc.scalar.activation(hT[:, bass.ds(at, 1), :], dense[:, b:b + 1, :], ACT.Copy, scale=0.5
                                         ).then_inc(evacuated[b], 1)
            norm("norm5", L, N_5, hT)

        @block.vector
        def _(dve):
            def result_in(name, l, c, j):
                dve.wait_ge(dense_done, PLAN.done(name, l, c, j))
                return PLAN.bank(name, l, c, j)

            def norm(name, l, number, gain, dst, src=xT, n=SEQ, sem=h_ready):
                b, held = result_in(name, l, 0, 0)
                nc.vector.tensor_scalar(Y[:, 0:n], dense[:, b, 0:n], 1.0 / D_MODEL, EPS, ALU.mult, ALU.add
                                        ).then_inc(evacuated[b], 1)
                dve.wait_ge(norm_root, number + 1)
                nc.vector.reciprocal(Y[:, 0:n], gC[:, 0:n]).then_inc(norm_inv, 1)
                dve.wait_ge(norm_inv, number + 1)
                for k in range(KC):
                    nc.vector.scalar_tensor_tensor(out=dst[:, k, 0:n], in0=src[:, k, 0:n], scalar=gain(k),
                                                   in1=Y[:, 0:n], op0=ALU.mult, op1=ALU.mult).then_inc(sem, 1)

            def split_weights(name, l, c, j):
                slot, count = PLAN.landed(name, l, c, j)
                hi = j % (2 if name.startswith("up") else HI_SLOTS)
                dve.wait_ge(landed[slot], count)
                nc.vector.tensor_copy(ring_hi[:, hi, :], ring[:, slot, :]).then_inc(weights_hi, 1)

            def split_h(l, ready):
                for k in range(KC + 1):
                    if k < KC:
                        dve.wait_ge(h_ready, ready + (k + 1))
                        nc.vector.tensor_copy(hT_hi[:, k, :], hT[:, k, :]).then_inc(h_hi, 1)
                    if k % 2:
                        dve.wait_ge(h_hi, l * KC + k)
                        nc.vector.tensor_tensor(hT_lo[:, k - 1, :], hT[:, k - 1, :], hT_hi[:, k - 1, :],
                                                ALU.subtract).then_inc(h_lo_even, 1)

            def up_split(name, l, c, j):
                split_weights(name, l, c + j // 2, (j + 2) % 4)

            def store_hidden(l, c, half, other):
                f = dve.snap(c * 2 + half)
                done = dve.snap(l * FC + c * 2 + (half + 1))
                here = bass.ds(f, 1)
                dve.wait_ge(up_gate, done + OPEN)
                nc.vector.tensor_tensor(hidden[:, here, :], probsT[:, 1:2, :], other[half].rearrange("p (a n) -> p a n", a=1),
                                        ALU.mult).then_inc(hidden_ready, 1)
                dve.wait_ge(hidden_ready, done + HIDDEN_OPEN)
                nc.vector.tensor_copy(hidden_hi[:, here, :], hidden[:, here, :]).then_inc(hidden_hi_ready, 1)
                dve.wait_ge(hidden_hi_ready, done)
                nc.vector.tensor_tensor(hidden_lo[:, here, :], hidden[:, here, :], hidden_hi[:, here, :], ALU.subtract
                                        ).then_inc(hidden_lo_ready, 1)

            def down_steps(name, l, evacuate):
                used = l * (2 * (FC // 2 - 1)) + OPEN
                for c in range(2):
                    steps = [(KC * (j - 3) + KC - 1, 0, c, j) for j in range(2, FC // 2)]
                    if c == 0:
                        steps += [(KC * (j + 8) + KC - 1, 0, 1, j) for j in range(2)]
                    steps += [(FC * (j + 1) - 1, 1, c, j) for j in range(4)]
                    for _, is_result, cc, j in sorted(steps):
                        if is_result:
                            evacuate(cc, j)
                            continue
                        if cc == 1 and j == 1:
                            dve.wait_ge(dense_done, PLAN.done(name, l, 0, 3))
                        elif cc or j > 2:
                            dve.wait_ge(weights_used, used + (cc * (FC // 2 - 1) + j - (2 if j > 2 else j // 2)))
                        split_weights(name, l, cc, j)

            def rope(name, l, c, j, r, dst):
                b, held = result_in(name, l, c, j)
                dve.wait_ge(swap_ready, r + 1)
                nc.vector.tensor_tensor(dst, dense[:, b, :], cos, ALU.mult).then_inc(evacuated[b], 1)
                dve.wait_ge(evacuated[b], held + 1)
                dve.wait_ge(swap_mul, r + (OPEN + 1))
                nc.vector.tensor_tensor(dst, dst, swapped_sin[:], ALU.add).then_inc(rope_done, 1)

            def pre(l):
                b, held = PLAN.bank("pre", l, 0, 0)
                dve.wait_ge(evacuated[b], held + 1)
                z = logf[:, 0, :].rearrange("p (t h) -> p t h", t=TB)
                at = dve.snap(l * HEADS + SMALL["forget_bias"])
                bias = small[:, bass.ds(at, HEADS)].unsqueeze(1).broadcast_to((P, TB, HEADS))
                nc.vector.tensor_tensor(z, tok[:, :, HEAD_DIM:HEAD_DIM + HEADS], bias, ALU.add).then_inc(f_dve, 1)
                dve.wait_ge(f_dve, l * 3 + 1)
                nc.vector.scalar_tensor_tensor(out=logf[:, 1, :], in0=logf[:, 0, :], scalar=-1.0,
                                               in1=logf[:, 0, :], op0=ALU.mult, op1=ALU.max).then_inc(f_dve, 1)
                rope("pre", l, 0, 1, rope_no("pre", l, 0, 0), kI[:])
                dve.wait_ge(f_act, l * 2 + 2)
                nc.vector.scalar_tensor_tensor(out=logf[:, 3, :], in0=logf[:, 0, :], scalar=0.0,
                                               in1=logf[:, 2, :], op0=ALU.min, op1=ALU.subtract).then_inc(f_dve, 1)
                rope("pre", l, 0, 2, rope_no("pre", l, 0, 1), qI[:, 0, :])
                rope("pre", l, 0, 3, rope_no("pre", l, 0, 2), qI[:, 1, :])
                rope("pre", l, 0, 4, rope_no("pre", l, 0, 3), kB[:])
                for i in range(1, TB):
                    for h in range(IDX_HEADS):
                        u = (i - 1) * IDX_HEADS + h
                        n = (i + 1) * P
                        dst = sel[:, SEL + i, 0:n]
                        w = tok[:, i, HEAD_DIM + HEADS + h:HEAD_DIM + HEADS + h + 1]
                        dve.wait_ge(relu_ready, l * DOTS + (u + 1))
                        if h == 0:
                            nc.vector.tensor_scalar(dst, probs[:, u % 2, 0:n], w, None, ALU.mult
                                                    ).then_inc(score_step, 1)
                        else:
                            dve.wait_ge(score_step, l * DOTS + u)
                            nc.vector.scalar_tensor_tensor(out=dst, in0=probs[:, u % 2, 0:n], scalar=w, in1=dst,
                                                           op0=ALU.mult, op1=ALU.add).then_inc(score_step, 1)
                step = 0
                base = dve.snap(l * TOPK_STEPS)
                dve.wait_ge(score_step, (l + 1) * DOTS)
                nc.vector.tensor_copy(sel[:, SEL, 0:P], causal).then_inc(topk_step, 1)
                step += 1
                for i in range(1, TB):
                    diag = sel[:, SEL + i, i * P:(i + 1) * P]
                    nc.vector.tensor_tensor(diag, diag, causal, ALU.add).then_inc(topk_step, 1)
                    step += 1
                dve.wait_ge(f_copied, (l + 1) * HEADS)
                settle(dve)

            def topk_part(l, c, s):
                for i in range(1, TB):
                    work = sel[:, SEL + i, 0:(i + 1) * P]
                    dve.wait_ge(topk_step, l * TOPK_STEPS + c * (STEPS * (TB - 1)) + (TB + s * (TB - 1) + i - (TB - 1)))
                    settle(dve)
                    if s % 2 == 0:
                        nc.vector.max(top8[:, i, :], work).then_inc(topk_step, 1)
                    else:
                        nc.vector.match_replace(out=work, in_to_replace=top8[:, i, :], in_values=work,
                                                imm_value=TAKEN).then_inc(topk_step, 1)

            def topk_mask(l):
                dve.wait_ge(topk_step, (l + 1) * TOPK_STEPS - (TB - 1))
                for i in range(1, TB):
                    work = sel[:, SEL + i, 0:(i + 1) * P]
                    nc.vector.tensor_scalar(work, work, TAKEN / 2, NEG, ALU.is_gt, ALU.mult).then_inc(topk_step, 1)
                dve.wait_ge(topk_step, (l + 1) * TOPK_STEPS)
                settle(dve)

            def attention(name, l, c):
                T = dve.snap(att_turn(name, l, c))
                if name != "A":
                    rope(name, l, c, 0, rope_no(name, l, c), qT[:])
                for s in range(STEPS):
                    i, hh = divmod(s, 2)
                    k0, k1 = key_range(name, i)
                    n = k1 - k0
                    dve.wait_ge(scores_ready, T * STEPS + (s + 1))
                    if s >= 2:
                        dve.wait_ge(turned_ready, T * STEPS + (s - 1))
                    mx = row_max[:, s:s + 1]
                    if name == "D":
                        nc.vector.tensor_reduce(mx, scores[:, s % 2, 0:n], AX_X, ALU.max).then_inc(logits_ready, 1)
                    elif name == "B":
                        settle(dve)
                        nc.vector.tensor_tensor_reduce(
                            probs[:, s % 2, 0:n], scores[:, s % 2, 0:n], sel[:, SEL + i, 0:n], QK_SCALE, TAKEN,
                            ALU.add, ALU.max, mx).then_inc(logits_ready, 1)
                    else:
                        at = dve.snap(c * 2 + (NEGF + hh))
                        nc.vector.tensor_tensor(probs[:, s % 2:s % 2 + 1, 0:n], scores[:, s % 2:s % 2 + 1, 0:n],
                                                negF[:, bass.ds(at, 1), 0:n], ALU.add).then_inc(biased, 1)
                        dve.wait_ge(biased, (l * PAIRS + c) * STEPS + (s + 1))
                        nc.vector.tensor_reduce(mx, probs[:, s % 2, 0:n], AX_X, ALU.max).then_inc(logits_ready, 1)
                    dve.wait_ge(logits_ready, T * STEPS + (s + 1))
                    if name == "D":
                        h = dve.snap(l * HEADS + c + hh * PAIRS)
                        nc.vector.tensor_scalar(neg_max[:, s:s + 1], mx, -QK_SCALE, neg_sink[:, bass.ds(h, 1)],
                                                ALU.mult, ALU.min).then_inc(negmax_ready, 1)
                    else:
                        nc.vector.tensor_scalar(neg_max[:, s:s + 1], mx, -1.0, None, ALU.mult
                                                ).then_inc(negmax_ready, 1)
                    if name == "A":
                        topk_part(l, c, s)
                dve.wait_ge(pv_done, T * STEPS + STEPS)
                if name == "D":
                    nc.vector.tensor_tensor(row_sum[:], row_sum[:], sink_exp[:], ALU.add).then_inc(y_sum, 1)
                    dve.wait_ge(y_sum, l * PAIRS + c + 1)
                nc.vector.reciprocal(inv_sum[:], row_sum[:]).then_inc(y_inv, 1)
                dve.wait_ge(y_inv, T + 1)
                nc.vector.tensor_tensor(by_head(Y), by_head(O), bcast(inv_sum), ALU.mult).then_inc(y_norm, 1)

            def by_head(t):
                return t[:].rearrange("p (s e) -> p s e", e=HEAD_DIM)

            def bcast(t):
                return t[:].unsqueeze(2).broadcast_to((P, STEPS, HEAD_DIM))

            def retention(l, c):
                R = dve.snap(l * PAIRS + c)
                rope("C", l, c, 0, rope_no("C", l, c, 0), qT[:])
                rope("C", l, c, 1, rope_no("C", l, c, 1), kT[:])
                b, held = result_in("C", l, c, 3)
                dve.wait_ge(gc_tanh, R + 1)
                nc.vector.scalar_tensor_tensor(out=gC[:], in0=gC[:], scalar=1.0, in1=dense[:, b, :], op0=ALU.add,
                                               op1=ALU.mult).then_inc(evacuated[b], 1)
                slot, count = PLAN.landed("C", l, c, DECAY_ITEM)
                dve.wait_ge(landed[slot], count)
                for s in range(STEPS):
                    hh, j = divmod(s, TB)
                    n = SEQ - j * P
                    dve.wait_ge(st_ready, R * STEPS + (s + 1))
                    if s >= 2:
                        dve.wait_ge(rv_done, R * STEPS + (s - 1))
                    nc.vector.tensor_tensor(probsT[:, s % 2, 0:n], scores[:, s % 2, 0:n],
                                            ring[:, slot, hh * SEQ:hh * SEQ + n], ALU.mult).then_inc(st_decayed, 1)
                dve.wait_ge(rv_done, R * STEPS + STEPS)
                nc.vector.tensor_reduce(mean[:], by_head(O), AX_X, ALU.add).then_inc(gn_step, 1)
                dve.wait_ge(gn_step, R * GN_STEPS + 1)
                nc.vector.tensor_scalar(mean[:], mean[:], 1.0 / HEAD_DIM, None, ALU.mult).then_inc(gn_step, 1)
                dve.wait_ge(gn_step, R * GN_STEPS + 2)
                nc.vector.tensor_tensor(by_head(Y), by_head(O), bcast(mean), ALU.subtract).then_inc(gn_step, 1)
                dve.wait_ge(gn_step, R * GN_STEPS + 3)
                nc.vector.tensor_tensor(probs[:, 0, :], Y[:], Y[:], ALU.mult).then_inc(gn_step, 1)
                dve.wait_ge(gn_step, R * GN_STEPS + 4)
                nc.vector.tensor_reduce(var[:], probs[:, 0, :].rearrange("p (s e) -> p s e", e=HEAD_DIM), AX_X,
                                        ALU.add).then_inc(gn_step, 1)
                dve.wait_ge(gn_step, R * GN_STEPS + 5)
                nc.vector.tensor_scalar(var[:], var[:], 1.0 / HEAD_DIM, EPS, ALU.mult, ALU.add).then_inc(gn_step, 1)
                dve.wait_ge(gn_pow, R + 1)
                nc.vector.tensor_tensor(by_head(Y), by_head(Y), bcast(inv_std), ALU.mult).then_inc(yc_norm, 1)
                at = dve.snap(PAIRS * BRANCH["C"] + c)
                dve.wait_ge(yc_turned, R + 1)
                nc.vector.scalar_tensor_tensor(out=yT[:, bass.ds(at, 1), :], in0=Yt[:].rearrange("p (a n) -> p a n", a=1),
                                               scalar=half_gain[:, bass.ds(R, 1)],
                                               in1=gC[:].rearrange("p (a n) -> p a n", a=1),
                                               op0=ALU.mult, op1=ALU.mult).then_inc(yc_stored, 1)

            nc.vector.memset(ones[:], 1.0).then_inc(s_init, 1)
            nc.vector.memset(halves[:], -0.5).then_inc(s_init, 1)
            dve.wait_ge(s_x, 16)
            dve.wait_ge(s_small, 16)
            nc.vector.tensor_scalar(neg_sink[:], small[:, SMALL["sinks"]:SMALL["sinks"] + DEPTH * HEADS], -1.0, None,
                                    ALU.mult).then_inc(s_init, 1)
            nc.vector.tensor_scalar(half_gain[:], small[:, SMALL["ret_norm"]:SMALL["ret_norm"] + DEPTH * PAIRS],
                                    0.5, None, ALU.mult).then_inc(s_init, 1)
            nc.vector.tensor_scalar(half_gdn[:], small[:, SMALL["g_gdn"]:SMALL["g_gdn"] + 1], 0.5, None, ALU.mult
                                    ).then_inc(s_init, 1)
            nc.vector.memset(minus_half[:], -0.5).then_inc(s_init, 1)
            dve.wait_ge(cond_step, 1)
            nc.vector.scalar_tensor_tensor(out=cond[:], in0=cond_tanh[:], scalar=1.0,
                                           in1=small[:, SMALL["cond"]:SMALL["cond"] + 2 * KC], op0=ALU.add,
                                           op1=ALU.mult).then_inc(cond_step, 1)
            dve.wait_ge(cond_step, 2)
            nc.vector.tensor_scalar(cond[:], cond[:], 0.5, None, ALU.mult).then_inc(cond_step, 1)
            dve.wait_ge(s_init, INITS)
            with dve.Fori(0, DEPTH) as l:
                norm("norm1", l, 2 * l, lambda k: small[:, bass.ds(l * KC + (SMALL["attn_norm"] + k), 1)], hT)
                dve.wait_ge(s_const, 16)
                at = CONST_AT["ident"]
                nc.vector.tensor_copy(masks[:], const[:, at:at + 3 * P]).then_inc(masks_ready, 1)
                pre(l)
                with dve.Fori(0, PAIRS) as c:
                    attention("A", l, c)
                topk_mask(l)
                with dve.Fori(0, PAIRS) as c:
                    attention("B", l, c)
                rope("Dkv", l, 0, 0, rope_no("Dkv", l, 0), kI[:])
                with dve.Fori(0, PAIRS) as c:
                    attention("D", l, c)
                with dve.Fori(0, PAIRS) as c:
                    retention(l, c)
                for b in range(BANKS):
                    dve.wait_ge(evacuated[b], held_before("merge", l, b))
                settle(dve)
                with dve.Fori(0, KC) as d:
                    for n in range(N_BRANCH):
                        b, held = result_in("merge", l, d, n)
                        g = dve.snap(d + KC * n)
                        tmp = hT[:, bass.ds(d, 1), :] if n == 0 else (Y if n % 2 else gC)[:].rearrange("p (a n) -> p a n", a=1)
                        nc.vector.scalar_tensor_tensor(out=tmp, in0=gates[:, bass.ds(g, 1), :], scalar=1.0,
                                                       in1=dense[:, b:b + 1, :], op0=ALU.add, op1=ALU.mult
                                                       ).then_inc(evacuated[b], 1)
                        dve.wait_ge(evacuated[b], held + 1)
                        if n:
                            dve.wait_ge(merge_add, l * (3 * KC) + d * 3 + (n - 1 + OPEN))
                            nc.vector.tensor_tensor(hT[:, bass.ds(d, 1), :], hT[:, bass.ds(d, 1), :], tmp, ALU.add
                                                    ).then_inc(merge_add, 1)
                bias = small[:, bass.ds(l * ADA_L + SMALL["b_ada"], ADA_L)].unsqueeze(2).broadcast_to((P, ADA_L, 2))
                nc.vector.tensor_tensor(mod[:, bass.ds(l * (2 * ADA_L), 2 * ADA_L)].rearrange("p (s w) -> p s w", w=2),
                                        Yt[:, 0:2 * ADA_L].rearrange("p (s w) -> p s w", w=2), bias, ALU.add
                                        ).then_inc(mod_step, 1)
                with dve.Fori(0, KC // 2) as c:
                    for j in range(2):
                        b, held = result_in("out", l, c, j)
                        x = xT[:, bass.ds(c * 2 + j, 1), :]
                        nc.vector.scalar_tensor_tensor(out=x, in0=dense[:, b:b + 1, :], scalar=0.5, in1=x,
                                                       op0=ALU.mult, op1=ALU.add).then_inc(evacuated[b], 1)
                for j in range(2):
                    split_weights("up", l, 0, j)
                norm("norm2", l, 2 * l + 1, lambda k: small[:, bass.ds(l * KC + (SMALL["ffn_norm"] + k), 1)], hT)
                split_h(l, l * (2 * KC) + KC)
                settle(dve)
                with dve.Fori(0, FC // 2) as c:
                    for half in range(2):
                        F = dve.snap(l * FC + c * 2 + half)
                        for j in range(2):
                            b, held = result_in("up", l, c, 2 * half + j)
                            up_split("up", l, c, 2 * half + j)
                            at = dve.snap((l * (2 * FC) + c * 2 + (half + j * FC)) * 4 + SMALL["conv"])
                            dve.wait_ge(taps, F * 2 + (j + 1))
                            for shift, tap, done in ((1, 1, conv_step), (2, 0, evacuated[b])):
                                u = (side_a, side_b)[j][half][:, shift:SEQ]
                                nc.vector.scalar_tensor_tensor(out=u, in0=dense[:, b, 0:SEQ - shift],
                                                               scalar=small[:, bass.ds(at + tap, 1)], in1=u,
                                                               op0=ALU.mult, op1=ALU.add).then_inc(done, 1)
                                if shift == 1:
                                    dve.wait_ge(conv_step, F * 2 + (j + 1))
                        dve.wait_ge(up_tanh, F + 1)
                        dve.wait_ge(hidden_ready, F + HIDDEN_OPEN)
                        nc.vector.scalar_tensor_tensor(out=probsT[:, 1, :], in0=probsT[:, 0, :], scalar=1.0,
                                                       in1=side_a[half], op0=ALU.add, op1=ALU.mult
                                                       ).then_inc(up_gate, 1)
                        dve.wait_ge(evacuated[1], held + 1)
                        store_hidden(l, c, half, side_b)

                def add_down(c, j):
                    b, held = result_in("down", l, c, j)
                    x = xT[:, c * 4 + j, :]
                    nc.vector.scalar_tensor_tensor(out=x, in0=dense[:, b, :], scalar=0.5, in1=x,
                                                   op0=ALU.mult, op1=ALU.add).then_inc(evacuated[b], 1)
                down_steps("down", l, add_down)
            norm("normf", DEPTH, N_F, lambda k: small[:, SMALL["final_norm"] + k:SMALL["final_norm"] + k + 1], xT)

            L = DEPTH
            sm = lambda name, at=0, n=1: small[:, SMALL[name] + at:SMALL[name] + at + n]
            m4 = mod[:].rearrange("p (s k w) -> p s k w", s=6, w=2)
            dve.wait_ge(mod_step, DEPTH)
            for r, (part, w, name) in enumerate(((1, 0, "g_pre_mix"), (1, 1, "g_pre_mix"), (2, 0, "g_post_mix"),
                                                 (4, 0, "g_pre_ffn"), (5, 0, "g_post_ffn"))):
                add = 1.0 if part in (1, 4) else 0.0
                nc.vector.scalar_tensor_tensor(out=gain[:, r, :], in0=m4[:, part, :, w], scalar=add,
                                               in1=sm(name, 0, KC), op0=ALU.add, op1=ALU.mult).then_inc(mod_step, 1)
            dve.wait_ge(mod_step, DEPTH + 5)

            def shifted(number, dst, part, w, n, before):
                dve.wait_ge(h_scaled, before + KC)
                for k in range(KC):
                    nc.vector.tensor_scalar(dst[:, k, 0:n], dst[:, k, 0:n], m4[:, part, k, w:w + 1], None, ALU.add
                                            ).then_inc(h_ready, 1)

            def residual(number):
                dve.wait_ge(h_ready, (number + 1) * KC)
                for k in range(KC):
                    nc.vector.tensor_tensor(xT[:, k, :], xT[:, k, :], hT[:, k, :], ALU.add).then_inc(x_added, 1)

            dve.wait_ge(h_ready, (N_F + 1) * KC)
            hctx = hx[:, :, SEQ:SEQ + CTX]
            norm("normX", L, N_X, lambda k: gain[:, 1, k:k + 1], hctx, src=xc, n=CTX, sem=h_scaled)
            shifted(N_X, hctx, 0, 1, CTX, 0)
            norm("normL", L, N_L, lambda k: gain[:, 0, k:k + 1], hx, sem=h_scaled)
            shifted(N_L, hx, 0, 0, SEQ, KC)

            with dve.Fori(0, 4) as c3:
                for third in range(3):
                    c = dve.snap(c3 * 3 + third)
                    at = dve.snap(c * 3 + SMALL["qkv_conv"])
                    for j, (lo, n) in enumerate(((0, SEQ), (SEQ, CTX))):
                        b, held = result_in("qkv", L, c3, 2 * third + j)
                        dve.wait_ge(cq_taps, c * 2 + (j + 1))
                        u = cv[:, bass.ds(c, 1), lo + 1:lo + n]
                        nc.vector.scalar_tensor_tensor(out=u, in0=dense[:, b:b + 1, 0:n - 1],
                                                       scalar=small[:, bass.ds(at, 1)], in1=u, op0=ALU.mult,
                                                       op1=ALU.add).then_inc(cq_conv, 1)
                        dve.wait_ge(cq_conv, c * 2 + (j + 1))
                        u = cv[:, bass.ds(c, 1), lo:lo + n - 1]
                        nc.vector.scalar_tensor_tensor(out=u, in0=dense[:, b:b + 1, 1:n],
                                                       scalar=small[:, bass.ds(at + 2, 1)], in1=u, op0=ALU.mult,
                                                       op1=ALU.add).then_inc(evacuated[b], 1)
                    dve.wait_ge(cq_tanh, c + 1)
                    u = cv[:, bass.ds(c, 1), :]
                    nc.vector.scalar_tensor_tensor(
                        out=u, in0=probsT[:].rearrange("p a n -> p (a n)")[:, 0:XB * P].rearrange("p (a n) -> p a n", a=1),
                        scalar=1.0, in1=u, op0=ALU.add, op1=ALU.mult).then_inc(cq_done, 1)
            with dve.Fori(0, 4) as c:
                b, held = result_in("uz", L, c, 1)
                dve.wait_ge(z_tanh, c + 1)
                nc.vector.scalar_tensor_tensor(out=yT[:, bass.ds(c + 4, 1), :], in0=gC[:].rearrange("p (a n) -> p a n", a=1),
                                               scalar=1.0, in1=dense[:, b:b + 1, :], op0=ALU.add, op1=ALU.mult
                                               ).then_inc(evacuated[b], 1)
                dve.wait_ge(evacuated[b], held + 1)
                dve.sem_inc(z_done, 1)
            dve.wait_ge(evacuated[0], PLAN.bank("ab", L, 0, 0)[1] + 1)
            ab = abt[:].rearrange("p (t g h) -> p t g h", t=XB, h=GH)
            rows = lambda t, d: t[:, d * GH:(d + 1) * GH].unsqueeze(1).broadcast_to((P, XB, GH))
            dtb = sm("dt_bias", 0, 2 * GH)
            for d in range(2):
                nc.vector.tensor_tensor(sc3(zz, d), ab[:, :, 2 + d, :], rows(dtb, d), ALU.add).then_inc(ab_step, 1)
            dve.wait_ge(ab_step, 2)
            nc.vector.scalar_tensor_tensor(out=tmp_sc[:, 0:SC], in0=zz[:], scalar=-1.0, in1=zz[:], op0=ALU.mult,
                                           op1=ALU.max).then_inc(ab_step, 1)
            dve.wait_ge(ab_act, 5)
            nc.vector.scalar_tensor_tensor(out=zz[:], in0=zz[:], scalar=0.0, in1=tmp_sc[:, SC:2 * SC], op0=ALU.max,
                                           op1=ALU.add).then_inc(ab_step, 1)
            nc.vector.tensor_scalar(half_beta[:], beta[:], 0.25, 0.25, ALU.mult, ALU.add).then_inc(ab_step, 1)
            dve.wait_ge(ab_step, 5)
            for d in range(2):
                nc.vector.scalar_tensor_tensor(out=sc3(gg, d), in0=sc3(zz, d), scalar=-1.0, in1=rows(decay_rate[:], d),
                                               op0=ALU.mult, op1=ALU.mult).then_inc(ab_step, 1)
            nc.vector.tensor_scalar(beta[:], beta[:], 0.5, 0.5, ALU.mult, ALU.add).then_inc(ab_step, 1)
            dve.wait_ge(l2_sums, 1)
            nc.vector.tensor_scalar(l2v[:], scores[:, 1, 0:8 * XB], 4 * EPS, None, ALU.add).then_inc(l2_var, 1)
            dve.wait_ge(ab_act, 6)
            dve.wait_ge(ab_step, 8)
            nc.vector.tensor_tensor(bg[:], beta[:], egc[:], ALU.mult).then_inc(ab_step, 1)
            nc.vector.tensor_tensor(tmp_sc[:, 0:SC], scores[:, 0, SC:2 * SC], gcum[:], ALU.subtract
                                    ).then_inc(ab_step, 1)
            dve.wait_ge(l2_ready, 1)
            lq = l2s[:, 0:GH * XB].rearrange("p (h t) -> p t h", t=XB)
            lk = l2s[:, GH * XB:2 * GH * XB].rearrange("p (h t) -> p t h", t=XB)
            nc.vector.tensor_scalar(qs[:].rearrange("p (t h) -> p t h", h=GH), lq, GD ** -0.5, None, ALU.mult
                                    ).then_inc(ab_step, 1)
            dve.wait_ge(ab_step, 11)
            q3 = qs[:].rearrange("p (t h) -> p t h", h=GH)
            for d in range(2):
                nc.vector.tensor_tensor(sc3(bs, d), sc3(beta, d), lk, ALU.mult)
                last = nc.vector.tensor_tensor(sc3(eqs, d), sc3(egc, d), q3, ALU.mult)
            last.then_inc(ab_step, 1)
            for t in range(XB):
                dve.wait_ge(k_turned, t + 1)
                nc.vector.tensor_tensor(heads(ktok[:, t, :]), heads(bankA[t % 2]), per_head(lk[:, t, :]), ALU.mult
                                        ).then_inc(k_scaled, 1)
            for d in range(2):
                nc.vector.memset(state[d], 0.0).then_inc(ab_step, 1)
            dve.wait_ge(ab_step, 14)

            for n in range(UNITS):
                isl = n >= FIRST_L
                both = [(d, ORDER[d][n]) for d in range(2)]
                hcol = [slice(h * P, (h + 1) * P) for h in range(GH)]
                for d, b in both:
                    dve.wait_ge(u_row[d], n + 1)
                    for h in range(GH):
                        last = nc.vector.scalar_tensor_tensor(
                            out=W2["decay"][d][:, hcol[h]], in0=bankA[d][:, hcol[h]], scalar=sc_at(gcum, d, b)[:, h:h + 1],
                            in1=barred[:, d * P:(d + 1) * P], op0=ALU.subtract, op1=ALU.add)
                    last.then_inc(u_diff[d], 1)
                for d, b in both:
                    dve.wait_ge(u_kk[d], n + 1)
                    dve.wait_ge(u_decay[d], n + 1)
                    for h in range(GH):
                        last = nc.vector.scalar_tensor_tensor(
                            out=W2["A"][d][:, hcol[h]], in0=bankB[d][:, hcol[h]], scalar=sc_at(bs, d, b)[:, h:h + 1],
                            in1=W2["decay"][d][:, hcol[h]], op0=ALU.mult, op1=ALU.mult)
                    last.then_inc(u_a[d], 1)
                if isl:
                    for d, b in both:
                        dve.wait_ge(u_qk[d], n - FIRST_L + 1)
                        for h in range(GH):
                            last = nc.vector.scalar_tensor_tensor(
                                out=W2["X"][d][:, hcol[h]], in0=bankC[d][:, hcol[h]],
                                scalar=qs[:, b * GH + h:b * GH + h + 1], in1=W2["decay"][d][:, hcol[h]],
                                op0=ALU.mult, op1=ALU.mult)
                        last.then_inc(u_x[d], 1)
                for d, b in both:
                    dve.wait_ge(u_a[d], n + 1)
                    nc.vector.tensor_tensor(heads(W2["A_level"][d]), heads(W2["A"][d]), level_mask(d, 0), ALU.mult
                                            ).then_inc(u_t0[d], 1)
                for d, b in both:
                    dve.wait_ge(u_t0[d], n + 1)
                    nc.vector.tensor_tensor(heads(W2["T"][d]), ident.unsqueeze(1).broadcast_to((P, GH, P)),
                                            heads(W2["A_level"][d]), ALU.subtract).then_inc(u_t[d], 1)
                for lev in range(1, LEVELS):
                    for d, b in both:
                        dve.wait_ge(u_upd[d], n * (LEVELS - 1) + lev)
                        if lev < LEVELS - 1:
                            nc.vector.tensor_tensor(W2["T"][d], W2["T"][d], bankA[d], ALU.subtract)
                        nc.vector.tensor_tensor(W2["TT"][d], W2["TT"][d], bankC[d], ALU.subtract).then_inc(u_lvl[d], 1)
                for d, b in both:
                    dve.wait_ge(u_wu[d], n + 1)
                    nc.vector.tensor_copy(W2["u"][d], bankC[d]).then_inc(u_u[d], 1)
                for i in range(2):
                    for d, b in both:
                        c, hs = chunk_of(d, i)
                        dve.wait_ge(c_ws[d], 2 * n + i + 1)
                        nc.vector.tensor_tensor(W2["vnew"][d][hs, :], W2["u"][d][hs, :], bankB[d][hs, :], ALU.subtract
                                                ).then_inc(c_v[d], 1)
                    for d, b in both:
                        c, hs = chunk_of(d, i)
                        dve.wait_ge(c_sd[d], 2 * n + i + 1)
                        for h in range(GH):
                            last = nc.vector.scalar_tensor_tensor(
                                out=state[d][:, hcol[h]], in0=state[d][:, hcol[h]], scalar=etot_at(c, d, b, h),
                                in1=bankA[d][:, hcol[h]], op0=ALU.mult, op1=ALU.add)
                        last.then_inc(c_s[d], 1)
                        if isl:
                            if n >= 4 and (n, i) != (4, 0):
                                dve.wait_ge(c_o3[d], 2 * (n - 4) + i)
                            nc.vector.tensor_tensor(heads(W2["oscan"][d][hs, :]), heads(bankC[d][hs, :]),
                                                    per_head(sc_at(eqs, d, b)[hs, :]), ALU.mult).then_inc(c_o1[d], 1)
                            dve.wait_ge(c_oi[d], seen(n, i))
                            dve.wait_ge(c_o1[d], seen(n, i))
                            dst = o2[b] if n < 4 else W2["oscan"][d]
                            nc.vector.tensor_tensor(dst[hs, :], W2["oscan"][d][hs, :], bankB[d][hs, :], ALU.add
                                                    ).then_inc(c_o2[d], 1)
            for t in range(TB):
                dve.wait_ge(p_sq, t + 1)
                nc.vector.tensor_reduce(osum[:, t * GH:(t + 1) * GH], heads(SQ4[t]), AX_X, ALU.add).then_inc(p_dve, 1)
            dve.wait_ge(p_dve, P_SUMS)
            nc.vector.tensor_scalar(osum[:], osum[:], 1.0 / GD, EPS, ALU.mult, ALU.add).then_inc(p_dve, 1)
            dve.wait_ge(p_pow, 1)
            for t in range(TB):
                nc.vector.tensor_tensor(heads(o2[t]), heads(o2[t]), per_head(oscale[:, t * GH:(t + 1) * GH]), ALU.mult
                                        ).then_inc(p_dve, 1)
            for t in range(TB):
                dve.wait_ge(p_turned, t + 1)
                z = zT[:, :, t * P:(t + 1) * P]
                nc.vector.scalar_tensor_tensor(out=z, in0=heads((bankA + bankB)[t]), scalar=half_gdn[:, 0:1], in1=z,
                                               op0=ALU.mult, op1=ALU.mult).then_inc(p_dve, 1)
            for j in range(2):
                split_weights("up2", L, 0, j)
            norm("norm3", L, N_3, lambda k: gain[:, 2, k:k + 1], hT, src=hT)
            residual(N_3)
            dve.wait_ge(x_added, KC)
            norm("norm4", L, N_4, lambda k: gain[:, 3, k:k + 1], hT, sem=h_scaled)
            shifted(N_4, hT, 3, 0, SEQ, 2 * KC)
            split_h(L, N_4 * KC)
            rows8 = SEQ // GRID_W
            grid = lambda t: t.rearrange("p (r c) -> p r c", c=GRID_W)
            others = [(dy, dx) for dy in (-1, 0, 1) for dx in (-1, 0, 1) if (dy, dx) != (0, 0)]
            with dve.Fori(0, FC // 2) as c:
                for half in range(2):
                    f = dve.snap(c * 2 + half)
                    b, held = result_in("up2", L, c, 2 * half + 1)
                    at = dve.snap(f * 9 + SMALL["dwc"])
                    dve.wait_ge(taps, f + (2 * DEPTH * FC + 1))
                    dve.wait_ge(evacuated[b], held + 1)
                    for m, (dy, dx) in enumerate(others):
                        r0, r1, c0, c1 = max(0, -dy), rows8 - max(0, dy), max(0, -dx), GRID_W - max(0, dx)
                        u = grid(side_b[half])[:, r0:r1, c0:c1]
                        v = grid(grid_in[half])[:, r0 + dy:r1 + dy, c0 + dx:c1 + dx]
                        if m:
                            dve.wait_ge(conv_step, f * 8 + (2 * DEPTH * FC + m))
                        nc.vector.scalar_tensor_tensor(out=u, in0=v,
                                                       scalar=small[:, bass.ds(at + (3 * (dy + 1) + dx + 1), 1)],
                                                       in1=u, op0=ALU.mult, op1=ALU.add
                                                       ).then_inc(conv_step, 1)
                    dve.wait_ge(up_tanh, f + (DEPTH * FC + 1))
                    nc.vector.scalar_tensor_tensor(out=probsT[:, 1, :], in0=probsT[:, 0, :], scalar=1.0,
                                                   in1=side_b[half], op0=ALU.add, op1=ALU.mult).then_inc(up_gate, 1)
                    dve.wait_ge(evacuated[0], PLAN.bank("up2", L, c, 2 * half)[1] + 1)
                    store_hidden(L, c, half, side_a)
            dve.wait_ge(weights_hi, weights_no("down2", L, 0, 2))
            down_steps("down2", L, lambda c, j: None)
            norm("norm5", L, N_5, lambda k: gain[:, 4, k:k + 1], hT, src=hT)
            residual(N_5)

        @block.gpsimd
        def _(pool):
            def swap_sin(r):
                pool.wait_ge(swap_ready, r + 1)
                pool.wait_ge(rope_done, r + OPEN)
                nc.gpsimd.tensor_tensor(swapped_sin[:], swapped[:], sin, ALU.mult).then_inc(swap_mul, 1)

            def low_weights(name, l, c, j):
                hi = j % (2 if name.startswith("up") else HI_SLOTS)
                slot = j % SLOTS
                pool.wait_ge(weights_hi, weights_no(name, l, c, j) + 1)
                nc.gpsimd.tensor_tensor(ring_lo[:, slot, :], ring[:, slot, :], ring_hi[:, hi, :], ALU.subtract
                                        ).then_inc(weights_lo, 1)

            def ffn(name, l):
                for j in range(2):
                    low_weights(name, l, 0, j)
                for k in range(1, KC, 2):
                    pool.wait_ge(h_hi, l * KC + (k + 1))
                    nc.gpsimd.tensor_tensor(hT_lo[:, k, :], hT[:, k, :], hT_hi[:, k, :], ALU.subtract
                                            ).then_inc(h_lo_odd, 1)
                settle(pool)
                with pool.Fori(0, FC // 2) as c:
                    for half in range(2):
                        for j in range(2 * half, 2 * half + 2):
                            low_weights(name, l, c + j // 2, (j + 2) % 4)
                down = name.replace("up", "down")
                for c in range(2):
                    for j in range(0 if c else 2, FC // 2):
                        low_weights(down, l, c, j)

            pool.wait_ge(s_const, 16)
            pool.wait_ge(s_init, INITS)
            with pool.Fori(0, DEPTH) as l:
                with pool.Fori(0, ROPES - 2 * PAIRS) as r:
                    swap_sin(l * ROPES + r)
                with pool.Fori(0, PAIRS) as c:
                    R = pool.snap(l * PAIRS + c)
                    for j in range(2):
                        swap_sin(rope_no("C", l, c, j))
                    pool.wait_ge(gn_step, R * GN_STEPS + GN_STEPS)
                    nc.gpsimd.tensor_tensor(inv_std[:], var[:], halves[:], ALU.pow).then_inc(gn_pow, 1)
                ffn("up", l)

            pool.wait_ge(l2_var, 1)
            nc.gpsimd.tensor_tensor(l2s[:], l2v[:], minus_half[:], ALU.pow).then_inc(l2_ready, 1)
            pool.wait_ge(kh_stored, XB)
            for n in range(UNITS):
                isl = n >= FIRST_L
                both = [(d, ORDER[d][n]) for d in range(2)]
                for lev in range(1, LEVELS):
                    for d, b in both:
                        if lev == 1:
                            pool.wait_ge(u_t[d], n + 1)
                        else:
                            pool.wait_ge(u_z[d], n * (LEVELS - 1) + lev - 1)
                        nc.gpsimd.tensor_tensor(heads(W2["A_level"][d]), heads(W2["A"][d]), level_mask(d, lev), ALU.mult
                                                ).then_inc(u_as[d], 1)
                    if lev == 2:
                        for d, b in both:
                            if n:
                                pool.wait_ge(c_sd[d], 2 * n)
                            if isl:
                                pool.wait_ge(u_xt[d], n - FIRST_L + 1)
                            for dst, src, scale in (("decay", ktok, bg), ("X", vtok, half_beta), ("kd", ktok, ed)):
                                nc.gpsimd.tensor_tensor(heads(W2[dst][d]), heads(src[:, b, :]), per_head(sc_at(scale, d, b)),
                                                        ALU.mult).then_inc(u_kv[d], 1)
                if n >= 4:
                    for i in range(2):
                        for d, b in both:
                            c, hs = chunk_of(d, i)
                            pool.wait_ge(c_o2[d], seen(n, i))
                            pool.wait_ge(c_o2[1 - d], seen(7 - n, 1))
                            nc.gpsimd.tensor_tensor(o2[b][hs, :], o2[b][hs, :], W2["oscan"][d][hs, :], ALU.add
                                                    ).then_inc(c_o3[d], 1)
                    for d in range(2):
                        pool.wait_ge(c_o3[d], 2 * (n - 4) + 2)
            pool.wait_ge(p_dve, P_MEANS)
            nc.gpsimd.tensor_tensor(oscale[:], osum[:], minus_half[:, 0:TB * GH], ALU.pow).then_inc(p_pow, 1)
            ffn("up2", DEPTH)


def _blocks(w, cols=P):
    return w.reshape(-1, P, P).transpose(1, 0, 2).reshape(P, -1)


def _columns():
    sizes = dict(qA=512, kA=512, vA=512, fA=8, qB=512, kB=64, vB=64, qI=256, kI=64, wI=4, qC=512, kC=512,
                 vC=512, gC=512, qD=512, kD=128, vD=128, gates=4096)
    return dict(zip(sizes, np.cumsum([0] + list(sizes.values()))[:-1].tolist()))


AT = _columns()


def _layer_items(a, l):
    w = a["w_in"][l]
    col = lambda name, j, n=P: w[:, AT[name] + j:AT[name] + j + n]
    gate = lambda branch, c: [_blocks(col("gates", BRANCH[branch] * D_MODEL + (2 * c + g) * P)) for g in range(2)]
    items = []
    tok = np.concatenate([col("vB", 0, 64), col("fA", 0, 8), col("wI", 0, 4),
                          np.zeros((D_MODEL, P - TOK_COLS), w.dtype)], axis=1)
    items += [_blocks(tok), _blocks(np.concatenate([col("kI", 0, 64)] * 2, 1)), _blocks(col("qI", 0)),
              _blocks(col("qI", P)), _blocks(np.concatenate([col("kB", 0, 64)] * 2, 1))]
    for c in range(PAIRS):
        items += [_blocks(col(n, c * P)) for n in ("qA", "kA", "vA")] + gate("A", c)
    for c in range(PAIRS):
        items += [_blocks(col("qB", c * P))] + gate("B", c)
    items += [_blocks(col("kD", 0)), _blocks(col("vD", 0))]
    for c in range(PAIRS):
        pair = np.concatenate([col("qD", c * 64, 64), col("qD", (c + PAIRS) * 64, 64)], 1)
        items += [_blocks(pair)] + gate("D", c)
    for c in range(PAIRS):
        items += [_blocks(col(n, c * P)) for n in ("qC", "kC", "vC", "gC")] + gate("C", c) + [DECAYS[c]]
    wb = a["w_branch"][l].copy()
    wb[3] = wb[3].reshape(2, PAIRS, 64, D_MODEL).transpose(1, 0, 2, 3).reshape(512, D_MODEL)
    for d in range(KC):
        for n in (0, 2):
            items.append(np.concatenate([_blocks(wb[n + m][:, d * P:(d + 1) * P]) for m in range(2)], 1))
            ada = (l * KC + d) * ADA_T + (0 if n == 0 else 2)
            items += [_blocks(a["w_ada_2"][0][:, j * P:(j + 1) * P]) for j in range(ada, ada + (2 if n == 0 else 1))]
    items += [_blocks(a["w_out"][l][:, d * P:(d + 1) * P]) for d in range(KC)]
    for f in range(FC):
        items += [_blocks(a["w_up"][l][:, j * D_FF + f * P:j * D_FF + (f + 1) * P]) for j in range(2)]
    down = np.concatenate([_blocks(a["w_down"][l][:, d * P:(d + 1) * P]) for d in range(KC)], 1)
    items += [down[:, i * KC * P:(i + 1) * KC * P] for i in range(FC)]
    return items


def _decays():
    g = np.log(1.0 - 2.0 ** (-5.0 - np.arange(HEADS)))
    dist = np.arange(SEQ)[None, :] - np.arange(P)[:, None]
    full = np.where(dist >= 0, np.exp(np.maximum(dist, 0)[None] * g[:, None, None]), 0.0) * QK_SCALE
    full = full.astype(np.float32)
    return [np.concatenate([full[2 * c], full[2 * c + 1]], 1) for c in range(PAIRS)]


DECAYS = _decays()


def _tail_items(a):
    w_in, w_out, w_up, w_down = (a[k][0] for k in ("w_in_2", "w_out_2", "w_up_2", "w_down_2"))
    items = []
    items.append(_blocks(np.concatenate([w_in[:, 2560:2576], np.zeros((D_MODEL, P - 16), w_in.dtype)], 1)))
    items += [_blocks(w_in[:, 512 + j * P:512 + (j + 1) * P]) for j in range(12)]
    for c in range(4):
        items += [_blocks(w_in[:, c * P:(c + 1) * P]), _blocks(w_in[:, 2048 + c * P:2048 + (c + 1) * P])]
    ch = np.arange(GD)
    angle = 2 * np.pi * (np.outer(ch, ch) % GD) / GD
    wf = a["w_fourier_2"][0].transpose(1, 0, 2).reshape(GD, 4 * GD)
    items.append(np.concatenate([wf, np.cos(angle).astype(np.float32), np.sin(angle).astype(np.float32),
                                 np.zeros((P, 2 * P), np.float32)], 1))
    at = np.arange(SEQ)
    angle = 2 * np.pi * (np.outer(at, at) % SEQ) / SEQ
    for m in (np.cos(angle), -np.sin(angle)):
        m = m.astype(np.float32).reshape(2, 2, P, SEQ).transpose(0, 2, 1, 3).reshape(2, P, 2 * SEQ)
        items += [m[0], m[1]]
    items += [_blocks(w_out[:, d * P:(d + 1) * P]) for d in range(KC)]
    for f in range(FC):
        items += [_blocks(w_up[:, j * D_FF + f * P:j * D_FF + (f + 1) * P]) for j in range(2)]
    down = np.concatenate([_blocks(w_down[:, d * P:(d + 1) * P]) for d in range(KC)], 1)
    items += [down[:, i * KC * P:(i + 1) * KC * P] for i in range(FC)]
    return items


def _consts2():
    i, j = np.arange(P)[:, None], np.arange(P)[None, :]
    same = i // CHUNK == j // CHUNK
    barred = [np.where(same & see, 0.0, -NEG) for see in (j <= i, j >= i)]
    upto = [same & (i <= j), same & (i >= j)]
    lev = []
    for s in (1 << n for n in range(LEVELS)):
        lev.append((i // (2 * s) == j // (2 * s)) & (i % (2 * s) >= s) & (j % (2 * s) < s))
    return [*barred, *upto, same, *lev, *[m.T for m in lev]]


def _consts():
    half = HEAD_DIM // 2
    inv = (1.0 / (np.float32(10000.0) ** (np.arange(half, dtype=np.float32) * 2.0 / HEAD_DIM))).astype(np.float32)
    ang = (np.arange(SEQ, dtype=np.float32)[None, :] * inv[:, None]).astype(np.float32)
    c, s = np.cos(ang), np.sin(ang)
    i = np.arange(P)
    return np.concatenate([
        np.concatenate([c] * 4), np.concatenate([-s, s] * 2), np.eye(P),
        np.where(i[None, :] <= i[:, None], 0.0, NEG), np.where(i[None, :] > i[:, None], 0.0, NEG),
        (np.arange(SEQ)[None, :] >= i[:, None]), *_consts2(),
    ], axis=1).astype(np.float32)


def _feature_major(v, n):
    v = np.asarray(v)
    return v.reshape(-1, n, P).transpose(2, 0, 1).reshape(P, -1)


def _small(a):
    rows = lambda v: np.broadcast_to(np.asarray(v).reshape(1, -1), (P, np.asarray(v).size))
    conv = np.concatenate([a["conv_w"], a["conv_b"][:, None]], 1)
    conv = conv.reshape(DEPTH, 4, 2 * FC, P).transpose(3, 0, 2, 1).reshape(P, -1)
    return np.concatenate([
        _feature_major(a["attn_norm"], KC), _feature_major(a["ffn_norm"], KC),
        _feature_major(a["ret_norm"], PAIRS), rows(a["forget_bias"]), rows(a["attn_sinks"]),
        _feature_major(a["final_norm"], KC), conv, _feature_major(a["b_ada_2"][0], ADA_N),
        *[_feature_major(a[n][0], KC) for n in ("g_pre_mix_2", "g_post_mix_2", "g_pre_ffn_2", "g_post_ffn_2")],
        a["g_gdn_2"].reshape(P, 1), rows(a["a_log_2"]), rows(a["dt_bias_2"]),
        a["w_qkv_conv_2"][0].reshape(3, 12, P).transpose(2, 1, 0).reshape(P, -1),
        a["w_dwc_2"][0].reshape(9, FC, P).transpose(2, 1, 0).reshape(P, -1),
        np.stack([a["c_2"][0], a["c_ctx_2"]], -1).reshape(KC, P, 2).transpose(1, 0, 2).reshape(P, -1),
    ], axis=1)


def kernel(**inputs):
    import concourse.bacc as bacc
    from concourse.bass_utils import run_bass_kernel_spmd

    a = {k: np.asarray(v) for k, v in inputs.items()}
    items = []
    for l in range(DEPTH):
        items += _layer_items(a, l)
    items += _tail_items(a)
    assert len(items) == PLAN.total_items, (len(items), PLAN.total_items)
    arrays = {
        "x_in": np.ascontiguousarray(a["x"][0].reshape(SEQ, KC, P).transpose(2, 1, 0)),
        "stream": np.stack(items),
        "small": np.ascontiguousarray(_small(a)),
        "consts": _consts(),
        "ctx": np.ascontiguousarray(a["ctx_2"][0].reshape(CTX, KC, P).transpose(2, 1, 0)),
    }
    nc = bacc.Bacc("TRN2", target_bir_lowering=False, num_devices=1)
    args = [nc.dram_tensor(k, v.shape, F32, kind="ExternalInput").ap() for k, v in arrays.items()]
    out = nc.dram_tensor("out", (P, KC, SEQ), F32, kind="ExternalOutput").ap()
    build_program(nc, *args, out)
    r = run_bass_kernel_spmd(nc, [arrays], core_ids=[0])
    y = np.asarray(r.results[0]["out"])
    return y.transpose(2, 1, 0).reshape(1, SEQ, D_MODEL)
```
